# Optimizing a Trainium2 kernel written in Bass

```python
import math
import jax, jax.numpy as jnp
from jax import lax
import numpy as np

D_MODEL = 1024
BATCH = 1
SEQ = 512
DEPTH = 2

N_CONV_LAYERS = DEPTH // 2
N_ATTN_LAYERS = DEPTH - N_CONV_LAYERS
CONV_WIDTH = 31
HEAD_DIM = 64
N_Q_HEADS = D_MODEL // HEAD_DIM
N_KV_HEADS = 4
GQA_GROUP = N_Q_HEADS // N_KV_HEADS
WINDOW = 128
ROPE_THETA = 10000.0
N_EXPERTS = 16
N_GROUPS = 4
EXPERTS_PER_GROUP = N_EXPERTS // N_GROUPS
TOP_K = 2
D_EXPERT = D_MODEL // 2
EXPERT_BLOCK = 256
LN_EPS = 1e-5
NEG_INF = -1e30
DEEPNORM_ALPHA = (2.0 * DEPTH) ** 0.25
DEEPNORM_BETA = (8.0 * DEPTH) ** -0.25

kernel_name = "yoco_conformer_swa_sink_grouped_moe"

def layer_norm(x, g, b):
    xf = x.astype(jnp.float32)
    mu = xf.mean(-1, keepdims=True)
    var = jnp.square(xf - mu).mean(-1, keepdims=True)
    y = (xf - mu) * lax.rsqrt(var + LN_EPS) * g.astype(jnp.float32) + b.astype(jnp.float32)
    return y.astype(x.dtype)

def deepnorm(x, sub, g, b):
    return layer_norm(DEEPNORM_ALPHA * x + sub, g, b)

def rope(x, positions):
    inv_freq = ROPE_THETA ** (-jnp.arange(0, HEAD_DIM, 2, dtype=jnp.float32) / HEAD_DIM)
    ang = positions.astype(jnp.float32)[..., None] * inv_freq
    cos = jnp.cos(ang)[:, :, None, :]
    sin = jnp.sin(ang)[:, :, None, :]
    xf = x.astype(jnp.float32)
    x1, x2 = xf[..., :HEAD_DIM // 2], xf[..., HEAD_DIM // 2:]
    out = jnp.concatenate([x1 * cos - x2 * sin, x2 * cos + x1 * sin], axis=-1)
    return out.astype(x.dtype)

def conformer_conv(x, w1, b1, dw, dwb, g, bn, w2, b2):
    h = x @ w1 + b1
    a, gate = jnp.split(h, 2, axis=-1)
    h = a * jax.nn.sigmoid(gate)
    h = lax.conv_general_dilated(
        h, dw[:, None, :].astype(h.dtype), window_strides=(1,),
        padding=[(CONV_WIDTH - 1, 0)], dimension_numbers=('NWC', 'WIO', 'NWC'),
        feature_group_count=D_MODEL) + dwb
    h = jax.nn.silu(layer_norm(h, g, bn))
    return h @ w2 + b2

def shared_kv(x, positions, kv_w, kv_b):
    B, S, _ = x.shape
    kv = x @ kv_w + kv_b
    k, v = jnp.split(kv, 2, axis=-1)
    k = rope(k.reshape(B, S, N_KV_HEADS, HEAD_DIM), positions)
    v = v.reshape(B, S, N_KV_HEADS, HEAD_DIM)
    return k, v

def window_mask(nb):
    n = jnp.arange(nb)[:, None, None]
    i = jnp.arange(WINDOW)[None, :, None]
    j = jnp.arange(2 * WINDOW)[None, None, :]
    qpos = n * WINDOW + i
    kpos = (n - 1) * WINDOW + j
    d = qpos - kpos
    return (d >= 0) & (d < WINDOW) & (kpos >= 0)

def swa_sink_attention(x, positions, wq, bq, sinks, k, v, wo, bo):
    B, S, _ = x.shape
    nb = S // WINDOW
    q = rope((x @ wq + bq).reshape(B, S, N_Q_HEADS, HEAD_DIM), positions)
    qb = q.reshape(B, nb, WINDOW, N_KV_HEADS, GQA_GROUP, HEAD_DIM)
    kb = k.reshape(B, nb, WINDOW, N_KV_HEADS, HEAD_DIM)
    vb = v.reshape(B, nb, WINDOW, N_KV_HEADS, HEAD_DIM)
    pad = ((0, 0), (1, 0), (0, 0), (0, 0), (0, 0))
    k2 = jnp.concatenate([jnp.pad(kb[:, :-1], pad), kb], axis=2)
    v2 = jnp.concatenate([jnp.pad(vb[:, :-1], pad), vb], axis=2)
    s = jnp.einsum('bnqkgd,bnskd->bnkgqs', qb, k2,
                   preferred_element_type=jnp.float32) * (1.0 / math.sqrt(HEAD_DIM))
    s = jnp.where(window_mask(nb)[None, :, None, None], s, NEG_INF)
    sink = sinks.astype(jnp.float32).reshape(N_KV_HEADS, GQA_GROUP)[None, None, :, :, None, None]
    m = jnp.maximum(s.max(-1, keepdims=True), sink)
    p = jnp.exp(s - m)
    denom = p.sum(-1, keepdims=True) + jnp.exp(sink - m)
    o = jnp.einsum('bnkgqs,bnskd->bnqkgd', (p / denom).astype(v2.dtype), v2)
    o = o.reshape(B, S, D_MODEL)
    return o @ wo + bo

def grouped_moe(x, router_w, router_b, w_gate, w_up, w_down):
    B, S, D = x.shape
    xt = x.reshape(-1, D)
    N = xt.shape[0]
    aff = jax.nn.sigmoid(xt.astype(jnp.float32) @ router_w.astype(jnp.float32))
    sel = aff + router_b.astype(jnp.float32)
    grp = sel.reshape(N, N_GROUPS, EXPERTS_PER_GROUP)
    gscore = lax.top_k(grp, 2)[0].sum(-1)
    g = jnp.argmax(gscore, axis=-1)
    sel_in = jnp.take_along_axis(grp, g[:, None, None], axis=1)[:, 0, :]
    _, idx = lax.top_k(sel_in, TOP_K)
    expert = g[:, None] * EXPERTS_PER_GROUP + idx
    gate = jnp.take_along_axis(aff, expert, axis=1)
    gate = gate / gate.sum(-1, keepdims=True)

    A = N * TOP_K
    e_flat = expert.reshape(A)
    tok_flat = jnp.repeat(jnp.arange(N, dtype=jnp.int32), TOP_K)
    gate_flat = gate.reshape(A)
    order = jnp.argsort(e_flat)
    e_sorted = e_flat[order]
    counts = jnp.bincount(e_flat, length=N_EXPERTS)
    start = jnp.cumsum(counts) - counts
    rank = jnp.arange(A) - start[e_sorted]
    padded = ((counts + EXPERT_BLOCK - 1) // EXPERT_BLOCK) * EXPERT_BLOCK
    pend = jnp.cumsum(padded)
    pstart = pend - padded
    dest = pstart[e_sorted] + rank
    P = ((A + N_EXPERTS * EXPERT_BLOCK + EXPERT_BLOCK - 1) // EXPERT_BLOCK) * EXPERT_BLOCK
    tok_buf = jnp.zeros((P,), jnp.int32).at[dest].set(tok_flat[order])
    gate_buf = jnp.zeros((P,), jnp.float32).at[dest].set(gate_flat[order])
    nblk = P // EXPERT_BLOCK
    blk_start = jnp.arange(nblk) * EXPERT_BLOCK
    blk_expert = jnp.minimum(jnp.searchsorted(pend, blk_start, side='right'), N_EXPERTS - 1)
    xb = xt[tok_buf].reshape(nblk, EXPERT_BLOCK, D)

    def expert_block(args):
        xblk, e = args
        h = jax.nn.silu(xblk @ w_gate[e]) * (xblk @ w_up[e])
        return h @ w_down[e]

    yb = lax.map(expert_block, (xb, blk_expert)).reshape(P, D)
    y = jnp.zeros_like(xt).at[tok_buf].add(yb * gate_buf[:, None].astype(yb.dtype))
    return y.reshape(B, S, D)

def setup_inputs(seed: int = 0) -> dict:
    key = jax.random.key(seed)
    ks = iter(jax.random.split(key, 32))
    f32 = jnp.float32

    def nrm(shape, scale):
        return jax.random.normal(next(ks), shape, f32) * scale

    D, E, F = D_MODEL, N_EXPERTS, D_EXPERT
    nA, nB = N_CONV_LAYERS, N_ATTN_LAYERS
    kvd = N_KV_HEADS * HEAD_DIM
    inp = {}
    inp['x'] = jax.random.normal(next(ks), (BATCH, SEQ, D), f32)
    inp['positions'] = jnp.broadcast_to(jnp.arange(SEQ, dtype=jnp.int32), (BATCH, SEQ))
    inp['conv_w1'] = nrm((nA, D, 2 * D), D ** -0.5)
    inp['conv_b1'] = nrm((nA, 2 * D), 0.02)
    inp['conv_dw'] = nrm((nA, CONV_WIDTH, D), CONV_WIDTH ** -0.5)
    inp['conv_dwb'] = nrm((nA, D), 0.02)
    inp['conv_ln_g'] = 1.0 + nrm((nA, D), 0.02)
    inp['conv_ln_b'] = nrm((nA, D), 0.02)
    inp['conv_w2'] = nrm((nA, D, D), D ** -0.5 * DEEPNORM_BETA)
    inp['conv_b2'] = nrm((nA, D), 0.02)
    inp['kv_w'] = jnp.concatenate([nrm((D, kvd), D ** -0.5),
                                   nrm((D, kvd), D ** -0.5 * DEEPNORM_BETA)], axis=1)
    inp['kv_b'] = nrm((2 * kvd,), 0.02)
    inp['attn_wq'] = nrm((nB, D, N_Q_HEADS * HEAD_DIM), D ** -0.5)
    inp['attn_bq'] = nrm((nB, N_Q_HEADS * HEAD_DIM), 0.02)
    inp['attn_sinks'] = nrm((nB, N_Q_HEADS), 1.0)
    inp['attn_wo'] = nrm((nB, N_Q_HEADS * HEAD_DIM, D), D ** -0.5 * DEEPNORM_BETA)
    inp['attn_bo'] = nrm((nB, D), 0.02)
    inp['router_w'] = nrm((D, E), D ** -0.5)
    inp['router_b'] = nrm((E,), 0.01)
    inp['moe_w_gate'] = nrm((DEPTH, E, D, F), D ** -0.5)
    inp['moe_w_up'] = nrm((DEPTH, E, D, F), D ** -0.5)
    inp['moe_w_down'] = nrm((DEPTH, E, F, D), F ** -0.5 * DEEPNORM_BETA)
    inp['ln_g'] = 1.0 + nrm((DEPTH, 2, D), 0.02)
    inp['ln_b'] = nrm((DEPTH, 2, D), 0.02)
    return inp

def reference(x, positions, conv_w1, conv_b1, conv_dw, conv_dwb, conv_ln_g, conv_ln_b,
              conv_w2, conv_b2, kv_w, kv_b, attn_wq, attn_bq, attn_sinks, attn_wo, attn_bo,
              router_w, router_b, moe_w_gate, moe_w_up, moe_w_down, ln_g, ln_b):
    k_shared = None
    v_shared = None
    for layer in range(DEPTH):
        if layer < N_CONV_LAYERS:
            i = layer
            mix = conformer_conv(x, conv_w1[i], conv_b1[i], conv_dw[i], conv_dwb[i],
                                 conv_ln_g[i], conv_ln_b[i], conv_w2[i], conv_b2[i])
        else:
            if layer == N_CONV_LAYERS:
                k_shared, v_shared = shared_kv(x, positions, kv_w, kv_b)
            j = layer - N_CONV_LAYERS
            mix = swa_sink_attention(x, positions, attn_wq[j], attn_bq[j], attn_sinks[j],
                                     k_shared, v_shared, attn_wo[j], attn_bo[j])
        x = deepnorm(x, mix, ln_g[layer, 0], ln_b[layer, 0])
        ffn = grouped_moe(x, router_w, router_b, moe_w_gate[layer], moe_w_up[layer],
                          moe_w_down[layer])
        x = deepnorm(x, ffn, ln_g[layer, 1], ln_b[layer, 1])
    return x


_drawn_inputs = setup_inputs


def setup_inputs(seed=0):
    import zlib

    import numpy as np

    out = dict(_drawn_inputs(seed))
    spreads = {}
    factors = {'conv_b1': 3.088,
     'conv_ln_g': 2.805,
     'conv_ln_b': 4.327,
     'kv_b': 3.937,
     'attn_bq': 44.364,
     'attn_sinks': 8.0}
    for name, (base, spread) in spreads.items():
        noise = np.random.default_rng([zlib.crc32(name.encode()), seed]).standard_normal(out[name].shape)
        drawn = base * np.exp(spread * noise) if base else spread * noise
        out[name] = __import__('jax').numpy.asarray(drawn.astype(out[name].dtype))
    for name, factor in factors.items():
        out[name] = (out[name] * factor).astype(out[name].dtype)
    return out
```

```python
import math
from contextlib import ExitStack

import concourse.bass as bass
from concourse import mybir

F32 = mybir.dt.float32
BF16 = mybir.dt.bfloat16
I32 = mybir.dt.int32
U32 = mybir.dt.uint32
ALU = mybir.AluOpType
ACT = mybir.ActivationFunctionType
AX = mybir.AxisListType

P = 128
D = 1024
S = 512
T = S // P
KD = D // P
CW = 31
HD = 64
HH = HD // 2
NQ = D // HD
NKV = 4
GQ = NQ // NKV
KVD = NKV * HD
E = 16
NG = 4
EPG = E // NG
F = D // 2
DEPTH = 2
CAP = 64
NBLK = S // CAP
TBLK = 2 * E
assert 2 * S // CAP <= E
ALPHA = (2.0 * DEPTH) ** 0.25
EPS = 1e-5
NEG = -1e30
THETA = 10000.0
NLN = 5 * T

PB1, PDWB, PGAM, PBET, NPRM = 0, 16, 24, 32, 40

TWO_PI = 2.0 * math.pi


def two_pi_parts():
    parts, rest = [], TWO_PI
    for bits in (6, 15, 24):
        part = math.floor(rest * 2.0 ** bits) / 2.0 ** bits
        parts.append(part)
        rest -= part
    return parts + [rest]


MAGIC = 1.5 * 2 ** 23


def trunk(nc, x_in, positions, conv_w1, conv_b1, conv_dw, conv_dwb, conv_ln_g, conv_ln_b,
          conv_w2, conv_b2, kv_w, kv_b, attn_wq, attn_bq, attn_sinks, attn_wo, attn_bo,
          router_w, router_b, moe_w_gate, moe_w_up, moe_w_down, ln_g, ln_b, out):
    x_rows = x_in.rearrange("a (t p) d -> p (a t) d", p=P)
    out_rows = out.rearrange("a (t p) d -> p (a t) d", p=P)

    x_dram = nc.dram_tensor("x_dram", [S, D], F32).ap()
    tok_dram = nc.dram_tensor("tok_dram", [TBLK * CAP, 1], U32).ap()
    y_dram = nc.dram_tensor("y_dram", [TBLK * CAP, D], F32).ap()
    xd_rows = x_dram.rearrange("(t p) d -> p t d", p=P)

    with ExitStack() as ctx:
        def sb(name, shape, dt=F32):
            return ctx.enter_context(nc.sbuf_tensor(name, shape, dt))

        def sem(name):
            return ctx.enter_context(nc.semaphore(name))

        wring = sb("wring", [P, 6, KD * F])
        x_sb = sb("x_sb", [P, T, D])
        arena = sb("arena", [P, 14592])
        rows = sb("rows", [P, 2 * D + KVD * 2])
        lnrow = sb("lnrow", [P, 2, 2, D])
        prm = sb("prm", [NPRM, P])
        prmT = sb("prmT", [P, NPRM])
        dwT = sb("dwT", [P, KD, 32])
        rw = sb("rw", [P, KD, E])
        ident = sb("ident", [P, P])
        upper = sb("upper", [P, P], BF16)
        ones = sb("ones", [P, P], BF16)
        mask = sb("mask", [P, 2 * P])
        rbrow = sb("rbrow", [P, E])
        sinkb = sb("sinkb", [P, NQ])
        pos_i = sb("pos_i", [T, P], I32)
        pos_f = sb("pos_f", [T, P])
        posT = sb("posT", [P, T])
        invf = sb("invf", [P, HH])
        cosb = sb("cosb", [P, T, HH])
        sinb = sb("sinb", [P, T, HH])
        tokid = sb("tokid", [P, T], U32)
        ramp4 = sb("ramp4", [P, NG])
        ramp16 = sb("ramp16", [P, E])
        ebase = sb("ebase", [P, E])
        thr = sb("thr", [P, NBLK - 1])
        zidx = sb("zidx", [P, TBLK * CAP // P], U32)
        half = sb("half", [P, 1])
        mv = sb("mv", [P, NLN, 2])
        vareps = sb("vareps", [P, NLN])
        rstd = sb("rstd", [P, NLN])
        bns = sb("bns", [P, 2, 6])
        lgs = sb("lgs", [P, T, E])
        aff = sb("aff", [P, T, E])
        gsm = sb("gsm", [P, 4, T])
        onehot = [sb(f"onehot{j}", [P, T, E]) for j in range(2)]
        gatev = sb("gatev", [P, 2, T])
        gsum = sb("gsum", [P, T])
        gate_w = sb("gate_w", [P, 2, T])
        mask_b = sb("mask_b", [P, T, E], BF16)
        rowf = sb("rowf", [P, 2, T])
        rowi = sb("rowi", [P, 2, T], U32)
        cntf = sb("cntf", [P, 4, E])
        before = sb("before", [P, E, E])
        extra = sb("extra", [1, DEPTH, E], I32)
        tok_r = sb("tok_r", [TBLK, CAP], U32)
        tok_f = sb("tok_f", [TBLK, CAP])
        tokT = sb("tokT", [CAP, TBLK], U32)
        idx = sb("idx", [CAP, 3], U32)
        exs = sb("exs", [P, 2, NQ])
        negm = sb("negm", [P, NQ])
        mxs = sb("mxs", [P, NQ])
        den = sb("den", [P, NQ])
        rden = sb("rden", [P, NQ])

        resrow, bqrow = (rows[:, i * D:(i + 1) * D] for i in range(2))
        rope_w = bqrow[:, 0:4 * T * HH].rearrange("p (a n) -> p a n", a=4)
        kvrow = rows[:, 2 * D:2 * D + 2 * KVD]

        def view(at, *shape):
            n = math.prod(shape)
            v = arena[:, at:at + n]
            if len(shape) == 2:
                v = v.rearrange("p (a b) -> p a b", a=shape[0])
            if len(shape) == 3:
                v = v.rearrange("p (a b c) -> p a b c", a=shape[0], b=shape[1])
            return v

        PADW = S + CW - 1
        xT = view(0, KD, S)
        hpad = view(4096, KD, PADW)
        cv = view(4096 + KD * PADW, KD, S)
        hc = [view(0 + i * D, KD, P) for i in range(2)]
        ntok = [view(2048 + i * D, D) for i in range(2)]
        AT = 4096 + KD * PADW + KD * S
        sgm = [view(AT + i * S, S) for i in range(2)]
        xTt = view(AT + 2 * S, KD, P)
        dw_r = view(AT, D)[0:CW, :]
        q_sb, k_sb = view(0, D), view(D, 2 * KVD)
        qr = view(1536, NQ, HD)
        kr = view(2560, NKV, 2, HD)
        tq = [view(3072 + i * S, S) for i in range(2)]
        tk = [view(4096 + i * P, P) for i in range(2)]
        kT = view(4352, NKV, S)
        v_sb = view(6400, T, KVD)
        qT = view(7424, KD, P)
        ss = [view(8448 + i * D, GQ, 2 * P) for i in range(2)]
        pr = [view(10496 + i * D, GQ, 2 * P) for i in range(2)]
        PT = view(12544, KD, P)
        o_sb = view(0, D)
        oT = view(13568, KD, P)
        xg = [view(i * D, D) for i in range(3)]
        xgT = [view(3072 + i * S, KD, CAP) for i in range(3)]
        sg = [view(4608 + i * 256, 256) for i in range(3)]
        hh = [view(5376 + i * 256, 256) for i in range(3)]
        hT = [view(6144 + i * 256, 2, P) for i in range(3)]
        ysb = [view(6912 + i * S, S) for i in range(3)]
        yg = [[view(8448 + (2 * i + j) * D, D) for j in range(2)] for i in range(2)]

        selv, seln, r1, r2 = (view(8448 + i * T * E, T, E) for i in range(4))
        gs = view(8448 + 4 * T * E, 5, T * NG)
        cmp7 = view(8448 + 6 * T * E, E, NBLK - 1)
        extras_before = view(8448 + 8 * T * E, E, E)

        ps = ctx.enter_context(nc.psum_tensor("ps", [P, 8, 512], F32))

        s_x = [sem(f"s_x{t}") for t in range(T)]
        s_small = sem("s_small")
        s_rows = sem("s_rows")
        s_rows1 = sem("s_rows1")
        s_rows2 = sem("s_rows2")
        s_pool0 = sem("s_pool0")
        s_pc = sem("s_pc")
        s_ac = sem("s_ac")
        s_dc = sem("s_dc")
        s_tokinit = sem("s_tokinit")
        s_yinit = sem("s_yinit")
        s_prT = sem("s_prT")
        s_prC = sem("s_prC")
        s_x0T = sem("s_x0T")
        s_xTd = sem("s_xTd")
        s_xTa = sem("s_xTa")
        s_w1 = [sem(f"s_w1_{i}") for i in range(4)]
        s_w2 = [sem(f"s_w2_{i}") for i in range(2)]
        s_g1 = sem("s_g1")
        s_sgm = sem("s_sgm")
        s_glu = sem("s_glu")
        s_tap = sem("s_tap")
        s_xa = sem("s_xa")
        s_At = sem("s_At")
        s_mv = sem("s_mv")
        s_rs = sem("s_rs")
        s_nt = sem("s_nt")
        s_Bt = sem("s_Bt")
        s_hc = sem("s_hc")
        s_C = sem("s_C")
        s_cadd = sem("s_cadd")
        s_ln = sem("s_ln")
        s_xst = sem("s_xst")
        s_Dt = sem("s_Dt")
        s_xTt = sem("s_xTt")
        s_lg = sem("s_lg")
        s_lgc = sem("s_lgc")
        s_aff = sem("s_aff")
        s_mask = sem("s_mask")
        s_rank = sem("s_rank")
        s_rowi = sem("s_rowi")
        s_extra = sem("s_extra")
        s_scat = sem("s_scat")
        s_tokr = sem("s_tokr")
        s_tokf = sem("s_tokf")
        s_tokt = sem("s_tokt")
        s_tokT = sem("s_tokT")
        s_wg = [sem(f"s_wg{i}") for i in range(2)]
        s_wu = [sem(f"s_wu{i}") for i in range(2)]
        s_wd = [sem(f"s_wd{i}") for i in range(2)]
        s_idx = sem("s_idx")
        s_xg = [sem(f"s_xg{i}") for i in range(2)]
        s_xt = sem("s_xt")
        s_xgT = sem("s_xgT")
        s_gate = sem("s_gate")
        s_gud = sem("s_gud")
        s_sg = sem("s_sg")
        s_up = sem("s_up")
        s_h = sem("s_h")
        s_ht = sem("s_ht")
        s_hTc = sem("s_hTc")
        s_dn = sem("s_dn")
        s_yc = sem("s_yc")
        s_y = [sem(f"s_y{i}") for i in range(2)]
        s_oidx = sem("s_oidx")
        s_oxg = sem("s_oxg")
        s_oxt = sem("s_oxt")
        s_oxgT = sem("s_oxgT")
        s_ogate = sem("s_ogate")
        s_osg = sem("s_osg")
        s_oup = sem("s_oup")
        s_oh = sem("s_oh")
        s_oht = sem("s_oht")
        s_ohTc = sem("s_ohTc")
        s_od = sem("s_od")
        s_oyc = sem("s_oyc")
        s_oy = sem("s_oy")
        s_yg = [sem(f"s_yg{i}") for i in range(2)]
        s_cmb = sem("s_cmb")
        s_rope = sem("s_rope")
        s_sin = sem("s_sin")
        s_ropeT = sem("s_ropeT")
        s_wkv = sem("s_wkv")
        s_wq = [sem(f"s_wq{i}") for i in range(2)]
        s_wo = [sem(f"s_wo{i}") for i in range(2)]
        s_X = sem("s_X")
        s_XT = sem("s_XT")
        s_kv = sem("s_kv")
        s_q = sem("s_q")
        s_kvb = sem("s_kvb")
        s_qb = sem("s_qb")
        s_kr = sem("s_kr")
        s_qr = sem("s_qr")
        s_kTt = sem("s_kTt")
        s_kT = sem("s_kT")
        s_qTt = sem("s_qTt")
        s_qT = sem("s_qT")
        s_S = sem("s_S")
        s_ss = sem("s_ss")
        s_negm = sem("s_negm")
        s_ex = sem("s_ex")
        s_pr = sem("s_pr")
        s_PTt = sem("s_PTt")
        s_PT = sem("s_PT")
        s_O = sem("s_O")
        s_o = sem("s_o")
        s_oTt = sem("s_oTt")
        s_oT = sem("s_oT")
        s_WO = sem("s_WO")
        s_wadd = sem("s_wadd")
        s_xb = sem("s_xb")
        s_out = sem("s_out")

        block = ctx.enter_context(nc.Block())

        w1_src = conv_w1[0].rearrange("(p k) (h n) -> p k h n", k=KD, h=2)
        w2_src = conv_w2[0].rearrange("(j p) n -> p j n", p=P)
        kv_src = kv_w.rearrange("(p k) n -> p k n", k=KD)
        wq_src = attn_wq[0].rearrange("(p k) n -> p k n", k=KD)
        wo_src = attn_wo[0].rearrange("(p k) n -> p k n", k=KD)
        gate_src = moe_w_gate.rearrange("l e (p k) f -> p (l e) (k f)", k=KD)
        up_src = moe_w_up.rearrange("l e (p k) f -> p (l e) (k f)", k=KD)
        down_src = moe_w_down.rearrange("l e (j p) n -> p (l e) j n", p=P)

        def slot(i, *dims):
            v = wring[:, i, :]
            if len(dims) == 1:
                return v.rearrange("p (k n) -> p k n", k=dims[0])
            return v.rearrange("p (k h n) -> p k h n", k=dims[0], h=dims[1])

        def in_register(eng, reg, value):
            if isinstance(value, int):
                return value
            eng.reg_mov(reg, value)
            return eng.snap(reg, min_val=0, max_val=1 << 16)

        @block.sync
        def _(sp):
            for t in range(T):
                sp.dma_start(x_sb[:, t, :], x_rows[:, t, :]).then_inc(s_x[t], 16)
            for i in range(4):
                for h in range(2):
                    sp.dma_start(slot(i, KD, 2)[:, :, h, :],
                                 w1_src[:, :, h, 256 * i:256 * i + 256]).then_inc(s_w1[i], 16)
            for i in range(2):
                sp.dma_start(slot(4 + i, 4), w2_src[:, 4 * i:4 * i + 4, :]).then_inc(s_w2[i], 16)

            def gate(l, e, b):
                sp.dma_start(wring[:, 3 * b, :], gate_src[:, bass.ds(E * l + e, 1), :]).then_inc(s_wg[b], 16)

            def up(l, e, b):
                sp.dma_start(wring[:, 3 * b + 1, :], up_src[:, bass.ds(E * l + e, 1), :]).then_inc(s_wu[b], 16)

            def down(l, e, b):
                sp.dma_start(slot(3 * b + 2, 4), down_src[:, bass.ds(E * l + e, 1), :, :]).then_inc(s_wd[b], 16)

            def experts_from_2(l):
                with sp.Fori(0, (E - 2) // 2) as i:
                    for b in range(2):
                        e = 2 * i + 2 + b
                        sp.wait_ge(s_gud, e + (E * l - 1))
                        gate(l, e, b)
                        up(l, e, b)
                        sp.wait_ge(s_dn, e + (E * l - 1))
                        down(l, e, b)

            sp.wait_ge(s_g1, 2)
            gate(0, 0, 0)
            sp.wait_ge(s_g1, 4)
            up(0, 0, 0)
            sp.wait_ge(s_g1, 6)
            down(0, 0, 0)
            sp.wait_ge(s_g1, 8)
            gate(0, 1, 1)
            sp.wait_ge(s_C, T)
            up(0, 1, 1)
            down(0, 1, 1)
            experts_from_2(0)
            sp.wait_ge(s_gud, E - 1)
            sp.dma_start(slot(0, KD), kv_src).then_inc(s_wkv, 16)
            sp.dma_start(slot(1, KD), wq_src[:, :, 0:512]).then_inc(s_wq[0], 16)
            sp.wait_ge(s_dn, E - 1)
            sp.dma_start(slot(2, KD), wq_src[:, :, 512:1024]).then_inc(s_wq[1], 16)
            sp.wait_ge(s_gud, E)
            sp.dma_start(slot(3, KD), wo_src[:, :, 0:512]).then_inc(s_wo[0], 16)
            sp.dma_start(slot(4, KD), wo_src[:, :, 512:1024]).then_inc(s_wo[1], 16)
            sp.wait_ge(s_dn, E)
            down(1, 1, 1)
            sp.wait_ge(s_kv, T)
            gate(1, 0, 0)
            sp.wait_ge(s_q, T)
            up(1, 0, 0)
            down(1, 0, 0)
            sp.wait_ge(s_WO, T)
            gate(1, 1, 1)
            up(1, 1, 1)
            experts_from_2(1)

        @block.tensor
        def _(pe):
            g = ctx.enter_context(pe.register("pe_extra"))
            r_pe = [ctx.enter_context(pe.register(f"pe_r{i}")) for i in range(2)]
            pe.reg_mov(g, 1)

            def transposes(bank, src, signal, count=KD, step=KD):
                for j in range(count):
                    last = pe.transpose(ps[:, bank + j // 4, (j % 4) * P:(j % 4) * P + P],
                                        src(j), ident[:, :])
                last.then_inc(signal, 1)

            pe.wait_ge(s_pool0, 1)
            pe.wait_ge(s_small, 16 * 6)
            pe.transpose(ps[:, 5, 0:NPRM], prm[:, :], ident[0:NPRM, 0:NPRM])
            for c in range(KD):
                pe.transpose(ps[:, 4, 32 * c:32 * c + CW], dw_r[:, c * P:(c + 1) * P], ident[0:CW, 0:CW])
            pe.wait_ge(s_rope, 1)
            pe.transpose(ps[:, 5, 64:64 + T], pos_f[:, :], ident[0:T, 0:T]).then_inc(s_prT, 1)
            for t in range(T):
                pe.wait_ge(s_x[t], 16)
                if t >= 2:
                    pe.wait_ge(s_xTd, t - 1)
                    pe.wait_ge(s_xTa, t - 1)
                transposes(2 * (t % 2), lambda j: x_sb[:, t, j::KD], s_x0T)
            pe.wait_ge(s_xTd, T)
            pe.wait_ge(s_xTa, T)
            for c in range(KD):
                pe.wait_ge(s_w1[c // 2], 32)
                if c == 0:
                    pe.wait_ge(s_prC, 1)
                if c >= 2:
                    pe.wait_ge(s_glu, c - 1)
                w = slot(c // 2, KD, 2)
                for h in range(2):
                    for k in range(KD):
                        last = pe.matmul(ps[:, 4 + 2 * (c % 2) + h, :],
                                         w[:, k, h, (c % 2) * P:(c % 2) * P + P], xT[:, k, :],
                                         start=(k == 0), stop=(k == KD - 1))
                last.then_inc(s_g1, 1)

            def stage_a(t):
                if t >= 1:
                    pe.wait_ge(s_nt, t)
                transposes(0, lambda c: cv[:, c, t * P:(t + 1) * P], s_At)

            def stage_b(t):
                pe.wait_ge(s_nt, t + 1)
                if t >= 1:
                    pe.wait_ge(s_hc, t)
                transposes(2, lambda c: ntok[t % 2][:, c * P:(c + 1) * P], s_Bt)

            def stage_c(t):
                pe.wait_ge(s_hc, t + 1)
                if t == 0:
                    pe.wait_ge(s_w2[0], 16)
                    pe.wait_ge(s_w2[1], 16)
                if t >= 1:
                    pe.wait_ge(s_cadd, t)
                for h in range(2):
                    for c in range(KD):
                        last = pe.matmul(ps[:, 4 + h, :], hc[t % 2][:, c, :],
                                         slot(4 + c // 4, 4)[:, c % 4, h * 512:(h + 1) * 512],
                                         start=(c == 0), stop=(c == KD - 1))
                last.then_inc(s_C, 1)

            def stage_d(l, t):
                n = T * l + t
                pe.wait_ge(s_ln, 2 * T * l + t + 1)
                if n >= 1:
                    pe.wait_ge(s_lgc, n)
                transposes(6, lambda j: x_sb[:, t, j::KD], s_Dt)
                pe.wait_ge(s_xTt, n + 1)
                for k in range(KD):
                    last = pe.matmul(ps[:, 6, 0:E], xTt[:, k, :], rw[:, k, :], start=(k == 0), stop=(k == KD - 1))
                last.then_inc(s_lg, 1)

            pe.wait_ge(s_tap, CW * KD)
            stage_a(0)
            stage_b(0)
            stage_a(1)
            for t in range(T):
                stage_c(t)
                if t + 1 < T:
                    stage_b(t + 1)
                if t + 2 < T:
                    stage_a(t + 2)
                if t >= 1:
                    stage_d(0, t - 1)
            stage_d(0, T - 1)

            def ranks(l):
                pe.wait_ge(s_mask, l + 1)
                for t in range(T):
                    for u in range(t + 1):
                        pe.matmul(ps[:, 0, t * E:(t + 1) * E], (upper if u == t else ones)[:, :], mask_b[:, u, :],
                                  start=(u == 0), stop=(u == t))
                for u in range(T):
                    last = pe.matmul(ps[:, 0, T * E:(T + 1) * E], ones[:, :], mask_b[:, u, :],
                                     start=(u == 0), stop=(u == T - 1))
                last.then_inc(s_rank, 1)
                pe.wait_ge(s_tokf, l + 1)
                pe.transpose(ps[0:CAP, 1, 0:TBLK], tok_f[:, :], ident[0:TBLK, 0:TBLK]).then_inc(s_tokt, 1)

            def gathered_T(src, signal):
                for j in range(KD):
                    last = pe.transpose(ps[:, 0, j * CAP:(j + 1) * CAP], src[0:CAP, j::KD], ident[0:CAP, 0:CAP])
                last.then_inc(signal, 1)

            def half_products(bank, act, w, signal, first=None):
                for k in range(KD):
                    for h in range(2):
                        mm = pe.matmul(ps[h * CAP:(h + 1) * CAP, bank, 0:256], act[:, k, :],
                                       w[:, k, h * 256:(h + 1) * 256], start=(k == 0), stop=(k == KD - 1))
                        if first is not None and k == 0 and h == 0:
                            mm.then_inc(first, 1)
                mm.then_inc(signal, 1)

            def down_products(bank, act, w, signal):
                for j in range(4):
                    for h in range(2):
                        mm = pe.matmul(ps[h * CAP:(h + 1) * CAP, bank, :],
                                       act[:, j % 2, (j // 2) * CAP:(j // 2 + 1) * CAP],
                                       w[:, j, h * 512:(h + 1) * 512], start=(j == 0), stop=(j == 3))
                mm.then_inc(signal, 1)

            def experts(l):
                M0 = E * l
                W0 = 8 * l

                def stage_t(e, eh, b):
                    gathered = in_register(pe, r_pe[0], 16 * (eh + (W0 + 1)))
                    copied = in_register(pe, r_pe[1], e + M0)
                    pe.wait_ge(s_pool0, 1)
                    pe.wait_ge(s_xg[b], gathered)
                    if not (l == 0 and isinstance(e, int) and e == 0):
                        pe.wait_ge(s_xgT, copied)
                    gathered_T(xg[b], s_xt)

                def stage_g(e, eh, b, first):
                    pe.wait_ge(s_wg[b], 16 * (eh + (W0 + 1)))
                    pe.wait_ge(s_xgT, e + (M0 + 1))
                    if first or l > 0:
                        pe.wait_ge(s_sg, e + M0)
                    half_products(1, xgT[b], slot(3 * b, KD), s_gate, s_gud if first else None)

                def stage_u(e, eh, b, later):
                    pe.wait_ge(s_wu[b], 16 * (eh + (W0 + 1)))
                    if later or l > 0:
                        pe.wait_ge(s_h, e + M0)
                    half_products(2, xgT[b], slot(3 * b + 1, KD), s_up)

                def stage_h(e, b, later=True, last=False):
                    pe.wait_ge(s_h, e + (M0 + 1))
                    if later or l > 0:
                        pe.wait_ge(s_hTc, e + M0)
                    for c in range(2):
                        tr = pe.transpose(ps[:, 3, c * P:(c + 1) * P], hh[b][:, c * P:(c + 1) * P], ident[:, :])
                        if last and c == 0:
                            tr.then_inc(s_gud, 1)
                    tr.then_inc(s_ht, 1)

                def stage_y(e, eh, b, later=True):
                    pe.wait_ge(s_wd[b], 16 * (eh + (W0 + 1)))
                    pe.wait_ge(s_hTc, e + (M0 + 1))
                    if later or l > 0:
                        pe.wait_ge(s_yc, e + M0)
                    down_products(4, hT[b], slot(3 * b + 2, 4), s_dn)

                def extras(e, b, ahead):
                    n = pe.value_load(extra[0:1, l, bass.ds(e, 1)], min_val=0, max_val=NBLK - 1)
                    with pe.If(n > 0):
                        with pe.Fori(0, n):
                            now = pe.snap(g, min_val=1, max_val=4096)
                            gathered = in_register(pe, r_pe[0], now * 16)
                            copied = in_register(pe, r_pe[1], e + (M0 + ahead))
                            pe.wait_ge(s_pool0, 1)
                            pe.wait_ge(s_oxg, gathered)
                            pe.wait_ge(s_xgT, copied)
                            gathered_T(xg[2], s_oxt)
                            pe.wait_ge(s_oxgT, now)
                            half_products(5, xgT[2], slot(3 * b, KD), s_ogate)
                            half_products(6, xgT[2], slot(3 * b + 1, KD), s_oup)
                            pe.wait_ge(s_oh, now)
                            for c in range(2):
                                tr = pe.transpose(ps[:, 3, c * P:(c + 1) * P], hh[2][:, c * P:(c + 1) * P],
                                                  ident[:, :])
                            tr.then_inc(s_oht, 1)
                            pe.wait_ge(s_ohTc, now)
                            pe.wait_ge(s_wd[b], 16 * (e_half(e, b) + (W0 + 1)))
                            pe.wait_ge(s_oyc, now)
                            down_products(7, hT[2], slot(3 * b + 2, 4), s_od)
                            pe.reg_add(g, g, 1)

                def e_half(e, b):
                    return halves[b]

                pe.wait_ge(s_extra, l + 1)
                halves = [0, 0]
                stage_t(0, 0, 0)
                stage_g(0, 0, 0, False)
                stage_u(0, 0, 0, False)
                stage_t(1, 0, 1)
                extras(0, 0, 2)

                def step(e, eh, b, first_h=False, last=False):
                    halves[b] = eh
                    stage_g(e, eh, b, True)
                    stage_h(e - 1, 1 - b, later=not first_h)
                    stage_u(e, eh, b, True)
                    if not last:
                        stage_t(e + 1, eh + b, 1 - b)
                    stage_y(e - 1, eh if b else eh - 1, 1 - b, later=not first_h)
                    extras(e, b, 1 if last else 2)

                step(1, 0, 1, first_h=True)
                with pe.Fori(0, (E - 4) // 2) as i:
                    step(2 * i + 2, i + 1, 0)
                    step(2 * i + 3, i + 1, 1)
                step(E - 2, E // 2 - 1, 0)
                step(E - 1, E // 2 - 1, 1, last=True)
                stage_h(E - 1, 1, last=True)
                stage_y(E - 1, E // 2 - 1, 1)

            ranks(0)
            experts(0)

            pe.wait_ge(s_wkv, 16)
            pe.wait_ge(s_wq[0], 16)
            pe.wait_ge(s_wq[1], 16)
            for t in range(T):
                pe.wait_ge(s_ln, 2 * T - T + t + 1)
                transposes(0, lambda j: x_sb[:, t, j::KD], s_X)
                pe.wait_ge(s_XT, t + 1)
                for k in range(KD):
                    last = pe.matmul(ps[:, 2, :], xTt[:, k, :], slot(0, KD)[:, k, :],
                                     start=(k == 0), stop=(k == KD - 1))
                last.then_inc(s_kv, 1)
                for h in range(2):
                    for k in range(KD):
                        last = pe.matmul(ps[:, 4 + h, :], xTt[:, k, :], slot(1 + h, KD)[:, k, :],
                                         start=(k == 0), stop=(k == KD - 1))
                last.then_inc(s_q, 1)
                pe.wait_ge(s_kr, t + 1)
                transposes(3, lambda j: kr[:, j, :, :].rearrange("p a b -> p (a b)"), s_kTt, count=NKV)
                pe.wait_ge(s_qr, t + 1)
                if t >= 1:
                    pe.wait_ge(s_lgc, T + t)
                transposes(6, lambda j: qr[:, 2 * j:2 * j + 2, :].rearrange("p a b -> p (a b)"), s_qTt)
                pe.wait_ge(s_kT, t + 1)
                pe.wait_ge(s_qT, t + 1)
                lo = 0 if t else P

                def scores(kh):
                    if kh >= 2:
                        pe.wait_ge(s_ss, NKV * t + kh - 1)
                    bank = 2 * (kh % 2)
                    for j in range(2):
                        for r in range(2):
                            part = slice(r * HD, (r + 1) * HD)
                            last = pe.matmul(ps[:, bank + r, j * 256 + lo:j * 256 + 256],
                                             qT[part, 2 * kh + j, :],
                                             kT[part, kh, (t - 1) * P + lo:(t + 1) * P],
                                             start=True, stop=True)
                    last.then_inc(s_S, 1)

                def values(kh):
                    n = NKV * t + kh
                    pe.wait_ge(s_pr, n + 1)
                    if n >= 1:
                        pe.wait_ge(s_PT, n)
                    halves = range(lo // P, 2)
                    for i in range(GQ):
                        for s in halves:
                            last = pe.transpose(ps[:, 6 + i // 2, ((2 * i + s) % 4) * P:((2 * i + s) % 4 + 1) * P],
                                                pr[n % 2][:, i, s * P:(s + 1) * P], ident[:, :])
                    last.then_inc(s_PTt, 1)
                    pe.wait_ge(s_PT, n + 1)
                    for i in range(GQ):
                        h = kh * GQ + 2 * (i % 2) + i // 2
                        for s in halves:
                            last = pe.matmul(ps[:, 4 + h // 8, (h % 8) * HD:(h % 8 + 1) * HD],
                                             PT[:, 2 * i + s, :],
                                             v_sb[:, t - 1 + s, kh * HD:(kh + 1) * HD],
                                             start=(s == halves[0]), stop=(s == 1))
                    last.then_inc(s_O, 1)

                pe.wait_ge(s_qb, t + 1)
                scores(0)
                for kh in range(NKV):
                    if kh + 1 < NKV:
                        scores(kh + 1)
                    values(kh)
                pe.wait_ge(s_o, t + 1)
                transposes(0, lambda j: o_sb[:, j::KD], s_oTt)
                pe.wait_ge(s_oT, t + 1)
                pe.wait_ge(s_wo[0], 16)
                pe.wait_ge(s_wo[1], 16)
                for h in range(2):
                    for k in range(KD):
                        last = pe.matmul(ps[:, 2 + h, :], oT[:, k, :], slot(3 + h, KD)[:, k, :],
                                         start=(k == 0), stop=(k == KD - 1))
                last.then_inc(s_WO, 1)
                stage_d(1, t)
            ranks(1)
            experts(1)

        @block.vector
        def _(dve):
            done = [0]
            g = ctx.enter_context(dve.register("dve_extra"))
            dve.reg_mov(g, 1)

            def own(ins):
                done[0] += 1
                ins.then_inc(s_dc, 1)
                dve.wait_ge(s_dc, done[0])

            dve.wait_ge(s_prT, 1)
            dve.tensor_copy(prmT[:, :], ps[:, 5, 0:NPRM])
            dve.tensor_copy(posT[:, :], ps[:, 5, 64:64 + T])
            dve.tensor_copy(dwT[:, :, 0:CW], ps[:, 4, 0:32 * KD].rearrange("p (c k) -> p c k", k=32)[:, :, 0:CW]
                            ).then_inc(s_prC, 1)
            for t in range(T):
                dve.wait_ge(s_x0T, t + 1)
                dve.tensor_copy(xT[:, 0:4, t * P:(t + 1) * P],
                                ps[:, 2 * (t % 2), :].rearrange("p (j n) -> p j n", j=4)).then_inc(s_xTd, 1)
            dve.wait_ge(s_pool0, 2)
            dve.wait_ge(s_yinit, 16)
            dve.wait_ge(s_prC, 1)
            with dve.Fori(0, KD // 2) as i:
                for b in range(2):
                    c = 2 * i + b
                    one = bass.ds(c, 1)
                    dve.wait_ge(s_g1, c + 1)
                    dve.wait_ge(s_sgm, c + 1)
                    dve.scalar_tensor_tensor(out=hpad[:, one, CW - 1:PADW], in0=ps[:, 4 + 2 * b, :],
                                             scalar=prmT[:, bass.ds(c + PB1, 1)], in1=sgm[b],
                                             op0=ALU.add, op1=ALU.mult).then_inc(s_glu, 1)
                    dve.wait_ge(s_glu, c + 1)
                    dve.tensor_scalar(cv[:, one, :], hpad[:, one, 0:S], dwT[:, one, 0:1],
                                      prmT[:, bass.ds(c + PDWB, 1)], ALU.mult, ALU.add).then_inc(s_tap, 1)
                    for k in range(1, CW):
                        dve.wait_ge(s_tap, c * CW + k)
                        dve.scalar_tensor_tensor(out=cv[:, one, :], in0=hpad[:, one, k:k + S],
                                                 scalar=dwT[:, one, k:k + 1], in1=cv[:, one, :],
                                                 op0=ALU.mult, op1=ALU.add).then_inc(s_tap, 1)

            def moments(src, n, signal):
                for h in range(2):
                    ins = dve.bn_stats(bns[:, h, :], src(h))
                own(ins)
                dve.bn_aggr(mv[:, n, :], bns[:, :, :]).then_inc(signal, 1)

            def norm_conv(t, n):
                dve.wait_ge(s_At, t + 1)
                moments(lambda h: ps[:, h, :], n, s_mv)
                dve.wait_ge(s_rs, n + 1)
                dve.wait_ge(s_mv, n + 1)
                if t >= 2:
                    dve.wait_ge(s_Bt, t - 1)
                dve.tensor_scalar(ntok[t % 2], ps[:, 0:2, :].rearrange("p a b -> p (a b)"), mv[:, n, 0:1],
                                  rstd[:, n:n + 1], ALU.subtract, ALU.mult).then_inc(s_nt, 1)

            def norm_x(t, n, l, which):
                xt = x_sb[:, t, :]
                moments(lambda h: x_sb[:, t, h * 512:(h + 1) * 512], n, s_mv)
                dve.wait_ge(s_mv, n + 1)
                own(dve.scalar_tensor_tensor(out=xt, in0=xt, scalar=mv[:, n, 0:1], in1=lnrow[:, which, 0, :],
                                             op0=ALU.subtract, op1=ALU.mult))
                dve.wait_ge(s_rs, n + 1)
                dve.scalar_tensor_tensor(out=xt, in0=xt, scalar=rstd[:, n:n + 1], in1=lnrow[:, which, 1, :],
                                         op0=ALU.mult, op1=ALU.add).then_inc(s_ln, 1)

            def add_product(t, bank, signal, count):
                for h in range(2):
                    ins = dve.tensor_tensor(x_sb[:, t, h * 512:(h + 1) * 512], x_sb[:, t, h * 512:(h + 1) * 512],
                                            ps[:, bank + h, :], ALU.add)
                ins.then_inc(signal, 1)
                dve.wait_ge(signal, count)

            def keep_logits(l, t):
                dve.wait_ge(s_lg, T * l + t + 1)
                dve.tensor_copy(lgs[:, t, :], ps[:, 6, 0:E]).then_inc(s_lgc, 1)

            dve.wait_ge(s_rows, 16 * 8)
            n = 0
            norm_conv(0, n)
            n += 1
            norm_conv(1, n)
            n += 1
            for t in range(T):
                dve.wait_ge(s_C, t + 1)
                dve.wait_ge(s_xa, t + 1)
                add_product(t, 4, s_cadd, t + 1)
                norm_x(t, n, 0, 0)
                n += 1
                if t + 2 < T:
                    norm_conv(t + 2, n)
                    n += 1
                if t >= 1:
                    keep_logits(0, t - 1)
            keep_logits(0, T - 1)

            def route(l):
                dve.wait_ge(s_aff, l + 1)
                tg = "p t (g e) -> p (t g) e"
                own(dve.tensor_tensor(selv[:, :, :], aff[:, :, :], rbrow[:, :].unsqueeze(1).to_broadcast([P, T, E]),
                                      ALU.add))
                v = selv[:, :, :].rearrange(tg, g=NG)
                a, b, c, d = (v[:, :, i] for i in range(EPG))
                dve.tensor_tensor(gs[:, 0, :], a, b, ALU.max)
                dve.tensor_tensor(gs[:, 1, :], a, b, ALU.min)
                dve.tensor_tensor(gs[:, 2, :], c, d, ALU.max)
                own(dve.tensor_tensor(gs[:, 3, :], c, d, ALU.min))
                dve.tensor_tensor(gs[:, 4, :], gs[:, 0, :], gs[:, 2, :], ALU.max)
                dve.tensor_tensor(gs[:, 1, :], gs[:, 1, :], gs[:, 3, :], ALU.max)
                own(dve.tensor_tensor(gs[:, 0, :], gs[:, 0, :], gs[:, 2, :], ALU.min))
                own(dve.tensor_tensor(gs[:, 1, :], gs[:, 1, :], gs[:, 0, :], ALU.max))
                own(dve.tensor_tensor(gs[:, 4, :], gs[:, 4, :], gs[:, 1, :], ALU.add))

                def first_of_max(score, width, ramp, out, tmp):
                    shape = [P, T, width]
                    rampb = ramp[:, :].unsqueeze(1).to_broadcast(shape)
                    own(dve.tensor_reduce(gsm[:, 0, :], score, AX.X, ALU.max))
                    own(dve.tensor_tensor(tmp, score, gsm[:, 0, :].unsqueeze(2).to_broadcast(shape), ALU.is_equal))
                    own(dve.tensor_tensor(tmp, tmp, rampb, ALU.mult))
                    own(dve.tensor_reduce(gsm[:, 1, :], tmp, AX.X, ALU.min))
                    own(dve.tensor_tensor(out, rampb, gsm[:, 1, :].unsqueeze(2).to_broadcast(shape), ALU.is_equal))

                def tgv(i):
                    return gs[:, i, :].rearrange("p (t g) -> p t g", g=NG)

                first_of_max(tgv(4), NG, ramp4, tgv(0), tgv(1))
                own(dve.tensor_scalar(gs[:, 1, :], gs[:, 0, :], -NEG, NEG, ALU.mult, ALU.add))
                full = [P, T * NG, EPG]
                sv = seln[:, :, :].rearrange(tg, g=NG)
                own(dve.tensor_tensor(sv, v, gs[:, 0, :].unsqueeze(2).to_broadcast(full), ALU.mult))
                own(dve.tensor_tensor(sv, sv, gs[:, 1, :].unsqueeze(2).to_broadcast(full), ALU.add))
                for j in range(2):
                    first_of_max(seln[:, :, :], E, ramp16, onehot[j][:, :, :], r1[:, :, :])
                    own(dve.tensor_tensor(r2[:, :, :], aff[:, :, :], onehot[j][:, :, :], ALU.mult))
                    own(dve.tensor_reduce(gatev[:, j, :], r2[:, :, :], AX.X, ALU.add))
                    if j == 0:
                        own(dve.scalar_tensor_tensor(out=seln[:, :, :], in0=onehot[0][:, :, :], scalar=-3e38,
                                                     in1=seln[:, :, :], op0=ALU.mult, op1=ALU.add))
                dve.tensor_tensor(mask_b[:, :, :], onehot[0][:, :, :], onehot[1][:, :, :], ALU.add).then_inc(s_mask, 1)
                own(dve.tensor_tensor(gsum[:, :], gatev[:, 0, :], gatev[:, 1, :], ALU.add))
                own(dve.reciprocal(gsum[:, :], gsum[:, :]))
                own(dve.tensor_tensor(gate_w[:, :, :], gatev[:, :, :],
                                      gsum[:, :].unsqueeze(1).to_broadcast([P, 2, T]), ALU.mult))
                dve.wait_ge(s_rank, l + 1)
                count, more, first, shift = (cntf[:, i, :] for i in range(4))
                own(dve.tensor_copy(count, ps[:, 0, T * E:(T + 1) * E]))
                shape = [P, E, NBLK - 1]
                own(dve.tensor_tensor(cmp7[:, :, :], count.unsqueeze(2).to_broadcast(shape),
                                      thr[:, :].unsqueeze(1).to_broadcast(shape), ALU.is_gt))
                own(dve.tensor_reduce(more, cmp7[:, :, :], AX.X, ALU.add))
                dve.tensor_copy(extra[:, l, :], more[0:1, :]).then_inc(s_extra, 1)
                own(dve.tensor_tensor(extras_before[:, :, :], before[:, :, :],
                                      more.unsqueeze(1).to_broadcast([P, E, E]), ALU.mult))
                own(dve.tensor_reduce(first, extras_before[:, :, :], AX.X, ALU.add))
                own(dve.scalar_tensor_tensor(out=shift, in0=first, scalar=float(CAP), in1=ebase[:, :],
                                             op0=ALU.mult, op1=ALU.subtract))
                own(dve.tensor_scalar(shift, shift, float(CAP * (E - 1)), None, ALU.add))
                rank = ps[:, 0, 0:T * E].rearrange("p (t e) -> p t e", e=E)
                wide = [P, T, E]
                own(dve.tensor_scalar(r1[:, :, :], rank, float(CAP), None, ALU.is_ge))
                own(dve.tensor_tensor(r1[:, :, :], r1[:, :, :], shift.unsqueeze(1).to_broadcast(wide), ALU.mult))
                own(dve.tensor_tensor(r1[:, :, :], r1[:, :, :], rank, ALU.add))
                own(dve.tensor_tensor(r1[:, :, :], r1[:, :, :], ebase[:, :].unsqueeze(1).to_broadcast(wide), ALU.add))
                for j in range(2):
                    own(dve.tensor_tensor(r2[:, :, :], r1[:, :, :], onehot[j][:, :, :], ALU.mult))
                    own(dve.tensor_reduce(rowf[:, j, :], r2[:, :, :], AX.X, ALU.add))
                dve.tensor_copy(rowi[:, :, :], rowf[:, :, :]).then_inc(s_rowi, 1)
                dve.wait_ge(s_tokr, 16 * (l + 1))
                dve.tensor_copy(tok_f[:, :], tok_r[:, :]).then_inc(s_tokf, 1)
                dve.wait_ge(s_tokt, l + 1)
                dve.tensor_copy(tokT[:, :], ps[0:CAP, 1, 0:TBLK]).then_inc(s_tokT, 1)

            def experts(l):
                M0 = E * l

                def copy_t(e, b, later):
                    dve.wait_ge(s_xt, e + (M0 + 1))
                    if later or l > 0:
                        dve.wait_ge(s_up, e + (M0 - 1))
                    dve.tensor_copy(xgT[b].rearrange("p a b -> p (a b)"), ps[:, 0, :]).then_inc(s_xgT, 1)

                def gated(e, b, later):
                    dve.wait_ge(s_up, e + (M0 + 1))
                    dve.wait_ge(s_sg, e + (M0 + 1))
                    if later or l > 0:
                        dve.wait_ge(s_ht, e + (M0 - 1))
                    dve.tensor_tensor(hh[b], sg[b], ps[:, 2, 0:256], ALU.mult).then_inc(s_h, 1)

                def copy_h(e, b, later):
                    dve.wait_ge(s_ht, e + (M0 + 1))
                    if later or l > 0:
                        dve.wait_ge(s_dn, e + (M0 - 1))
                    dve.tensor_copy(hT[b].rearrange("p a b -> p (a b)"), ps[:, 3, 0:256]).then_inc(s_hTc, 1)

                def extras(e):
                    k = dve.value_load(extra[0:1, l, bass.ds(e, 1)], min_val=0, max_val=NBLK - 1)
                    with dve.If(k > 0):
                        with dve.Fori(0, k):
                            now = dve.snap(g, min_val=1, max_val=4096)
                            dve.wait_ge(s_oxt, now + 1)
                            dve.tensor_copy(xgT[2].rearrange("p a b -> p (a b)"), ps[:, 0, :]).then_inc(s_oxgT, 1)
                            dve.wait_ge(s_oup, now)
                            dve.wait_ge(s_osg, now)
                            dve.tensor_tensor(hh[2], sg[2], ps[:, 6, 0:256], ALU.mult).then_inc(s_oh, 1)
                            dve.wait_ge(s_oht, now)
                            dve.tensor_copy(hT[2].rearrange("p a b -> p (a b)"), ps[:, 3, 0:256]).then_inc(s_ohTc, 1)
                            dve.reg_add(g, g, 1)

                dve.wait_ge(s_extra, l + 1)
                copy_t(0, 0, False)
                gated(0, 0, False)
                copy_t(1, 1, False)
                extras(0)
                copy_h(0, 0, False)
                gated(1, 1, False)
                copy_t(2, 0, True)
                extras(1)

                def step(e, b, last=False):
                    copy_h(e - 1, 1 - b, True)
                    gated(e, b, True)
                    if not last:
                        copy_t(e + 1, 1 - b, True)
                    extras(e)

                with dve.Fori(0, (E - 4) // 2) as i:
                    step(2 * i + 2, 0)
                    step(2 * i + 3, 1)
                step(E - 2, 0)
                step(E - 1, 1, last=True)
                copy_h(E - 1, 1, True)

            def combine(l, n):
                for t in range(T):
                    b = t % 2
                    dve.wait_ge(s_yg[b], 32 * (2 * l + t // 2 + 1))
                    y0, y1 = yg[b]
                    own(dve.tensor_scalar(y0, y0, gate_w[:, 0, t:t + 1], None, ALU.mult))
                    own(dve.scalar_tensor_tensor(out=y0, in0=y1, scalar=gate_w[:, 1, t:t + 1], in1=y0,
                                                 op0=ALU.mult, op1=ALU.add))
                    dve.scalar_tensor_tensor(out=x_sb[:, t, :], in0=x_sb[:, t, :], scalar=ALPHA, in1=y0,
                                             op0=ALU.mult, op1=ALU.add).then_inc(s_cmb, 1)
                    dve.wait_ge(s_cmb, T * l + t + 1)
                    norm_x(t, n + t, l, 1)

            route(0)
            experts(0)
            combine(0, n)
            n += T

            dve.wait_ge(s_ropeT, 1)
            dve.wait_ge(s_rows1, 16 * 5)
            for t in range(T):
                dve.wait_ge(s_kv, t + 1)
                dve.tensor_tensor(v_sb[:, t, :], ps[:, 2, KVD:2 * KVD], kvrow[:, KVD:2 * KVD], ALU.add)
                own(dve.tensor_tensor(k_sb[:, 0:KVD], ps[:, 2, 0:KVD], kvrow[:, 0:KVD], ALU.add))

                def rotate(src, heads, dst, tmp):
                    cs = cosb[:, t, :].unsqueeze(1).to_broadcast([P, heads, HH])
                    sn = sinb[:, t, :].unsqueeze(1).to_broadcast([P, heads, HH])
                    lo, hi = src[:, :, 0:HH], src[:, :, HH:HD]
                    ta = tmp[0].rearrange("p (h d) -> p h d", h=heads)
                    tb = tmp[1].rearrange("p (h d) -> p h d", h=heads)
                    dve.tensor_tensor(ta, lo, cs, ALU.mult)
                    own(dve.tensor_tensor(tb, hi, sn, ALU.mult))
                    own(dve.tensor_tensor(dst[0], ta, tb, ALU.subtract))
                    dve.tensor_tensor(ta, hi, cs, ALU.mult)
                    own(dve.tensor_tensor(tb, lo, sn, ALU.mult))
                    return dve.tensor_tensor(dst[1], ta, tb, ALU.add)

                if t >= 1:
                    dve.wait_ge(s_kTt, t)
                own(rotate(k_sb[:, 0:KVD].rearrange("p (h d) -> p h d", h=NKV), NKV,
                           (kr[:, :, 0, 0:HH], kr[:, :, 0, HH:HD]), tk))
                dve.tensor_copy(kr[:, :, 1, :], kr[:, :, 0, :]).then_inc(s_kr, 1)
                dve.wait_ge(s_q, t + 1)
                dve.tensor_tensor(q_sb, ps[:, 4:6, :].rearrange("p a b -> p (a b)"), bqrow, ALU.add).then_inc(s_qb, 1)
                dve.wait_ge(s_qb, t + 1)
                if t >= 1:
                    dve.wait_ge(s_qTt, t)
                rotate(q_sb.rearrange("p (h d) -> p h d", h=NQ), NQ,
                       (qr[:, :, 0:HH], qr[:, :, HH:HD]), tq).then_inc(s_qr, 1)
                dve.wait_ge(s_kTt, t + 1)
                dve.tensor_copy(kT[:, :, t * P:(t + 1) * P], ps[:, 3, :].rearrange("p (h n) -> p h n", h=NKV)
                                ).then_inc(s_kT, 1)
                lo = 0 if t else P
                for kh in range(NKV):
                    m = NKV * t + kh
                    b = m % 2
                    dve.wait_ge(s_S, m + 1)
                    if m >= 2:
                        dve.wait_ge(s_pr, m - 1)
                    bank = 2 * (kh % 2)
                    sc = ps[:, bank:bank + 2, :].rearrange("p a (j s) -> p (a j) s", j=2)[:, :, lo:256]
                    sv = ss[b][:, :, lo:256]
                    dve.scalar_tensor_tensor(out=sv, in0=sc, scalar=1.0 / math.sqrt(HD),
                                             in1=mask[:, lo:256].unsqueeze(1).to_broadcast([P, GQ, 256 - lo]),
                                             op0=ALU.mult, op1=ALU.add).then_inc(s_ss, 1)
                    dve.wait_ge(s_ss, m + 1)
                    gq = slice(kh * GQ, (kh + 1) * GQ)
                    own(dve.tensor_reduce(mxs[:, gq], sv, AX.X, ALU.max))
                    sk = sinkb[:, gq].rearrange("p (j r) -> p r j", r=2)
                    mx = mxs[:, gq].rearrange("p (r j) -> p r j", r=2)
                    own(dve.tensor_tensor(mx, mx, sk, ALU.max))
                    dve.tensor_tensor(exs[:, 0, gq].rearrange("p (r j) -> p r j", r=2), sk, mx, ALU.subtract)
                    dve.tensor_scalar(negm[:, gq], mxs[:, gq], -1.0, None, ALU.mult).then_inc(s_negm, 1)
                dve.wait_ge(s_pr, NKV * (t + 1))
                own(dve.tensor_tensor(den[:, :], den[:, :], exs[:, 1, :], ALU.add))
                own(dve.reciprocal(rden[:, :], den[:, :]))
                dve.wait_ge(s_O, NKV * (t + 1))
                if t >= 1:
                    dve.wait_ge(s_oTt, t)
                for kh in range(NKV):
                    o4 = o_sb[:, kh * 256:(kh + 1) * 256]
                    p4 = ps[:, 4 + kh // 2, (kh % 2) * 256:(kh % 2 + 1) * 256]
                    for r in range(2):
                        ov = o4.rearrange("p (j r d) -> p j r d", r=2, d=HD)[:, :, r, :]
                        pv = p4.rearrange("p (j r d) -> p j r d", r=2, d=HD)[:, :, r, :]
                        rd = rden[:, kh * GQ + 2 * r:kh * GQ + 2 * r + 2].unsqueeze(2).to_broadcast([P, 2, HD])
                        last = dve.tensor_tensor(ov, pv, rd, ALU.mult)
                last.then_inc(s_o, 1)
                dve.wait_ge(s_WO, t + 1)
                dve.wait_ge(s_xb, t + 1)
                add_product(t, 2, s_wadd, t + 1)
                norm_x(t, n, 1, 0)
                n += 1
                keep_logits(1, t)
            route(1)
            experts(1)
            dve.wait_ge(s_rows2, 16 * 2)
            combine(1, n)

        @block.scalar
        def _(act):
            g = ctx.enter_context(act.register("act_extra"))
            act.reg_mov(g, 1)
            nth = ctx.enter_context(act.register("act_nth"))
            act.sem_inc(s_oyc, 1)
            act.sem_inc(s_oy, 32)
            act.dma_start(prm[PB1:PB1 + 16, :], conv_b1.rearrange("a (j p) -> (a j) p", p=P)).then_inc(s_small, 16)
            act.dma_start(prm[PDWB:PDWB + KD, :], conv_dwb.rearrange("a (j p) -> (a j) p", p=P)).then_inc(s_small, 16)
            act.dma_start(prm[PGAM:PGAM + KD, :], conv_ln_g.rearrange("a (j p) -> (a j) p", p=P)).then_inc(s_small, 16)
            act.dma_start(prm[PBET:PBET + KD, :], conv_ln_b.rearrange("a (j p) -> (a j) p", p=P)).then_inc(s_small, 16)
            act.dma_start(dw_r[:, :], conv_dw[0]).then_inc(s_small, 16)
            act.dma_start(pos_i[:, :], positions.rearrange("a (t p) -> (a t) p", p=P)).then_inc(s_small, 16)

            def norm_rows(l, w, signal):
                act.dma_start(lnrow[:, w, 0, :], ln_g[l, w].partition_broadcast(P)).then_inc(signal, 16)
                act.dma_start(lnrow[:, w, 1, :], ln_b[l, w].partition_broadcast(P)).then_inc(signal, 16)

            act.wait_ge(s_pool0, 2)
            act.dma_start(y_dram.rearrange("(p n) (h d) -> p (n h) d", p=P, h=2),
                          cv[:, KD - 1, :].unsqueeze(1).to_broadcast([P, TBLK * CAP // P * 2, S])).then_inc(s_yinit, 16)
            act.dma_start(resrow, conv_b2[0].partition_broadcast(P)).then_inc(s_rows, 16)
            act.dma_start(rw[:, :, :], router_w.rearrange("(p k) e -> p k e", k=KD)).then_inc(s_rows, 16)
            for w in range(2):
                norm_rows(0, w, s_rows)
            act.dma_start(rbrow[:, :], router_b.partition_broadcast(P)).then_inc(s_rows, 16)
            act.dma_start(sinkb[:, :], attn_sinks[0].partition_broadcast(P)).then_inc(s_rows, 16)
            for t in range(T):
                act.wait_ge(s_x0T, t + 1)
                act.activation(xT[:, 4:8, t * P:(t + 1) * P],
                               ps[:, 2 * (t % 2) + 1, :].rearrange("p (j n) -> p j n", j=4), ACT.Copy
                               ).then_inc(s_xTa, 1)
            act.wait_ge(s_prC, 1)
            for c in range(KD):
                act.wait_ge(s_g1, c + 1)
                if c >= 2:
                    act.wait_ge(s_glu, c - 1)
                act.activation(sgm[c % 2], ps[:, 5 + 2 * (c % 2), :], ACT.Sigmoid,
                               bias=prmT[:, PB1 + KD + c:PB1 + KD + c + 1]).then_inc(s_sgm, 1)
            act.wait_ge(s_rope, 2)
            act.activation(rope_w[:, 1, :], rope_w[:, 0, :], ACT.Sin, scale=0.5)
            act.activation(rope_w[:, 3, :], rope_w[:, 2, :], ACT.Sin, scale=1.0).then_inc(s_sin, 1)

            def silu_conv(t):
                act.wait_ge(s_Bt, t + 1)
                if t >= 2:
                    act.wait_ge(s_C, t - 1)
                for c in range(KD):
                    ins = act.activation(hc[t % 2][:, c, :], ps[:, 2 + c // 4, (c % 4) * P:(c % 4 + 1) * P], ACT.Silu,
                                         bias=prmT[:, PBET + c:PBET + c + 1], scale=prmT[:, PGAM + c:PGAM + c + 1])
                ins.then_inc(s_hc, 1)

            def normed(l, t):
                act.wait_ge(s_ln, 2 * T * l + t + 1)
                act.dma_start(xd_rows[:, t, :], x_sb[:, t, :]).then_inc(s_xst, 16)
                act.wait_ge(s_Dt, T * l + t + 1)
                act.activation(xTt.rearrange("p a b -> p (a b)"), ps[:, 6:8, :].rearrange("p a b -> p (a b)"),
                               ACT.Copy).then_inc(s_xTt, 1)

            silu_conv(0)
            for t in range(T):
                if t + 1 < T:
                    silu_conv(t + 1)
                if t >= 1:
                    normed(0, t - 1)
            normed(0, T - 1)
            act.dma_start(resrow, attn_bo[0].partition_broadcast(P)).then_inc(s_rows1, 16)
            norm_rows(1, 0, s_rows1)
            act.wait_ge(s_ropeT, 1)
            act.dma_start(bqrow, attn_bq[0].partition_broadcast(P)).then_inc(s_rows1, 16)
            act.dma_start(kvrow, kv_b.partition_broadcast(P)).then_inc(s_rows1, 16)

            def affinities(l):
                act.wait_ge(s_lgc, T * (l + 1))
                act.activation(aff[:, :, :], lgs[:, :, :], ACT.Sigmoid).then_inc(s_aff, 1)

            def experts(l):
                M0 = E * l

                def silu(e, b, later):
                    act.wait_ge(s_gate, e + (M0 + 1))
                    if later or l > 0:
                        act.wait_ge(s_h, e + (M0 - 1))
                    act.activation(sg[b], ps[:, 1, 0:256], ACT.Silu).then_inc(s_sg, 1)

                def store(e, eh, b, later):
                    act.wait_ge(s_dn, e + (M0 + 1))
                    if later or l > 0:
                        act.wait_ge(s_y[b], 32 * (eh + 8 * l))
                    act.activation(ysb[b], ps[:, 4, :], ACT.Copy).then_inc(s_yc, 1)
                    act.wait_ge(s_yc, e + (M0 + 1))
                    for h in range(2):
                        act.dma_start(y_dram[bass.ds(e * CAP, CAP), h * 512:(h + 1) * 512],
                                      ysb[b][h * CAP:(h + 1) * CAP, :]).then_inc(s_y[b], 16)

                def extras(e):
                    n = act.value_load(extra[0:1, l, bass.ds(e, 1)], min_val=0, max_val=NBLK - 1)
                    with act.If(n > 0):
                        with act.Fori(0, n):
                            now = act.snap(g, min_val=1, max_val=4096)
                            row = act.snap(nth, min_val=0, max_val=E - 2) * CAP + E * CAP
                            act.wait_ge(s_ogate, now)
                            act.activation(sg[2], ps[:, 5, 0:256], ACT.Silu).then_inc(s_osg, 1)
                            act.wait_ge(s_od, now)
                            act.wait_ge(s_oy, now * 32)
                            act.activation(ysb[2], ps[:, 7, :], ACT.Copy).then_inc(s_oyc, 1)
                            act.wait_ge(s_oyc, now + 1)
                            for h in range(2):
                                act.dma_start(y_dram[bass.ds(row, CAP), h * 512:(h + 1) * 512],
                                              ysb[2][h * CAP:(h + 1) * CAP, :]).then_inc(s_oy, 16)
                            act.reg_add(g, g, 1)
                            act.reg_add(nth, nth, 1)

                act.wait_ge(s_extra, l + 1)
                act.reg_mov(nth, 0)
                silu(0, 0, False)
                extras(0)
                silu(1, 1, False)
                store(0, 0, 0, False)
                extras(1)
                silu(2, 0, True)
                store(1, 0, 1, False)
                extras(2)
                silu(3, 1, True)
                store(2, 1, 0, True)
                extras(3)
                with act.Fori(0, (E - 4) // 2) as i:
                    silu(2 * i + 4, 0, True)
                    store(2 * i + 3, i + 1, 1, True)
                    extras(2 * i + 4)
                    silu(2 * i + 5, 1, True)
                    store(2 * i + 4, i + 2, 0, True)
                    extras(2 * i + 5)
                store(E - 1, E // 2 - 1, 1, True)

            affinities(0)
            experts(0)
            for t in range(T):
                act.wait_ge(s_X, t + 1)
                act.activation(xTt.rearrange("p a b -> p (a b)"), ps[:, 0:2, :].rearrange("p a b -> p (a b)"),
                               ACT.Copy).then_inc(s_XT, 1)
                act.wait_ge(s_qTt, t + 1)
                act.activation(qT.rearrange("p a b -> p (a b)"), ps[:, 6:8, :].rearrange("p a b -> p (a b)"),
                               ACT.Copy).then_inc(s_qT, 1)
                lo = 0 if t else P

                def exps(kh):
                    m = NKV * t + kh
                    act.wait_ge(s_negm, m + 1)
                    if m >= 2:
                        act.wait_ge(s_PTt, m - 1)
                    for i in range(GQ):
                        h = kh * GQ + i
                        act.activation(pr[m % 2][:, i, lo:256], ss[m % 2][:, i, lo:256], ACT.Exp,
                                       bias=negm[:, h:h + 1], accum_out=den[:, h:h + 1])
                    gq = slice(kh * GQ, (kh + 1) * GQ)
                    act.activation(exs[:, 1, gq], exs[:, 0, gq], ACT.Exp).then_inc(s_pr, 1)

                def keep_pt(kh):
                    m = NKV * t + kh
                    act.wait_ge(s_PTt, m + 1)
                    if m >= 1:
                        act.wait_ge(s_O, m)
                    pt = PT.rearrange("p (i s) n -> p i s n", s=2)[:, :, lo // P:2, :]
                    src = ps[:, 6:8, :].rearrange("p a (i s n) -> p (a i) s n", i=2, s=2)[:, :, lo // P:2, :]
                    act.activation(pt, src, ACT.Copy).then_inc(s_PT, 1)

                exps(0)
                for kh in range(NKV):
                    if kh + 1 < NKV:
                        exps(kh + 1)
                    keep_pt(kh)
                act.wait_ge(s_oTt, t + 1)
                act.activation(oT.rearrange("p a b -> p (a b)"), ps[:, 0:2, :].rearrange("p a b -> p (a b)"),
                               ACT.Copy).then_inc(s_oT, 1)
                normed(1, t)
            norm_rows(1, 1, s_rows2)
            affinities(1)
            experts(1)
            for t in range(T):
                act.wait_ge(s_ln, 3 * T + t + 1)
                act.dma_start(out_rows[:, t, :], x_sb[:, t, :]).then_inc(s_out, 16)
            act.wait_ge(s_out, 16 * T)

        @block.gpsimd
        def _(pool):
            done = [0]
            g = ctx.enter_context(pool.register("pool_extra"))
            r_pool = ctx.enter_context(pool.register("pool_r"))
            pool.reg_mov(g, 1)
            nth = ctx.enter_context(pool.register("pool_nth"))
            pool.sem_inc(s_oxt, 1)

            def own(ins):
                done[0] += 1
                ins.then_inc(s_pc, 1)
                pool.wait_ge(s_pc, done[0])

            own(pool.memset(ident[:, :], 0.0))
            pool.affine_select(out=ident[:, :], in_=ident[:, :], compare_op=ALU.not_equal, fill=1.0, base=0,
                               pattern=[[-1, P]], channel_multiplier=1).then_inc(s_pool0, 1)
            pool.memset(half[:, :], -0.5)
            pool.memset(cv[:, KD - 1, :], 0.0)
            pool.memset(hpad[:, :, 0:CW - 1], 0.0).then_inc(s_pool0, 1)
            pool.wait_ge(s_small, 16 * 6)
            pool.tensor_copy(pos_f[:, :], pos_i[:, :]).then_inc(s_rope, 1)
            own(pool.memset(zidx[:, :], 0))
            pool.dma_start(tok_dram.rearrange("(p n) a -> p (n a)", p=P), zidx[:, :]).then_inc(s_tokinit, 16)
            own(pool.memset(ones[:, :], 1.0))
            pool.affine_select(out=upper[:, :], in_=ones[:, :], compare_op=ALU.is_gt, fill=0.0, base=0,
                               pattern=[[1, P]], channel_multiplier=-1)
            own(pool.memset(before[:, :, :], 1.0))
            pool.affine_select(out=before[:, :, :], in_=before[:, :, :], compare_op=ALU.is_gt, fill=0.0, base=0,
                               pattern=[[1, E], [-1, E]], channel_multiplier=0)
            own(pool.memset(mask[:, :], 0.0))
            pool.affine_select(out=mask[:, 0:P], in_=mask[:, 0:P], compare_op=ALU.is_gt, fill=NEG, base=0,
                               pattern=[[1, P]], channel_multiplier=-1)
            pool.affine_select(out=mask[:, P:2 * P], in_=mask[:, P:2 * P], compare_op=ALU.is_ge, fill=NEG, base=0,
                               pattern=[[-1, P]], channel_multiplier=1)
            pool.iota(tokid[:, :], pattern=[[P, T]], base=0, channel_multiplier=1)
            exact = {"allow_small_or_imprecise_dtypes": True}
            pool.iota(ramp4[:, :], pattern=[[1, NG]], base=-NG, channel_multiplier=0, **exact)
            pool.iota(ramp16[:, :], pattern=[[1, E]], base=-E, channel_multiplier=0, **exact)
            pool.iota(ebase[:, :], pattern=[[CAP, E]], base=0, channel_multiplier=0, **exact)
            own(pool.iota(thr[:, :], pattern=[[CAP, NBLK - 1]], base=CAP, channel_multiplier=0, **exact))
            for i in range(HH):
                ins = pool.memset(invf[:, i:i + 1], float(THETA ** (-2.0 * i / HD)))
            own(ins)
            pool.wait_ge(s_x0T, T)
            pool.wait_ge(s_rows, 16 * 8)
            for t in range(T):
                own(pool.tensor_scalar(x_sb[:, t, :], x_sb[:, t, :], ALPHA, None, ALU.mult))
                pool.tensor_tensor(x_sb[:, t, :], x_sb[:, t, :], resrow, ALU.add).then_inc(s_xa, 1)
            pool.wait_ge(s_prC, 1)
            ang, turns, tmp = rope_w[:, 0, :], rope_w[:, 1, :], rope_w[:, 2, :]
            for t in range(T):
                ins = pool.tensor_scalar(rope_w[:, 0, t * HH:(t + 1) * HH], invf[:, :], posT[:, t:t + 1], None, ALU.mult)
            own(ins)
            own(pool.tensor_scalar(turns, ang, 1.0 / TWO_PI, None, ALU.mult))
            own(pool.tensor_scalar(turns, turns, MAGIC, None, ALU.add))
            own(pool.tensor_scalar(turns, turns, -MAGIC, None, ALU.add))
            for part in two_pi_parts():
                own(pool.tensor_scalar(tmp, turns, part, None, ALU.mult))
                own(pool.tensor_tensor(ang, ang, tmp, ALU.subtract))
            own(pool.tensor_scalar(ang, ang, 3.1415925, -3.1415925, ALU.min, ALU.max))
            pool.tensor_scalar(tmp, ang, 0.5, math.pi / 2, ALU.mult, ALU.add).then_inc(s_rope, 1)
            pool.wait_ge(s_sin, 1)
            sv, cv_ = rope_w[:, 1, :], rope_w[:, 3, :]
            sflat, cflat = (b[:, :, :].rearrange("p t d -> p (t d)") for b in (sinb, cosb))
            own(pool.tensor_tensor(sflat, sv, cv_, ALU.mult))
            pool.tensor_scalar(sflat, sflat, 2.0, None, ALU.mult)
            own(pool.tensor_tensor(cflat, sv, sv, ALU.mult))
            pool.tensor_scalar(cflat, cflat, -2.0, 1.0, ALU.mult, ALU.add).then_inc(s_ropeT, 1)

            def inverse_std(n):
                pool.wait_ge(s_mv, n + 1)
                own(pool.tensor_scalar(vareps[:, n:n + 1], mv[:, n, 1:2], EPS, None, ALU.add))
                pool.tensor_tensor(rstd[:, n:n + 1], vareps[:, n:n + 1], half[:, :], ALU.pow).then_inc(s_rs, 1)

            for n in range(2 * T):
                inverse_std(n)

            def rows_of_tokens(l):
                if l == 0:
                    pool.wait_ge(s_tokinit, 16)
                pool.wait_ge(s_rowi, l + 1)
                for t in range(T):
                    for j in range(2):
                        pool.indirect_dma_start(out=tok_dram[:, :],
                                                out_offset=bass.IndirectOffsetOnAxis(ap=rowi[:, j, t:t + 1], axis=0),
                                                in_=tokid[:, t:t + 1], in_offset=None).then_inc(s_scat, 16)
                pool.wait_ge(s_scat, 16 * 2 * T * (l + 1))
                pool.dma_start(tok_r[:, :], tok_dram.rearrange("(p n) a -> p (n a)", p=TBLK)).then_inc(s_tokr, 16)
                pool.wait_ge(s_tokT, l + 1)

            def gather_x(where, idx_col, signal):
                pool.indirect_dma_start(out=where[0:CAP, :], out_offset=None, in_=x_dram[:, :],
                                        in_offset=bass.IndirectOffsetOnAxis(ap=idx[:, idx_col:idx_col + 1], axis=0)
                                        ).then_inc(signal, 16)

            def experts(l):
                M0 = E * l

                def gather(e, b, later):
                    if later or l > 0:
                        pool.wait_ge(s_xt, e + (M0 - 1))
                    pool.tensor_copy(idx[:, b:b + 1], tokT[:, bass.ds(e, 1)]).then_inc(s_idx, 1)
                    count = in_register(pool, r_pool, e + (M0 + 1))
                    pool.wait_ge(s_xst, 16 * T * (l + 1))
                    pool.wait_ge(s_idx, count)
                    gather_x(xg[b], b, s_xg[b])

                def extras(e):
                    n = pool.value_load(extra[0:1, l, bass.ds(e, 1)], min_val=0, max_val=NBLK - 1)
                    with pool.If(n > 0):
                        with pool.Fori(0, n):
                            now = pool.snap(g, min_val=1, max_val=4096)
                            column = pool.snap(nth, min_val=0, max_val=E - 2) + E
                            pool.wait_ge(s_oxt, now)
                            pool.tensor_copy(idx[:, 2:3], tokT[:, bass.ds(column, 1)]).then_inc(s_oidx, 1)
                            pool.wait_ge(s_xst, 16 * T * (l + 1))
                            pool.wait_ge(s_oidx, now)
                            gather_x(xg[2], 2, s_oxg)
                            pool.reg_add(g, g, 1)
                            pool.reg_add(nth, nth, 1)

                pool.wait_ge(s_extra, l + 1)
                pool.reg_mov(nth, 0)
                gather(0, 0, False)
                gather(1, 1, False)
                extras(0)
                with pool.Fori(0, (E - 2) // 2) as i:
                    gather(2 * i + 2, 0, True)
                    extras(2 * i + 1)
                    gather(2 * i + 3, 1, True)
                    extras(2 * i + 2)
                extras(E - 1)

            def combine(l, n):
                stored = in_register(pool, r_pool, pool.snap(g, min_val=1, max_val=4096) * 32)
                for b in range(2):
                    pool.wait_ge(s_y[b], 32 * 8 * (l + 1))
                pool.wait_ge(s_oy, stored)

                def gather_y(t):
                    if T * l + t >= 2:
                        pool.wait_ge(s_cmb, T * l + t - 1)
                    for j in range(2):
                        pool.indirect_dma_start(out=yg[t % 2][j], out_offset=None, in_=y_dram[:, :],
                                                in_offset=bass.IndirectOffsetOnAxis(ap=rowi[:, j, t:t + 1], axis=0)
                                                ).then_inc(s_yg[t % 2], 16)

                gather_y(0)
                gather_y(1)
                for t in range(T):
                    if t + 2 < T:
                        gather_y(t + 2)
                    inverse_std(n + t)

            rows_of_tokens(0)
            experts(0)
            combine(0, 2 * T)
            pool.wait_ge(s_rows1, 16 * 5)
            for t in range(T):
                pool.wait_ge(s_X, t + 1)
                own(pool.tensor_scalar(x_sb[:, t, :], x_sb[:, t, :], ALPHA, None, ALU.mult))
                pool.tensor_tensor(x_sb[:, t, :], x_sb[:, t, :], resrow, ALU.add).then_inc(s_xb, 1)
                inverse_std(3 * T + t)
            rows_of_tokens(1)
            experts(1)
            combine(1, 4 * T)


_INS = ['x', 'positions', 'conv_w1', 'conv_b1', 'conv_dw', 'conv_dwb', 'conv_ln_g', 'conv_ln_b',
        'conv_w2', 'conv_b2', 'kv_w', 'kv_b', 'attn_wq', 'attn_bq', 'attn_sinks', 'attn_wo', 'attn_bo',
        'router_w', 'router_b', 'moe_w_gate', 'moe_w_up', 'moe_w_down', 'ln_g', 'ln_b']
_OUTS = [((1, 512, 1024), 'float32')]


def kernel(**inputs):
    import numpy as _np
    import concourse.bacc as _bacc
    from concourse import mybir as _mybir
    from concourse.bass_utils import run_bass_kernel_spmd as _run

    nc = _bacc.Bacc("TRN2", target_bir_lowering=False, num_devices=1)
    arrays, args = {}, []
    for name in _INS:
        a = _np.ascontiguousarray(inputs[name])
        arrays[f"in_{name}_dram"] = a
        args.append(nc.dram_tensor(f"in_{name}_dram", a.shape, _mybir.dt.from_np(a.dtype), kind="ExternalInput").ap())
    for i, (shape, dtype) in enumerate(_OUTS):
        dt = _mybir.dt.from_np(_np.dtype(dtype))
        args.append(nc.dram_tensor(f"out_{i}_dram", shape, dt, kind="ExternalOutput").ap())
    trunk(nc, *args)
    r = _run(nc, [arrays], core_ids=[0])
    got = tuple(r.results[0][f"out_{i}_dram"] for i in range(len(_OUTS)))
    return got[0]
```

```python
import math
from contextlib import ExitStack

import concourse.bass as bass
from concourse import mybir

F32 = mybir.dt.float32
BF16 = mybir.dt.bfloat16
I32 = mybir.dt.int32
U32 = mybir.dt.uint32
ALU = mybir.AluOpType
ACT = mybir.ActivationFunctionType
AX = mybir.AxisListType

P = 128
D = 1024
S = 512
T = S // P
KD = D // P
CW = 31
HD = 64
HH = HD // 2
NQ = D // HD
NKV = 4
GQ = NQ // NKV
KVD = NKV * HD
E = 16
NG = 4
EPG = E // NG
F = D // 2
DEPTH = 2
CAP = 64
NBLK = S // CAP
TBLK = 2 * E
assert 2 * S // CAP <= E
DVE_TILES = 6
ALPHA = (2.0 * DEPTH) ** 0.25
EPS = 1e-5
NEG = -1e30
THETA = 10000.0
NLN = 5 * T

PB1, PDWB, PGAM, PBET, NPRM = 0, 16, 24, 32, 40

TWO_PI = 2.0 * math.pi


def two_pi_parts():
    parts, rest = [], TWO_PI
    for bits in (6, 15, 24):
        part = math.floor(rest * 2.0 ** bits) / 2.0 ** bits
        parts.append(part)
        rest -= part
    return parts + [rest]


MAGIC = 1.5 * 2 ** 23


def trunk(nc, x_in, positions, conv_w1, conv_b1, conv_dw, conv_dwb, conv_ln_g, conv_ln_b,
          conv_w2, conv_b2, kv_w, kv_b, attn_wq, attn_bq, attn_sinks, attn_wo, attn_bo,
          router_w, router_b, moe_w_gate, moe_w_up, moe_w_down, ln_g, ln_b, out):
    x_rows = x_in.rearrange("a (t p) d -> p (a t) d", p=P)
    out_rows = out.rearrange("a (t p) d -> p (a t) d", p=P)

    x_dram = nc.dram_tensor("x_dram", [S, D], F32).ap()
    tok_dram = nc.dram_tensor("tok_dram", [TBLK * CAP, 1], U32).ap()
    y_dram = nc.dram_tensor("y_dram", [TBLK * CAP, D], F32).ap()
    xd_rows = x_dram.rearrange("(t p) d -> p t d", p=P)

    with ExitStack() as ctx:
        def sb(name, shape, dt=F32):
            return ctx.enter_context(nc.sbuf_tensor(name, shape, dt))

        def sem(name):
            return ctx.enter_context(nc.semaphore(name))

        wring = sb("wring", [P, 6, KD * F])
        x_sb = sb("x_sb", [P, T, D])
        arena = sb("arena", [P, 14592])
        rows = sb("rows", [P, 2 * D + KVD * 2])
        lnrow = sb("lnrow", [P, 2, 2, D])
        prm = sb("prm", [NPRM, P])
        prmT = sb("prmT", [P, NPRM])
        dwT = sb("dwT", [P, KD, 32])
        rw = sb("rw", [P, KD, E])
        ident = sb("ident", [P, P])
        upper = sb("upper", [P, P], BF16)
        ones = sb("ones", [P, P], BF16)
        mask = sb("mask", [P, 2 * P])
        rbrow = sb("rbrow", [P, E])
        sinkb = sb("sinkb", [P, NQ])
        pos_i = sb("pos_i", [T, P], I32)
        pos_f = sb("pos_f", [T, P])
        posT = sb("posT", [P, T])
        invf = sb("invf", [P, HH])
        cosb = sb("cosb", [P, T, HH])
        sinb = sb("sinb", [P, T, HH])
        tokid = sb("tokid", [P, T], U32)
        ramp4 = sb("ramp4", [P, NG])
        ramp16 = sb("ramp16", [P, E])
        ebase = sb("ebase", [P, E])
        thr = sb("thr", [P, NBLK - 1])
        zidx = sb("zidx", [P, TBLK * CAP // P], U32)
        half = sb("half", [P, 1])
        mv = sb("mv", [P, NLN, 2])
        vareps = sb("vareps", [P, NLN])
        rstd = sb("rstd", [P, NLN])
        bns = sb("bns", [P, 2, 6])
        lgs = sb("lgs", [P, T, E])
        aff = sb("aff", [P, T, E])
        gsm = sb("gsm", [P, 4, T])
        onehot = [sb(f"onehot{j}", [P, T, E]) for j in range(2)]
        gatev = sb("gatev", [P, 2, T])
        gsum = sb("gsum", [P, T])
        gate_w = sb("gate_w", [P, 2, T])
        mask_b = sb("mask_b", [P, T, E], BF16)
        rowf = sb("rowf", [P, 2, T])
        rowi = sb("rowi", [P, 2, T], U32)
        cntf = sb("cntf", [P, 4, E])
        before = sb("before", [P, E, E])
        extra = sb("extra", [1, DEPTH, E], I32)
        tok_r = sb("tok_r", [TBLK, CAP], U32)
        tok_f = sb("tok_f", [TBLK, CAP])
        tokT = sb("tokT", [CAP, TBLK], U32)
        idx = sb("idx", [CAP, 3], U32)
        exs = sb("exs", [P, 2, NQ])
        negm = sb("negm", [P, NQ])
        mxs = sb("mxs", [P, NQ])
        den = sb("den", [P, NQ])
        rden = sb("rden", [P, NQ])

        resrow, bqrow = (rows[:, i * D:(i + 1) * D] for i in range(2))
        rope_w = bqrow[:, 0:4 * T * HH].rearrange("p (a n) -> p a n", a=4)
        kvrow = rows[:, 2 * D:2 * D + 2 * KVD]

        def view(at, *shape):
            n = math.prod(shape)
            v = arena[:, at:at + n]
            if len(shape) == 2:
                v = v.rearrange("p (a b) -> p a b", a=shape[0])
            if len(shape) == 3:
                v = v.rearrange("p (a b c) -> p a b c", a=shape[0], b=shape[1])
            return v

        PADW = S + CW - 1
        xT = view(0, KD, S)
        hpad = view(4096, KD, PADW)
        cv = view(4096 + KD * PADW, KD, S)
        hc = [view(0 + i * D, KD, P) for i in range(2)]
        ntok = [view(2048 + i * D, D) for i in range(2)]
        odd = view(13568, S)
        AT = 4096 + KD * PADW + KD * S
        sgm = [view(AT + i * S, S) for i in range(2)]
        xTt = view(13568, KD, P)
        dw_r = view(AT, D)[0:CW, :]
        q_sb = view(0, D // 2)
        k_sb = view(512, KVD)
        tk = [view(768 + i * P, P) for i in range(2)]
        qr = view(1024, NQ, HD)
        kr = view(2048, NKV, 2, HD)
        tq = [view(2560 + i * 256, 256) for i in range(2)]
        kT = view(3072, NKV, S)
        v_sb = view(5120, T, KVD)
        qT = [view(6144 + i * D, KD, P) for i in range(2)]
        pr = [view(8192 + i * D, GQ, 2 * P) for i in range(2)]
        PT = view(10240, KD, P)
        oT = [view(11264 + i * D, KD, P) for i in range(2)]
        xg = [view(i * D, D) for i in range(3)]
        xgT = [view(3072 + i * S, KD, CAP) for i in range(3)]
        sg = [view(4608 + i * 256, 256) for i in range(3)]
        hh = [view(5376 + i * 256, 256) for i in range(3)]
        hT = [view(6144 + i * 256, 2, P) for i in range(3)]
        ysb = [view(6912 + i * S, S) for i in range(3)]
        yg = [[view(8448 + (2 * i + j) * D, D) for j in range(2)] for i in range(2)]

        selv, seln, r1, r2 = (view(8448 + i * T * E, T, E) for i in range(4))
        gs = view(8448 + 4 * T * E, 5, T * NG)
        cmp7 = view(8448 + 6 * T * E, E, NBLK - 1)
        extras_before = view(8448 + 8 * T * E, E, E)

        ps = ctx.enter_context(nc.psum_tensor("ps", [P, 8, 512], F32))

        s_x = [sem(f"s_x{t}") for t in range(T)]
        s_small = sem("s_small")
        s_rows = sem("s_rows")
        s_rows1 = sem("s_rows1")
        s_rows2 = sem("s_rows2")
        s_pool0 = sem("s_pool0")
        s_pc = sem("s_pc")
        s_ac = sem("s_ac")
        s_dc = sem("s_dc")
        s_tokinit = sem("s_tokinit")
        s_yinit = sem("s_yinit")
        s_prT = sem("s_prT")
        s_prC = sem("s_prC")
        s_x0T = sem("s_x0T")
        s_xTd = sem("s_xTd")
        s_xTa = sem("s_xTa")
        s_w1 = [sem(f"s_w1_{i}") for i in range(4)]
        s_w2 = [sem(f"s_w2_{i}") for i in range(2)]
        s_g1 = sem("s_g1")
        s_sgm = sem("s_sgm")
        s_glu = sem("s_glu")
        s_tap = sem("s_tap")
        s_diag = sem("s_diag")
        s_pec = sem("s_pec")
        s_pecv = sem("s_pecv")
        s_xa = sem("s_xa")
        s_At = sem("s_At")
        s_mv = sem("s_mv")
        s_rs = sem("s_rs")
        s_nt = sem("s_nt")
        s_Bt = sem("s_Bt")
        s_hc = sem("s_hc")
        s_C = sem("s_C")
        s_cadd = sem("s_cadd")
        s_ln = sem("s_ln")
        s_xst = sem("s_xst")
        s_Dt = sem("s_Dt")
        s_xTt = sem("s_xTt")
        s_lg = sem("s_lg")
        s_lgc = sem("s_lgc")
        s_aff = sem("s_aff")
        s_mask = sem("s_mask")
        s_rank = sem("s_rank")
        s_rowi = sem("s_rowi")
        s_extra = sem("s_extra")
        s_scat = sem("s_scat")
        s_tokr = sem("s_tokr")
        s_tokf = sem("s_tokf")
        s_tokt = sem("s_tokt")
        s_tokT = sem("s_tokT")
        s_wg = [sem(f"s_wg{i}") for i in range(2)]
        s_wu = [sem(f"s_wu{i}") for i in range(2)]
        s_wd = [sem(f"s_wd{i}") for i in range(2)]
        s_idx = sem("s_idx")
        s_xg = [sem(f"s_xg{i}") for i in range(2)]
        s_xt = sem("s_xt")
        s_xgT = sem("s_xgT")
        s_gate = sem("s_gate")
        s_gud = sem("s_gud")
        s_sg = sem("s_sg")
        s_up = sem("s_up")
        s_h = sem("s_h")
        s_ht = sem("s_ht")
        s_hTc = sem("s_hTc")
        s_dn = sem("s_dn")
        s_yc = sem("s_yc")
        s_y = [sem(f"s_y{i}") for i in range(2)]
        s_oidx = sem("s_oidx")
        s_oxg = sem("s_oxg")
        s_oxt = sem("s_oxt")
        s_oxgT = sem("s_oxgT")
        s_ogate = sem("s_ogate")
        s_osg = sem("s_osg")
        s_oup = sem("s_oup")
        s_oh = sem("s_oh")
        s_oht = sem("s_oht")
        s_ohTc = sem("s_ohTc")
        s_od = sem("s_od")
        s_oyc = sem("s_oyc")
        s_oy = sem("s_oy")
        s_yg = [sem(f"s_yg{i}") for i in range(2)]
        s_cmb = sem("s_cmb")
        s_rope = sem("s_rope")
        s_sin = sem("s_sin")
        s_ropeT = sem("s_ropeT")
        s_wkv = sem("s_wkv")
        s_wq = [sem(f"s_wq{i}") for i in range(2)]
        s_wo = [sem(f"s_wo{i}") for i in range(2)]
        bank_full = [sem(f"bank_full{i}") for i in range(3)]
        bank_read = [sem(f"bank_read{i}") for i in range(3)]
        s_kb = sem("s_kb")
        s_qb = sem("s_qb")
        s_kr = sem("s_kr")
        s_qr = sem("s_qr")
        s_S = sem("s_S")
        s_ss = sem("s_ss")
        s_negm = sem("s_negm")
        s_ex = sem("s_ex")
        s_pn = sem("s_pn")
        s_PTt = sem("s_PTt")
        s_PT = sem("s_PT")
        s_O = sem("s_O")
        s_oT = sem("s_oT")
        s_wadd = sem("s_wadd")
        s_xb = sem("s_xb")
        s_out = sem("s_out")

        block = ctx.enter_context(nc.Block())

        w1_src = conv_w1[0].rearrange("(p k) (h n) -> p k h n", k=KD, h=2)
        w2_src = conv_w2[0].rearrange("(j p) n -> p j n", p=P)
        kv_src = kv_w.rearrange("(p k) n -> p k n", k=KD)
        wq_src = attn_wq[0].rearrange("(p k) n -> p k n", k=KD)
        wo_src = attn_wo[0].rearrange("(k p) n -> p k n", p=P)
        gate_src = moe_w_gate.rearrange("l e (p k) f -> p (l e) (k f)", k=KD)
        up_src = moe_w_up.rearrange("l e (p k) f -> p (l e) (k f)", k=KD)
        down_src = moe_w_down.rearrange("l e (j p) n -> p (l e) j n", p=P)

        def fillers(t):
            plan = [("Xa Xb", "KV"), ("Q0", "W0"), ("Q1", "KT W1"), ("QTa Da Db", "QTb E")]
            return [tuple([(u, t + 1 if u[0] in "XKQ" else t - 1) for u in part.split()
                           if (t + 1 < T if u[0] in "XKQ" else t >= 1)] for part in pair) for pair in plan]

        first_units = [(u, 0) for u in "Xa Xb KV Q0 Q1 KT QTa QTb".split()]
        last_units = [(u, T - 1) for u in "W0 W1 Da Db E".split()]
        order = first_units + [u for t in range(T) for pair in fillers(t) for part in pair for u in part] + last_units
        place = {u: (5 + i % 3, i // 3 + 1) for i, u in enumerate(order)}

        def free(pe, u):
            bank, n = place[u]
            if n > 1:
                pe.wait_ge(bank_read[bank - 5], n - 1)

        def full(eng, u):
            bank, n = place[u]
            eng.wait_ge(bank_full[bank - 5], n)
            return bank

        def taken(eng, u):
            bank, n = place[u]
            eng.wait_ge(bank_read[bank - 5], n)

        glu_order = [0, 1, 2, 3, 4, 6, 5, 7]

        def glu_count(c):
            return glu_order.index(c) + 1

        def diag(c):
            return wring[:, 2 + c - DVE_TILES, 0:CW * P].rearrange("p (k n) -> p k n", k=CW)

        def slot(i, *dims):
            v = wring[:, i, :]
            if len(dims) == 1:
                return v.rearrange("p (k n) -> p k n", k=dims[0])
            return v.rearrange("p (k h n) -> p k h n", k=dims[0], h=dims[1])

        def in_register(eng, reg, value):
            if isinstance(value, int):
                return value
            eng.reg_mov(reg, value)
            return eng.snap(reg, min_val=0, max_val=1 << 16)

        @block.sync
        def _(sp):
            for t in range(T):
                sp.dma_start(x_sb[:, t, :], x_rows[:, t, :]).then_inc(s_x[t], 16)
            for i in range(4):
                for h in range(2):
                    sp.dma_start(slot(i, KD, 2)[:, :, h, :],
                                 w1_src[:, :, h, 256 * i:256 * i + 256]).then_inc(s_w1[i], 16)
            for i in range(2):
                sp.dma_start(slot(4 + i, 4), w2_src[:, 4 * i:4 * i + 4, :]).then_inc(s_w2[i], 16)

            def gate(l, e, b):
                sp.dma_start(wring[:, 3 * b, :], gate_src[:, bass.ds(E * l + e, 1), :]).then_inc(s_wg[b], 16)

            def up(l, e, b):
                sp.dma_start(wring[:, 3 * b + 1, :], up_src[:, bass.ds(E * l + e, 1), :]).then_inc(s_wu[b], 16)

            def down(l, e, b):
                sp.dma_start(slot(3 * b + 2, 4), down_src[:, bass.ds(E * l + e, 1), :, :]).then_inc(s_wd[b], 16)

            def experts_from_2(l):
                with sp.Fori(0, (E - 2) // 2) as i:
                    for b in range(2):
                        e = 2 * i + 2 + b
                        sp.wait_ge(s_gud, e + (E * l - 1))
                        gate(l, e, b)
                        up(l, e, b)
                        sp.wait_ge(s_dn, e + (E * l - 1))
                        down(l, e, b)

            sp.wait_ge(s_g1, 2)
            gate(0, 0, 0)
            sp.wait_ge(s_g1, 4)
            up(0, 0, 0)
            sp.wait_ge(s_pec, 1)
            down(0, 0, 0)
            sp.wait_ge(s_pec, 2)
            gate(0, 1, 1)
            sp.wait_ge(s_C, T)
            up(0, 1, 1)
            down(0, 1, 1)
            experts_from_2(0)
            sp.wait_ge(s_gud, E - 1)
            sp.dma_start(slot(0, KD), kv_src).then_inc(s_wkv, 16)
            sp.dma_start(slot(1, KD), wq_src[:, :, 0:512]).then_inc(s_wq[0], 16)
            sp.wait_ge(s_dn, E - 1)
            sp.dma_start(slot(2, KD), wq_src[:, :, 512:1024]).then_inc(s_wq[1], 16)
            sp.wait_ge(s_gud, E)
            sp.dma_start(slot(3, KD), wo_src[:, :, 0:512]).then_inc(s_wo[0], 16)
            sp.dma_start(slot(4, KD), wo_src[:, :, 512:1024]).then_inc(s_wo[1], 16)
            sp.wait_ge(s_dn, E)
            down(1, 1, 1)
            full(sp, ("KV", T - 1))
            gate(1, 0, 0)
            full(sp, ("Q1", T - 1))
            up(1, 0, 0)
            down(1, 0, 0)
            full(sp, ("W1", T - 1))
            gate(1, 1, 1)
            up(1, 1, 1)
            experts_from_2(1)

        @block.tensor
        def _(pe):
            g = ctx.enter_context(pe.register("pe_extra"))
            r_pe = [ctx.enter_context(pe.register(f"pe_r{i}")) for i in range(2)]
            pe.reg_mov(g, 1)

            def transposes(bank, src, signal, count=KD, step=KD):
                for j in range(count):
                    last = pe.transpose(ps[:, bank + j // 4, (j % 4) * P:(j % 4) * P + P],
                                        src(j), ident[:, :])
                last.then_inc(signal, 1)

            pe.wait_ge(s_pool0, 1)
            pe.wait_ge(s_small, 16 * 6)
            pe.transpose(ps[:, 5, 0:NPRM], prm[:, :], ident[0:NPRM, 0:NPRM])
            for c in range(KD):
                pe.transpose(ps[:, 4, 32 * c:32 * c + CW], dw_r[:, c * P:(c + 1) * P], ident[0:CW, 0:CW])
            pe.wait_ge(s_rope, 1)
            pe.transpose(ps[:, 5, 64:64 + T], pos_f[:, :], ident[0:T, 0:T]).then_inc(s_prT, 1)
            for t in range(T):
                pe.wait_ge(s_x[t], 16)
                if t >= 2:
                    pe.wait_ge(s_xTd, t - 1)
                    pe.wait_ge(s_xTa, t - 1)
                transposes(2 * (t % 2), lambda j: x_sb[:, t, j::KD], s_x0T)
            pe.wait_ge(s_xTd, T)
            pe.wait_ge(s_xTa, T)
            for c in range(KD):
                pe.wait_ge(s_w1[c // 2], 32)
                if c == 2:
                    pe.wait_ge(s_prC, 1)
                if c >= 4:
                    pe.wait_ge(s_glu, c - 3)
                w = slot(c // 2, KD, 2)
                for h in range(2):
                    for k in range(KD):
                        last = pe.matmul(ps[:, 2 * (c % 4) + h, :],
                                         w[:, k, h, (c % 2) * P:(c % 2) * P + P], xT[:, k, :],
                                         start=(k == 0), stop=(k == KD - 1))
                last.then_inc(s_g1, 1)

            for c in range(DVE_TILES, KD):
                pe.wait_ge(s_glu, glu_count(c))
                pe.wait_ge(s_diag, c - DVE_TILES + 1)
                for k in range(CW):
                    last = pe.matmul(ps[:, 2 * (c % 4) - 4, :], diag(c)[:, k, :], hpad[:, c, k:k + S],
                                     start=(k == 0), stop=(k == CW - 1))
                last.then_inc(s_pec, 1)

            def stage_a(t):
                if t >= 1:
                    pe.wait_ge(s_nt, t)
                transposes(0, lambda c: cv[:, c, t * P:(t + 1) * P], s_At)

            def stage_b(t):
                pe.wait_ge(s_nt, t + 1)
                if t >= 1:
                    pe.wait_ge(s_hc, t)
                transposes(2, lambda c: ntok[t % 2][:, c * P:(c + 1) * P], s_Bt)

            def stage_c(t):
                pe.wait_ge(s_hc, t + 1)
                if t == 0:
                    pe.wait_ge(s_w2[0], 16)
                    pe.wait_ge(s_w2[1], 16)
                if t >= 1:
                    pe.wait_ge(s_cadd, t)
                for h in range(2):
                    for c in range(KD):
                        last = pe.matmul(ps[:, 4 + h, :], hc[t % 2][:, c, :],
                                         slot(4 + c // 4, 4)[:, c % 4, h * 512:(h + 1) * 512],
                                         start=(c == 0), stop=(c == KD - 1))
                last.then_inc(s_C, 1)

            def stage_d(t):
                n = t
                pe.wait_ge(s_ln, t + 1)
                if n >= 1:
                    pe.wait_ge(s_lgc, n)
                transposes(6, lambda j: x_sb[:, t, j::KD], s_Dt)
                pe.wait_ge(s_xTt, n + 1)
                for k in range(KD):
                    last = pe.matmul(ps[:, 6, 0:E], xTt[:, k, :], rw[:, k, :], start=(k == 0), stop=(k == KD - 1))
                last.then_inc(s_lg, 1)

            pe.wait_ge(s_pecv, KD - DVE_TILES)
            pe.wait_ge(s_tap, (CW + 1) * DVE_TILES)
            stage_a(0)
            stage_b(0)
            stage_a(1)
            for t in range(T):
                stage_c(t)
                if t + 1 < T:
                    stage_b(t + 1)
                if t + 2 < T:
                    stage_a(t + 2)
                if t >= 1:
                    stage_d(t - 1)
            stage_d(T - 1)

            def ranks(l):
                pe.wait_ge(s_mask, l + 1)
                for t in range(T):
                    for u in range(t + 1):
                        pe.matmul(ps[:, 0, t * E:(t + 1) * E], (upper if u == t else ones)[:, :], mask_b[:, u, :],
                                  start=(u == 0), stop=(u == t))
                for u in range(T):
                    last = pe.matmul(ps[:, 0, T * E:(T + 1) * E], ones[:, :], mask_b[:, u, :],
                                     start=(u == 0), stop=(u == T - 1))
                last.then_inc(s_rank, 1)
                pe.wait_ge(s_tokf, l + 1)
                pe.transpose(ps[0:CAP, 1, 0:TBLK], tok_f[:, :], ident[0:TBLK, 0:TBLK]).then_inc(s_tokt, 1)

            def gathered_T(src, signal):
                for j in range(KD):
                    last = pe.transpose(ps[:, 0, j * CAP:(j + 1) * CAP], src[0:CAP, j::KD], ident[0:CAP, 0:CAP])
                last.then_inc(signal, 1)

            def half_products(bank, act, w, signal, first=None):
                for k in range(KD):
                    for h in range(2):
                        mm = pe.matmul(ps[h * CAP:(h + 1) * CAP, bank, 0:256], act[:, k, :],
                                       w[:, k, h * 256:(h + 1) * 256], start=(k == 0), stop=(k == KD - 1))
                        if first is not None and k == 0 and h == 0:
                            mm.then_inc(first, 1)
                mm.then_inc(signal, 1)

            def down_products(bank, act, w, signal):
                for j in range(4):
                    for h in range(2):
                        mm = pe.matmul(ps[h * CAP:(h + 1) * CAP, bank, :],
                                       act[:, j % 2, (j // 2) * CAP:(j // 2 + 1) * CAP],
                                       w[:, j, h * 512:(h + 1) * 512], start=(j == 0), stop=(j == 3))
                mm.then_inc(signal, 1)

            def experts(l):
                M0 = E * l
                W0 = 8 * l

                def stage_t(e, eh, b):
                    gathered = in_register(pe, r_pe[0], 16 * (eh + (W0 + 1)))
                    copied = in_register(pe, r_pe[1], e + M0)
                    pe.wait_ge(s_pool0, 1)
                    pe.wait_ge(s_xg[b], gathered)
                    if not (l == 0 and isinstance(e, int) and e == 0):
                        pe.wait_ge(s_xgT, copied)
                    gathered_T(xg[b], s_xt)

                def stage_g(e, eh, b, first):
                    pe.wait_ge(s_wg[b], 16 * (eh + (W0 + 1)))
                    pe.wait_ge(s_xgT, e + (M0 + 1))
                    if first or l > 0:
                        pe.wait_ge(s_sg, e + M0)
                    half_products(1, xgT[b], slot(3 * b, KD), s_gate, s_gud if first else None)

                def stage_u(e, eh, b, later):
                    pe.wait_ge(s_wu[b], 16 * (eh + (W0 + 1)))
                    if later or l > 0:
                        pe.wait_ge(s_h, e + M0)
                    half_products(2, xgT[b], slot(3 * b + 1, KD), s_up)

                def stage_h(e, b, later=True, last=False):
                    pe.wait_ge(s_h, e + (M0 + 1))
                    if later or l > 0:
                        pe.wait_ge(s_hTc, e + M0)
                    for c in range(2):
                        tr = pe.transpose(ps[:, 3, c * P:(c + 1) * P], hh[b][:, c * P:(c + 1) * P], ident[:, :])
                        if last and c == 0:
                            tr.then_inc(s_gud, 1)
                    tr.then_inc(s_ht, 1)

                def stage_y(e, eh, b, later=True):
                    pe.wait_ge(s_wd[b], 16 * (eh + (W0 + 1)))
                    pe.wait_ge(s_hTc, e + (M0 + 1))
                    if later or l > 0:
                        pe.wait_ge(s_yc, e + M0)
                    down_products(4, hT[b], slot(3 * b + 2, 4), s_dn)

                def extras(e, b, ahead):
                    n = pe.value_load(extra[0:1, l, bass.ds(e, 1)], min_val=0, max_val=NBLK - 1)
                    with pe.If(n > 0):
                        with pe.Fori(0, n):
                            now = pe.snap(g, min_val=1, max_val=4096)
                            gathered = in_register(pe, r_pe[0], now * 16)
                            copied = in_register(pe, r_pe[1], e + (M0 + ahead))
                            pe.wait_ge(s_pool0, 1)
                            pe.wait_ge(s_oxg, gathered)
                            pe.wait_ge(s_xgT, copied)
                            gathered_T(xg[2], s_oxt)
                            pe.wait_ge(s_oxgT, now)
                            half_products(5, xgT[2], slot(3 * b, KD), s_ogate)
                            half_products(6, xgT[2], slot(3 * b + 1, KD), s_oup)
                            pe.wait_ge(s_oh, now)
                            for c in range(2):
                                tr = pe.transpose(ps[:, 3, c * P:(c + 1) * P], hh[2][:, c * P:(c + 1) * P],
                                                  ident[:, :])
                            tr.then_inc(s_oht, 1)
                            pe.wait_ge(s_ohTc, now)
                            pe.wait_ge(s_wd[b], 16 * (e_half(e, b) + (W0 + 1)))
                            pe.wait_ge(s_oyc, now)
                            down_products(7, hT[2], slot(3 * b + 2, 4), s_od)
                            pe.reg_add(g, g, 1)

                def e_half(e, b):
                    return halves[b]

                pe.wait_ge(s_extra, l + 1)
                halves = [0, 0]
                stage_t(0, 0, 0)
                stage_g(0, 0, 0, False)
                stage_u(0, 0, 0, False)
                stage_t(1, 0, 1)
                extras(0, 0, 2)

                def step(e, eh, b, first_h=False, last=False):
                    halves[b] = eh
                    stage_g(e, eh, b, True)
                    stage_h(e - 1, 1 - b, later=not first_h)
                    stage_u(e, eh, b, True)
                    if not last:
                        stage_t(e + 1, eh + b, 1 - b)
                    stage_y(e - 1, eh if b else eh - 1, 1 - b, later=not first_h)
                    extras(e, b, 1 if last else 2)

                step(1, 0, 1, first_h=True)
                with pe.Fori(0, (E - 4) // 2) as i:
                    step(2 * i + 2, i + 1, 0)
                    step(2 * i + 3, i + 1, 1)
                step(E - 2, E // 2 - 1, 0)
                step(E - 1, E // 2 - 1, 1, last=True)
                stage_h(E - 1, 1, last=True)
                stage_y(E - 1, E // 2 - 1, 1)

            ranks(0)
            experts(0)

            def unit(u):
                kind, t = u
                free(pe, u)
                bank = place[u][0]
                if kind in ("Xa", "Da"):
                    pe.wait_ge(s_ln, (T if kind == "Xa" else 2 * T) + t + 1)
                if kind in ("Xa", "Xb", "Da", "Db"):
                    j0 = 0 if kind[1] == "a" else 4
                    for j in range(4):
                        last = pe.transpose(ps[:, bank, j * P:(j + 1) * P], x_sb[:, t, j0 + j::KD], ident[:, :])
                elif kind in ("KV", "Q0", "Q1"):
                    taken(pe, ("Xa", t))
                    taken(pe, ("Xb", t))
                    w = {"KV": s_wkv, "Q0": s_wq[0], "Q1": s_wq[1]}[kind]
                    pe.wait_ge(w, 16)
                    at = {"KV": 0, "Q0": 1, "Q1": 2}[kind]
                    for k in range(KD):
                        last = pe.matmul(ps[:, bank, :], xTt[:, k, :], slot(at, KD)[:, k, :],
                                         start=(k == 0), stop=(k == KD - 1))
                elif kind == "KT":
                    pe.wait_ge(s_kr, t + 1)
                    for j in range(NKV):
                        last = pe.transpose(ps[:, bank, j * P:(j + 1) * P],
                                            kr[:, j, :, :].rearrange("p a b -> p (a b)"), ident[:, :])
                elif kind in ("QTa", "QTb"):
                    h = "ab".index(kind[2])
                    pe.wait_ge(s_qr, 2 * t + h + 1)
                    for j in range(4):
                        i = 8 * h + 2 * j
                        last = pe.transpose(ps[:, bank, j * P:(j + 1) * P],
                                            qr[:, i:i + 2, :].rearrange("p a b -> p (a b)"), ident[:, :])
                elif kind in ("W0", "W1"):
                    h = int(kind[1])
                    pe.wait_ge(s_oT, NKV * (t + 1))
                    pe.wait_ge(s_wo[h], 16)
                    for k in range(KD):
                        last = pe.matmul(ps[:, bank, :], oT[t % 2][:, k, :], slot(3 + h, KD)[:, k, :],
                                         start=(k == 0), stop=(k == KD - 1))
                else:
                    taken(pe, ("Da", t))
                    taken(pe, ("Db", t))
                    for k in range(KD):
                        last = pe.matmul(ps[:, bank, 0:E], xTt[:, k, :], rw[:, k, :],
                                         start=(k == 0), stop=(k == KD - 1))
                last.then_inc(bank_full[bank - 5], 1)

            def scores(t, kh):
                n = NKV * t + kh
                lo = 0 if t else P
                if kh == 0:
                    taken(pe, ("KT", t))
                    taken(pe, ("QTa", t))
                if kh == 2:
                    taken(pe, ("QTb", t))
                if n >= 1:
                    pe.wait_ge(s_ss, n)
                for j in range(2):
                    for r in range(2):
                        part = slice(r * HD, (r + 1) * HD)
                        last = pe.matmul(ps[:, r, j * 256 + lo:j * 256 + 256], qT[t % 2][part, 2 * kh + j, :],
                                         kT[part, kh, (t - 1) * P + lo:(t + 1) * P], start=True, stop=True)
                last.then_inc(s_S, 1)

            def turn(t, kh):
                n = NKV * t + kh
                pe.wait_ge(s_pn, n + 1)
                if n >= 1:
                    pe.wait_ge(s_PT, n)
                for i in range(GQ):
                    for s in range(0 if t else 1, 2):
                        last = pe.transpose(ps[:, 2 + i // 2, ((2 * i + s) % 4) * P:((2 * i + s) % 4 + 1) * P],
                                            pr[n % 2][:, i, s * P:(s + 1) * P], ident[:, :])
                last.then_inc(s_PTt, 1)

            def values(t, kh):
                n = NKV * t + kh
                pe.wait_ge(s_PT, n + 1)
                if n >= 1:
                    pe.wait_ge(s_oT, n)
                s0 = 0 if t else 1
                pt = PT.rearrange("p (r j s) n -> p r j s n", r=2, s=2)
                for s in range(s0, 2):
                    for r in range(2):
                        last = pe.matmul(ps[r * HD:(r + 1) * HD, 4, 0:256], v_sb[:, t - 1 + s, kh * HD:(kh + 1) * HD],
                                         pt[:, r, :, s, :], start=(s == s0), stop=(s == 1))
                last.then_inc(s_O, 1)

            for u in first_units:
                unit(u)
            for t in range(T):
                scores(t, 0)
                for kh, (early, late) in enumerate(fillers(t)):
                    for u in early:
                        unit(u)
                    if kh:
                        values(t, kh - 1)
                    for u in late:
                        unit(u)
                    if kh + 1 < NKV:
                        scores(t, kh + 1)
                    turn(t, kh)
                values(t, NKV - 1)
            for u in last_units:
                unit(u)
            ranks(1)
            experts(1)

        @block.vector
        def _(dve):
            done = [0]
            g = ctx.enter_context(dve.register("dve_extra"))
            dve.reg_mov(g, 1)

            def own(ins):
                done[0] += 1
                ins.then_inc(s_dc, 1)
                dve.wait_ge(s_dc, done[0])

            dve.wait_ge(s_prT, 1)
            dve.tensor_copy(prmT[:, :], ps[:, 5, 0:NPRM])
            dve.tensor_copy(posT[:, :], ps[:, 5, 64:64 + T])
            dve.tensor_copy(dwT[:, :, 0:CW], ps[:, 4, 0:32 * KD].rearrange("p (c k) -> p c k", k=32)[:, :, 0:CW]
                            ).then_inc(s_prC, 1)
            for t in range(T):
                dve.wait_ge(s_x0T, t + 1)
                dve.tensor_copy(xT[:, 0:4, t * P:(t + 1) * P],
                                ps[:, 2 * (t % 2), :].rearrange("p (j n) -> p j n", j=4)).then_inc(s_xTd, 1)
            dve.wait_ge(s_pool0, 2)
            dve.wait_ge(s_prC, 1)

            def glu(c, parity):
                one = bass.ds(c, 1)
                bank = 2 * c if not isinstance(c, int) else 2 * (c % 4)
                dve.wait_ge(s_g1, c + 1)
                dve.wait_ge(s_sgm, c + 1)
                dve.scalar_tensor_tensor(out=hpad[:, one, CW - 1:PADW], in0=ps[:, bass.ds(bank, 1), :],
                                         scalar=prmT[:, bass.ds(c + PB1, 1)], in1=sgm[parity],
                                         op0=ALU.add, op1=ALU.mult).then_inc(s_glu, 1)

            def taps(c, glus):
                one = bass.ds(c, 1)
                even = cv[:, one, :]
                dve.wait_ge(s_glu, glus)
                dve.tensor_scalar(even, hpad[:, one, 0:S], dwT[:, one, 0:1],
                                  prmT[:, bass.ds(c + PDWB, 1)], ALU.mult, ALU.add).then_inc(s_tap, 1)
                dve.tensor_scalar(odd, hpad[:, one, 1:1 + S], dwT[:, one, 1:2], None, ALU.mult).then_inc(s_tap, 1)
                for k in range(2, CW):
                    acc = (even, odd)[k % 2]
                    dve.wait_ge(s_tap, c * (CW + 1) + (k - 1))
                    dve.scalar_tensor_tensor(out=acc, in0=hpad[:, one, k:k + S], scalar=dwT[:, one, k:k + 1],
                                             in1=acc, op0=ALU.mult, op1=ALU.add).then_inc(s_tap, 1)
                dve.wait_ge(s_tap, c * (CW + 1) + CW)
                dve.tensor_tensor(even, even, odd, ALU.add).then_inc(s_tap, 1)

            with dve.Fori(0, 2) as i:
                for b in range(2):
                    glu(2 * i + b, b)
                    taps(2 * i + b, 2 * i + (b + 1))
            glu(4, 0)
            glu(6, 0)
            taps(4, glu_count(4))
            glu(5, 1)
            glu(7, 1)
            taps(5, glu_count(5))

            def moments(src, n, signal):
                for h in range(2):
                    ins = dve.bn_stats(bns[:, h, :], src(h))
                own(ins)
                dve.bn_aggr(mv[:, n, :], bns[:, :, :]).then_inc(signal, 1)

            def norm_conv(t, n):
                dve.wait_ge(s_At, t + 1)
                moments(lambda h: ps[:, h, :], n, s_mv)
                dve.wait_ge(s_rs, n + 1)
                dve.wait_ge(s_mv, n + 1)
                if t >= 2:
                    dve.wait_ge(s_Bt, t - 1)
                dve.tensor_scalar(ntok[t % 2], ps[:, 0:2, :].rearrange("p a b -> p (a b)"), mv[:, n, 0:1],
                                  rstd[:, n:n + 1], ALU.subtract, ALU.mult).then_inc(s_nt, 1)

            def norm_x(t, n, l, which):
                xt = x_sb[:, t, :]
                moments(lambda h: x_sb[:, t, h * 512:(h + 1) * 512], n, s_mv)
                dve.wait_ge(s_mv, n + 1)
                own(dve.scalar_tensor_tensor(out=xt, in0=xt, scalar=mv[:, n, 0:1], in1=lnrow[:, which, 0, :],
                                             op0=ALU.subtract, op1=ALU.mult))
                dve.wait_ge(s_rs, n + 1)
                dve.scalar_tensor_tensor(out=xt, in0=xt, scalar=rstd[:, n:n + 1], in1=lnrow[:, which, 1, :],
                                         op0=ALU.mult, op1=ALU.add).then_inc(s_ln, 1)

            def add_product(t, bank, signal, count):
                for h in range(2):
                    ins = dve.tensor_tensor(x_sb[:, t, h * 512:(h + 1) * 512], x_sb[:, t, h * 512:(h + 1) * 512],
                                            ps[:, bank + h, :], ALU.add)
                ins.then_inc(signal, 1)
                dve.wait_ge(signal, count)

            def keep_logits(t):
                dve.wait_ge(s_lg, t + 1)
                dve.tensor_copy(lgs[:, t, :], ps[:, 6, 0:E]).then_inc(s_lgc, 1)

            dve.wait_ge(s_rows, 16 * 8)
            n = 0
            norm_conv(0, n)
            n += 1
            norm_conv(1, n)
            n += 1
            for t in range(T):
                dve.wait_ge(s_C, t + 1)
                dve.wait_ge(s_xa, t + 1)
                add_product(t, 4, s_cadd, t + 1)
                norm_x(t, n, 0, 0)
                n += 1
                if t + 2 < T:
                    norm_conv(t + 2, n)
                    n += 1
                if t >= 1:
                    keep_logits(t - 1)
            keep_logits(T - 1)

            def route(l):
                dve.wait_ge(s_aff, l + 1)
                tg = "p t (g e) -> p (t g) e"
                own(dve.tensor_tensor(selv[:, :, :], aff[:, :, :], rbrow[:, :].unsqueeze(1).to_broadcast([P, T, E]),
                                      ALU.add))
                v = selv[:, :, :].rearrange(tg, g=NG)
                a, b, c, d = (v[:, :, i] for i in range(EPG))
                dve.tensor_tensor(gs[:, 0, :], a, b, ALU.max)
                dve.tensor_tensor(gs[:, 1, :], a, b, ALU.min)
                dve.tensor_tensor(gs[:, 2, :], c, d, ALU.max)
                own(dve.tensor_tensor(gs[:, 3, :], c, d, ALU.min))
                dve.tensor_tensor(gs[:, 4, :], gs[:, 0, :], gs[:, 2, :], ALU.max)
                dve.tensor_tensor(gs[:, 1, :], gs[:, 1, :], gs[:, 3, :], ALU.max)
                own(dve.tensor_tensor(gs[:, 0, :], gs[:, 0, :], gs[:, 2, :], ALU.min))
                own(dve.tensor_tensor(gs[:, 1, :], gs[:, 1, :], gs[:, 0, :], ALU.max))
                own(dve.tensor_tensor(gs[:, 4, :], gs[:, 4, :], gs[:, 1, :], ALU.add))

                def first_of_max(score, width, ramp, out, tmp):
                    shape = [P, T, width]
                    rampb = ramp[:, :].unsqueeze(1).to_broadcast(shape)
                    own(dve.tensor_reduce(gsm[:, 0, :], score, AX.X, ALU.max))
                    own(dve.tensor_tensor(tmp, score, gsm[:, 0, :].unsqueeze(2).to_broadcast(shape), ALU.is_equal))
                    own(dve.tensor_tensor(tmp, tmp, rampb, ALU.mult))
                    own(dve.tensor_reduce(gsm[:, 1, :], tmp, AX.X, ALU.min))
                    own(dve.tensor_tensor(out, rampb, gsm[:, 1, :].unsqueeze(2).to_broadcast(shape), ALU.is_equal))

                def tgv(i):
                    return gs[:, i, :].rearrange("p (t g) -> p t g", g=NG)

                first_of_max(tgv(4), NG, ramp4, tgv(0), tgv(1))
                own(dve.tensor_scalar(gs[:, 1, :], gs[:, 0, :], -NEG, NEG, ALU.mult, ALU.add))
                full = [P, T * NG, EPG]
                sv = seln[:, :, :].rearrange(tg, g=NG)
                own(dve.tensor_tensor(sv, v, gs[:, 0, :].unsqueeze(2).to_broadcast(full), ALU.mult))
                own(dve.tensor_tensor(sv, sv, gs[:, 1, :].unsqueeze(2).to_broadcast(full), ALU.add))
                for j in range(2):
                    first_of_max(seln[:, :, :], E, ramp16, onehot[j][:, :, :], r1[:, :, :])
                    own(dve.tensor_tensor(r2[:, :, :], aff[:, :, :], onehot[j][:, :, :], ALU.mult))
                    own(dve.tensor_reduce(gatev[:, j, :], r2[:, :, :], AX.X, ALU.add))
                    if j == 0:
                        own(dve.scalar_tensor_tensor(out=seln[:, :, :], in0=onehot[0][:, :, :], scalar=-3e38,
                                                     in1=seln[:, :, :], op0=ALU.mult, op1=ALU.add))
                dve.tensor_tensor(mask_b[:, :, :], onehot[0][:, :, :], onehot[1][:, :, :], ALU.add).then_inc(s_mask, 1)
                own(dve.tensor_tensor(gsum[:, :], gatev[:, 0, :], gatev[:, 1, :], ALU.add))
                own(dve.reciprocal(gsum[:, :], gsum[:, :]))
                own(dve.tensor_tensor(gate_w[:, :, :], gatev[:, :, :],
                                      gsum[:, :].unsqueeze(1).to_broadcast([P, 2, T]), ALU.mult))
                dve.wait_ge(s_rank, l + 1)
                count, more, first, shift = (cntf[:, i, :] for i in range(4))
                own(dve.tensor_copy(count, ps[:, 0, T * E:(T + 1) * E]))
                shape = [P, E, NBLK - 1]
                own(dve.tensor_tensor(cmp7[:, :, :], count.unsqueeze(2).to_broadcast(shape),
                                      thr[:, :].unsqueeze(1).to_broadcast(shape), ALU.is_gt))
                own(dve.tensor_reduce(more, cmp7[:, :, :], AX.X, ALU.add))
                dve.tensor_copy(extra[:, l, :], more[0:1, :]).then_inc(s_extra, 1)
                own(dve.tensor_tensor(extras_before[:, :, :], before[:, :, :],
                                      more.unsqueeze(1).to_broadcast([P, E, E]), ALU.mult))
                own(dve.tensor_reduce(first, extras_before[:, :, :], AX.X, ALU.add))
                own(dve.scalar_tensor_tensor(out=shift, in0=first, scalar=float(CAP), in1=ebase[:, :],
                                             op0=ALU.mult, op1=ALU.subtract))
                own(dve.tensor_scalar(shift, shift, float(CAP * (E - 1)), None, ALU.add))
                rank = ps[:, 0, 0:T * E].rearrange("p (t e) -> p t e", e=E)
                wide = [P, T, E]
                own(dve.tensor_scalar(r1[:, :, :], rank, float(CAP), None, ALU.is_ge))
                own(dve.tensor_tensor(r1[:, :, :], r1[:, :, :], shift.unsqueeze(1).to_broadcast(wide), ALU.mult))
                own(dve.tensor_tensor(r1[:, :, :], r1[:, :, :], rank, ALU.add))
                own(dve.tensor_tensor(r1[:, :, :], r1[:, :, :], ebase[:, :].unsqueeze(1).to_broadcast(wide), ALU.add))
                for j in range(2):
                    own(dve.tensor_tensor(r2[:, :, :], r1[:, :, :], onehot[j][:, :, :], ALU.mult))
                    own(dve.tensor_reduce(rowf[:, j, :], r2[:, :, :], AX.X, ALU.add))
                dve.tensor_copy(rowi[:, :, :], rowf[:, :, :]).then_inc(s_rowi, 1)
                dve.wait_ge(s_tokr, 16 * (l + 1))
                dve.tensor_copy(tok_f[:, :], tok_r[:, :]).then_inc(s_tokf, 1)
                dve.wait_ge(s_tokt, l + 1)
                dve.tensor_copy(tokT[:, :], ps[0:CAP, 1, 0:TBLK]).then_inc(s_tokT, 1)

            def experts(l):
                M0 = E * l

                def copy_t(e, b, later):
                    dve.wait_ge(s_xt, e + (M0 + 1))
                    if later or l > 0:
                        dve.wait_ge(s_up, e + (M0 - 1))
                    dve.tensor_copy(xgT[b].rearrange("p a b -> p (a b)"), ps[:, 0, :]).then_inc(s_xgT, 1)

                def gated(e, b, later):
                    dve.wait_ge(s_up, e + (M0 + 1))
                    dve.wait_ge(s_sg, e + (M0 + 1))
                    if later or l > 0:
                        dve.wait_ge(s_ht, e + (M0 - 1))
                    dve.tensor_tensor(hh[b], sg[b], ps[:, 2, 0:256], ALU.mult).then_inc(s_h, 1)

                def copy_h(e, b, later):
                    dve.wait_ge(s_ht, e + (M0 + 1))
                    if later or l > 0:
                        dve.wait_ge(s_dn, e + (M0 - 1))
                    dve.tensor_copy(hT[b].rearrange("p a b -> p (a b)"), ps[:, 3, 0:256]).then_inc(s_hTc, 1)

                def extras(e):
                    k = dve.value_load(extra[0:1, l, bass.ds(e, 1)], min_val=0, max_val=NBLK - 1)
                    with dve.If(k > 0):
                        with dve.Fori(0, k):
                            now = dve.snap(g, min_val=1, max_val=4096)
                            dve.wait_ge(s_oxt, now + 1)
                            dve.tensor_copy(xgT[2].rearrange("p a b -> p (a b)"), ps[:, 0, :]).then_inc(s_oxgT, 1)
                            dve.wait_ge(s_oup, now)
                            dve.wait_ge(s_osg, now)
                            dve.tensor_tensor(hh[2], sg[2], ps[:, 6, 0:256], ALU.mult).then_inc(s_oh, 1)
                            dve.wait_ge(s_oht, now)
                            dve.tensor_copy(hT[2].rearrange("p a b -> p (a b)"), ps[:, 3, 0:256]).then_inc(s_ohTc, 1)
                            dve.reg_add(g, g, 1)

                dve.wait_ge(s_extra, l + 1)
                copy_t(0, 0, False)
                gated(0, 0, False)
                copy_t(1, 1, False)
                extras(0)
                copy_h(0, 0, False)
                gated(1, 1, False)
                copy_t(2, 0, True)
                extras(1)

                def step(e, b, last=False):
                    copy_h(e - 1, 1 - b, True)
                    gated(e, b, True)
                    if not last:
                        copy_t(e + 1, 1 - b, True)
                    extras(e)

                with dve.Fori(0, (E - 4) // 2) as i:
                    step(2 * i + 2, 0)
                    step(2 * i + 3, 1)
                step(E - 2, 0)
                step(E - 1, 1, last=True)
                copy_h(E - 1, 1, True)

            def combine(l, n):
                for t in range(T):
                    b = t % 2
                    dve.wait_ge(s_yg[b], 32 * (2 * l + t // 2 + 1))
                    y0, y1 = yg[b]
                    own(dve.tensor_scalar(y0, y0, gate_w[:, 0, t:t + 1], None, ALU.mult))
                    own(dve.scalar_tensor_tensor(out=y0, in0=y1, scalar=gate_w[:, 1, t:t + 1], in1=y0,
                                                 op0=ALU.mult, op1=ALU.add))
                    dve.scalar_tensor_tensor(out=x_sb[:, t, :], in0=x_sb[:, t, :], scalar=ALPHA, in1=y0,
                                             op0=ALU.mult, op1=ALU.add).then_inc(s_cmb, 1)
                    dve.wait_ge(s_cmb, T * l + t + 1)
                    norm_x(t, n + t, l, 1)

            route(0)
            experts(0)
            combine(0, n)
            n += T

            dve.wait_ge(s_ropeT, 1)
            dve.wait_ge(s_rows1, 16 * 5)

            def rotate(t, src, heads, dst, tmp):
                cs = cosb[:, t, :].unsqueeze(1).to_broadcast([P, heads, HH])
                sn = sinb[:, t, :].unsqueeze(1).to_broadcast([P, heads, HH])
                lo, hi = src[:, :, 0:HH], src[:, :, HH:HD]
                ta = tmp[0].rearrange("p (h d) -> p h d", h=heads)
                tb = tmp[1].rearrange("p (h d) -> p h d", h=heads)
                dve.tensor_tensor(ta, lo, cs, ALU.mult)
                own(dve.tensor_tensor(tb, hi, sn, ALU.mult))
                own(dve.tensor_tensor(dst[0], ta, tb, ALU.subtract))
                dve.tensor_tensor(ta, hi, cs, ALU.mult)
                own(dve.tensor_tensor(tb, lo, sn, ALU.mult))
                return dve.tensor_tensor(dst[1], ta, tb, ALU.add)

            def take(u, n):
                kind, t = u
                if kind[0] in "XD" or kind in ("KT", "QTa", "QTb"):
                    return
                bank = full(dve, u)
                if kind == "KV":
                    if t >= 1:
                        full(dve, ("KT", t - 1))
                    dve.tensor_tensor(v_sb[:, t, :], ps[:, bank, KVD:2 * KVD], kvrow[:, KVD:2 * KVD], ALU.add)
                    dve.tensor_tensor(k_sb, ps[:, bank, 0:KVD], kvrow[:, 0:KVD], ALU.add
                                      ).then_inc(bank_read[bank - 5], 1)
                    taken(dve, u)
                    own(rotate(t, k_sb.rearrange("p (h d) -> p h d", h=NKV), NKV,
                               (kr[:, :, 0, 0:HH], kr[:, :, 0, HH:HD]), tk))
                    dve.tensor_copy(kr[:, :, 1, :], kr[:, :, 0, :]).then_inc(s_kr, 1)
                elif kind in ("Q0", "Q1"):
                    h = int(kind[1])
                    if t >= 1:
                        full(dve, ("QT" + "ab"[h], t - 1))
                    dve.tensor_tensor(q_sb, ps[:, bank, :], bqrow[:, h * 512:(h + 1) * 512], ALU.add
                                      ).then_inc(bank_read[bank - 5], 1)
                    taken(dve, u)
                    part = qr[:, 8 * h:8 * h + 8, :]
                    rotate(t, q_sb.rearrange("p (h d) -> p h d", h=8), 8,
                           (part[:, :, 0:HH], part[:, :, HH:HD]), tq).then_inc(s_qr, 1)
                elif kind in ("W0", "W1"):
                    h = int(kind[1])
                    dve.wait_ge(s_xb, t + 1)
                    half_x = x_sb[:, t, h * 512:(h + 1) * 512]
                    dve.tensor_tensor(half_x, half_x, ps[:, bank, :], ALU.add).then_inc(bank_read[bank - 5], 1)
                    if h == 1:
                        taken(dve, ("W0", t))
                        taken(dve, ("W1", t))
                        norm_x(t, n + t, 1, 0)
                else:
                    dve.tensor_copy(lgs[:, t, :], ps[:, bank, 0:E]).then_inc(bank_read[bank - 5], 1)

            def soft(t, kh):
                m = NKV * t + kh
                lo = 0 if t else P
                dve.wait_ge(s_S, m + 1)
                if m >= 2:
                    dve.wait_ge(s_PTt, m - 1)
                sc = ps[:, 0:2, :].rearrange("p a (j s) -> p (a j) s", j=2)[:, :, lo:256]
                sv = pr[m % 2][:, :, lo:256]
                dve.scalar_tensor_tensor(out=sv, in0=sc, scalar=1.0 / math.sqrt(HD),
                                         in1=mask[:, lo:256].unsqueeze(1).to_broadcast([P, GQ, 256 - lo]),
                                         op0=ALU.mult, op1=ALU.add).then_inc(s_ss, 1)
                dve.wait_ge(s_ss, m + 1)
                gq = slice(kh * GQ, (kh + 1) * GQ)
                own(dve.tensor_reduce(mxs[:, gq], sv, AX.X, ALU.max))
                sk = sinkb[:, gq].rearrange("p (j r) -> p r j", r=2)
                mx = mxs[:, gq].rearrange("p (r j) -> p r j", r=2)
                own(dve.tensor_tensor(mx, mx, sk, ALU.max))
                dve.tensor_tensor(exs[:, 0, gq].rearrange("p (r j) -> p r j", r=2), sk, mx, ALU.subtract)
                dve.tensor_scalar(negm[:, gq], mxs[:, gq], -1.0, None, ALU.mult).then_inc(s_negm, 1)

            def normed_probs(t, kh):
                m = NKV * t + kh
                lo = 0 if t else P
                gq = slice(kh * GQ, (kh + 1) * GQ)
                dve.wait_ge(s_ex, m + 1)
                own(dve.tensor_tensor(den[:, gq], den[:, gq], exs[:, 1, gq], ALU.add))
                own(dve.reciprocal(rden[:, gq], den[:, gq]))
                sv = pr[m % 2][:, :, lo:256]
                dve.tensor_tensor(sv, sv, rden[:, gq].unsqueeze(2).to_broadcast([P, GQ, 256 - lo]), ALU.mult
                                  ).then_inc(s_pn, 1)

            for u in first_units:
                take(u, n)
            for t in range(T):
                soft(t, 0)
                for kh, (early, late) in enumerate(fillers(t)):
                    normed_probs(t, kh)
                    for u in early + late:
                        take(u, n)
                    if kh + 1 < NKV:
                        soft(t, kh + 1)
            for u in last_units:
                take(u, n)
            n += T
            route(1)
            experts(1)
            dve.wait_ge(s_rows2, 16 * 2)
            combine(1, n)

        @block.scalar
        def _(act):
            g = ctx.enter_context(act.register("act_extra"))
            act.reg_mov(g, 1)
            nth = ctx.enter_context(act.register("act_nth"))
            act.sem_inc(s_oyc, 1)
            act.sem_inc(s_oy, 32)
            act.dma_start(prm[PB1:PB1 + 16, :], conv_b1.rearrange("a (j p) -> (a j) p", p=P)).then_inc(s_small, 16)
            act.dma_start(prm[PDWB:PDWB + KD, :], conv_dwb.rearrange("a (j p) -> (a j) p", p=P)).then_inc(s_small, 16)
            act.dma_start(prm[PGAM:PGAM + KD, :], conv_ln_g.rearrange("a (j p) -> (a j) p", p=P)).then_inc(s_small, 16)
            act.dma_start(prm[PBET:PBET + KD, :], conv_ln_b.rearrange("a (j p) -> (a j) p", p=P)).then_inc(s_small, 16)
            act.dma_start(dw_r[:, :], conv_dw[0]).then_inc(s_small, 16)
            act.dma_start(pos_i[:, :], positions.rearrange("a (t p) -> (a t) p", p=P)).then_inc(s_small, 16)

            def norm_rows(l, w, signal):
                act.dma_start(lnrow[:, w, 0, :], ln_g[l, w].partition_broadcast(P)).then_inc(signal, 16)
                act.dma_start(lnrow[:, w, 1, :], ln_b[l, w].partition_broadcast(P)).then_inc(signal, 16)

            act.dma_start(resrow, conv_b2[0].partition_broadcast(P)).then_inc(s_rows, 16)
            act.dma_start(rw[:, :, :], router_w.rearrange("(p k) e -> p k e", k=KD)).then_inc(s_rows, 16)
            for w in range(2):
                norm_rows(0, w, s_rows)
            act.dma_start(rbrow[:, :], router_b.partition_broadcast(P)).then_inc(s_rows, 16)
            act.dma_start(sinkb[:, :], attn_sinks[0].partition_broadcast(P)).then_inc(s_rows, 16)
            for t in range(T):
                act.wait_ge(s_x0T, t + 1)
                act.activation(xT[:, 4:8, t * P:(t + 1) * P],
                               ps[:, 2 * (t % 2) + 1, :].rearrange("p (j n) -> p j n", j=4), ACT.Copy
                               ).then_inc(s_xTa, 1)
            act.wait_ge(s_pool0, 2)
            act.wait_ge(s_w1[KD // 2 - 1], 32)
            act.dma_start(y_dram[E * CAP:, :].rearrange("(p n) (h d) -> p (n h) d", p=P, h=2),
                          cv[:, KD - 1, :].unsqueeze(1).to_broadcast([P, (TBLK - E) * CAP // P * 2, S])
                          ).then_inc(s_yinit, 16)
            act.wait_ge(s_prC, 1)
            for c in range(KD):
                act.wait_ge(s_g1, c + 1)
                if c >= 2:
                    act.wait_ge(s_glu, glu_count(c - 2))
                act.activation(sgm[c % 2], ps[:, 1 + 2 * (c % 4), :], ACT.Sigmoid,
                               bias=prmT[:, PB1 + KD + c:PB1 + KD + c + 1]).then_inc(s_sgm, 1)
            act.wait_ge(s_yinit, 16)
            for c in range(DVE_TILES, KD):
                act.wait_ge(s_pec, c - DVE_TILES + 1)
                act.activation(cv[:, c, :], ps[:, 2 * (c % 4) - 4, :], ACT.Identity,
                               bias=prmT[:, PDWB + c:PDWB + c + 1]).then_inc(s_pecv, 1)
            act.wait_ge(s_rope, 2)
            act.activation(rope_w[:, 1, :], rope_w[:, 0, :], ACT.Sin, scale=0.5)
            act.activation(rope_w[:, 3, :], rope_w[:, 2, :], ACT.Sin, scale=1.0).then_inc(s_sin, 1)

            def silu_conv(t):
                act.wait_ge(s_Bt, t + 1)
                if t >= 2:
                    act.wait_ge(s_C, t - 1)
                for c in range(KD):
                    ins = act.activation(hc[t % 2][:, c, :], ps[:, 2 + c // 4, (c % 4) * P:(c % 4 + 1) * P], ACT.Silu,
                                         bias=prmT[:, PBET + c:PBET + c + 1], scale=prmT[:, PGAM + c:PGAM + c + 1])
                ins.then_inc(s_hc, 1)

            def normed(t):
                act.wait_ge(s_ln, t + 1)
                act.dma_start(xd_rows[:, t, :], x_sb[:, t, :]).then_inc(s_xst, 16)
                act.wait_ge(s_Dt, t + 1)
                act.activation(xTt.rearrange("p a b -> p (a b)"), ps[:, 6:8, :].rearrange("p a b -> p (a b)"),
                               ACT.Copy).then_inc(s_xTt, 1)

            silu_conv(0)
            for t in range(T):
                if t + 1 < T:
                    silu_conv(t + 1)
                if t >= 1:
                    normed(t - 1)
            normed(T - 1)
            act.dma_start(resrow, attn_bo[0].partition_broadcast(P)).then_inc(s_rows1, 16)
            norm_rows(1, 0, s_rows1)
            act.wait_ge(s_ropeT, 1)
            act.dma_start(bqrow, attn_bq[0].partition_broadcast(P)).then_inc(s_rows1, 16)
            act.dma_start(kvrow, kv_b.partition_broadcast(P)).then_inc(s_rows1, 16)

            def affinities(l):
                if l == 0:
                    act.wait_ge(s_lgc, T)
                else:
                    taken(act, ("E", T - 1))
                act.activation(aff[:, :, :], lgs[:, :, :], ACT.Sigmoid).then_inc(s_aff, 1)

            def experts(l):
                M0 = E * l

                def silu(e, b, later):
                    act.wait_ge(s_gate, e + (M0 + 1))
                    if later or l > 0:
                        act.wait_ge(s_h, e + (M0 - 1))
                    act.activation(sg[b], ps[:, 1, 0:256], ACT.Silu).then_inc(s_sg, 1)

                def store(e, eh, b, later):
                    act.wait_ge(s_dn, e + (M0 + 1))
                    if later or l > 0:
                        act.wait_ge(s_y[b], 32 * (eh + 8 * l))
                    act.activation(ysb[b], ps[:, 4, :], ACT.Copy).then_inc(s_yc, 1)
                    act.wait_ge(s_yc, e + (M0 + 1))
                    for h in range(2):
                        act.dma_start(y_dram[bass.ds(e * CAP, CAP), h * 512:(h + 1) * 512],
                                      ysb[b][h * CAP:(h + 1) * CAP, :]).then_inc(s_y[b], 16)

                def extras(e):
                    n = act.value_load(extra[0:1, l, bass.ds(e, 1)], min_val=0, max_val=NBLK - 1)
                    with act.If(n > 0):
                        with act.Fori(0, n):
                            now = act.snap(g, min_val=1, max_val=4096)
                            row = act.snap(nth, min_val=0, max_val=E - 2) * CAP + E * CAP
                            act.wait_ge(s_ogate, now)
                            act.activation(sg[2], ps[:, 5, 0:256], ACT.Silu).then_inc(s_osg, 1)
                            act.wait_ge(s_od, now)
                            act.wait_ge(s_oy, now * 32)
                            act.activation(ysb[2], ps[:, 7, :], ACT.Copy).then_inc(s_oyc, 1)
                            act.wait_ge(s_oyc, now + 1)
                            for h in range(2):
                                act.dma_start(y_dram[bass.ds(row, CAP), h * 512:(h + 1) * 512],
                                              ysb[2][h * CAP:(h + 1) * CAP, :]).then_inc(s_oy, 16)
                            act.reg_add(g, g, 1)
                            act.reg_add(nth, nth, 1)

                act.wait_ge(s_extra, l + 1)
                act.reg_mov(nth, 0)
                silu(0, 0, False)
                extras(0)
                silu(1, 1, False)
                store(0, 0, 0, False)
                extras(1)
                silu(2, 0, True)
                store(1, 0, 1, False)
                extras(2)
                silu(3, 1, True)
                store(2, 1, 0, True)
                extras(3)
                with act.Fori(0, (E - 4) // 2) as i:
                    silu(2 * i + 4, 0, True)
                    store(2 * i + 3, i + 1, 1, True)
                    extras(2 * i + 4)
                    silu(2 * i + 5, 1, True)
                    store(2 * i + 4, i + 2, 0, True)
                    extras(2 * i + 5)
                store(E - 1, E // 2 - 1, 1, True)

            affinities(0)
            experts(0)
            def take(u):
                kind, t = u
                into = {"Xa": xTt[:, 0:4, :], "Xb": xTt[:, 4:8, :], "Da": xTt[:, 0:4, :], "Db": xTt[:, 4:8, :],
                        "KT": kT[:, :, t * P:(t + 1) * P], "QTa": qT[t % 2][:, 0:4, :],
                        "QTb": qT[t % 2][:, 4:8, :]}.get(kind)
                if kind == "Da":
                    act.wait_ge(s_ln, 2 * T + t + 1)
                    act.dma_start(xd_rows[:, t, :], x_sb[:, t, :]).then_inc(s_xst, 16)
                if into is not None:
                    bank = full(act, u)
                    act.activation(into, ps[:, bank, :].rearrange("p (j n) -> p j n", j=4), ACT.Copy
                                   ).then_inc(bank_read[bank - 5], 1)

            def exps(t, kh):
                m = NKV * t + kh
                lo = 0 if t else P
                act.wait_ge(s_negm, m + 1)
                gq = slice(kh * GQ, (kh + 1) * GQ)
                for i in range(GQ):
                    h = kh * GQ + i
                    act.activation(pr[m % 2][:, i, lo:256], pr[m % 2][:, i, lo:256], ACT.Exp,
                                   bias=negm[:, h:h + 1], accum_out=den[:, h:h + 1])
                act.activation(exs[:, 1, gq], exs[:, 0, gq], ACT.Exp).then_inc(s_ex, 1)

            def keep_pt(t, kh):
                m = NKV * t + kh
                act.wait_ge(s_PTt, m + 1)
                if m >= 1:
                    act.wait_ge(s_O, m)
                s0 = 0 if t else 1
                pt = PT.rearrange("p (i s) n -> p i s n", s=2)[:, :, s0:2, :]
                src = ps[:, 2:4, :].rearrange("p a (i s n) -> p (a i) s n", i=2, s=2)[:, :, s0:2, :]
                act.activation(pt, src, ACT.Copy).then_inc(s_PT, 1)

            def keep_o(t, kh):
                m = NKV * t + kh
                act.wait_ge(s_O, m + 1)
                if t >= 2 and kh == 0:
                    full(act, ("W1", t - 2))
                act.activation(oT[t % 2][:, 2 * kh:2 * kh + 2, :], ps[:, 4, 0:256].rearrange("p (j n) -> p j n", j=2),
                               ACT.Copy).then_inc(s_oT, 1)

            for u in first_units:
                take(u)
            for t in range(T):
                exps(t, 0)
                for kh, (early, late) in enumerate(fillers(t)):
                    for u in early:
                        take(u)
                    if kh:
                        keep_o(t, kh - 1)
                    for u in late:
                        take(u)
                    keep_pt(t, kh)
                    if kh + 1 < NKV:
                        exps(t, kh + 1)
                keep_o(t, NKV - 1)
            for u in last_units:
                take(u)
            norm_rows(1, 1, s_rows2)
            affinities(1)
            experts(1)
            for t in range(T):
                act.wait_ge(s_ln, 3 * T + t + 1)
                act.dma_start(out_rows[:, t, :], x_sb[:, t, :]).then_inc(s_out, 16)
            act.wait_ge(s_out, 16 * T)

        @block.gpsimd
        def _(pool):
            done = [0]
            g = ctx.enter_context(pool.register("pool_extra"))
            r_pool = ctx.enter_context(pool.register("pool_r"))
            pool.reg_mov(g, 1)
            nth = ctx.enter_context(pool.register("pool_nth"))
            pool.sem_inc(s_oxt, 1)

            def own(ins):
                done[0] += 1
                ins.then_inc(s_pc, 1)
                pool.wait_ge(s_pc, done[0])

            own(pool.memset(ident[:, :], 0.0))
            pool.affine_select(out=ident[:, :], in_=ident[:, :], compare_op=ALU.not_equal, fill=1.0, base=0,
                               pattern=[[-1, P]], channel_multiplier=1).then_inc(s_pool0, 1)
            pool.memset(half[:, :], -0.5)
            pool.memset(cv[:, KD - 1, :], 0.0)
            pool.memset(hpad[:, :, 0:CW - 1], 0.0).then_inc(s_pool0, 1)
            pool.wait_ge(s_small, 16 * 6)
            pool.tensor_copy(pos_f[:, :], pos_i[:, :]).then_inc(s_rope, 1)
            own(pool.memset(zidx[:, :], 0))
            pool.dma_start(tok_dram.rearrange("(p n) a -> p (n a)", p=P), zidx[:, :]).then_inc(s_tokinit, 16)
            own(pool.memset(ones[:, :], 1.0))
            pool.affine_select(out=upper[:, :], in_=ones[:, :], compare_op=ALU.is_gt, fill=0.0, base=0,
                               pattern=[[1, P]], channel_multiplier=-1)
            own(pool.memset(before[:, :, :], 1.0))
            pool.affine_select(out=before[:, :, :], in_=before[:, :, :], compare_op=ALU.is_gt, fill=0.0, base=0,
                               pattern=[[1, E], [-1, E]], channel_multiplier=0)
            own(pool.memset(mask[:, :], 0.0))
            pool.affine_select(out=mask[:, 0:P], in_=mask[:, 0:P], compare_op=ALU.is_gt, fill=NEG, base=0,
                               pattern=[[1, P]], channel_multiplier=-1)
            pool.affine_select(out=mask[:, P:2 * P], in_=mask[:, P:2 * P], compare_op=ALU.is_ge, fill=NEG, base=0,
                               pattern=[[-1, P]], channel_multiplier=1)
            pool.iota(tokid[:, :], pattern=[[P, T]], base=0, channel_multiplier=1)
            exact = {"allow_small_or_imprecise_dtypes": True}
            pool.iota(ramp4[:, :], pattern=[[1, NG]], base=-NG, channel_multiplier=0, **exact)
            pool.iota(ramp16[:, :], pattern=[[1, E]], base=-E, channel_multiplier=0, **exact)
            pool.iota(ebase[:, :], pattern=[[CAP, E]], base=0, channel_multiplier=0, **exact)
            own(pool.iota(thr[:, :], pattern=[[CAP, NBLK - 1]], base=CAP, channel_multiplier=0, **exact))
            for i in range(HH):
                ins = pool.memset(invf[:, i:i + 1], float(THETA ** (-2.0 * i / HD)))
            own(ins)
            pool.wait_ge(s_x0T, T)
            pool.wait_ge(s_rows, 16 * 8)
            for t in range(T):
                own(pool.tensor_scalar(x_sb[:, t, :], x_sb[:, t, :], ALPHA, None, ALU.mult))
                pool.tensor_tensor(x_sb[:, t, :], x_sb[:, t, :], resrow, ALU.add).then_inc(s_xa, 1)
            pool.wait_ge(s_prC, 1)
            for c in range(DVE_TILES, KD):
                pool.wait_ge(s_g1, c if c < KD - 1 else KD)
                pool.affine_select(out=diag(c), in_=dwT[:, c, 0:CW].unsqueeze(2).to_broadcast([P, CW, P]),
                                   compare_op=ALU.is_equal, fill=0.0, base=0, pattern=[[0, CW], [-1, P]],
                                   channel_multiplier=1).then_inc(s_diag, 1)
            ang, turns, tmp = rope_w[:, 0, :], rope_w[:, 1, :], rope_w[:, 2, :]
            for t in range(T):
                ins = pool.tensor_scalar(rope_w[:, 0, t * HH:(t + 1) * HH], invf[:, :], posT[:, t:t + 1], None, ALU.mult)
            own(ins)
            own(pool.tensor_scalar(turns, ang, 1.0 / TWO_PI, None, ALU.mult))
            own(pool.tensor_scalar(turns, turns, MAGIC, None, ALU.add))
            own(pool.tensor_scalar(turns, turns, -MAGIC, None, ALU.add))
            for part in two_pi_parts():
                own(pool.tensor_scalar(tmp, turns, part, None, ALU.mult))
                own(pool.tensor_tensor(ang, ang, tmp, ALU.subtract))
            own(pool.tensor_scalar(ang, ang, 3.1415925, -3.1415925, ALU.min, ALU.max))
            pool.tensor_scalar(tmp, ang, 0.5, math.pi / 2, ALU.mult, ALU.add).then_inc(s_rope, 1)
            pool.wait_ge(s_sin, 1)
            sv, cv_ = rope_w[:, 1, :], rope_w[:, 3, :]
            sflat, cflat = (b[:, :, :].rearrange("p t d -> p (t d)") for b in (sinb, cosb))
            own(pool.tensor_tensor(sflat, sv, cv_, ALU.mult))
            pool.tensor_scalar(sflat, sflat, 2.0, None, ALU.mult)
            own(pool.tensor_tensor(cflat, sv, sv, ALU.mult))
            pool.tensor_scalar(cflat, cflat, -2.0, 1.0, ALU.mult, ALU.add).then_inc(s_ropeT, 1)

            def inverse_std(n):
                pool.wait_ge(s_mv, n + 1)
                own(pool.tensor_scalar(vareps[:, n:n + 1], mv[:, n, 1:2], EPS, None, ALU.add))
                pool.tensor_tensor(rstd[:, n:n + 1], vareps[:, n:n + 1], half[:, :], ALU.pow).then_inc(s_rs, 1)

            for n in range(2 * T):
                inverse_std(n)

            def rows_of_tokens(l):
                if l == 0:
                    pool.wait_ge(s_tokinit, 16)
                pool.wait_ge(s_rowi, l + 1)
                for t in range(T):
                    for j in range(2):
                        pool.indirect_dma_start(out=tok_dram[:, :],
                                                out_offset=bass.IndirectOffsetOnAxis(ap=rowi[:, j, t:t + 1], axis=0),
                                                in_=tokid[:, t:t + 1], in_offset=None).then_inc(s_scat, 16)
                pool.wait_ge(s_scat, 16 * 2 * T * (l + 1))
                pool.dma_start(tok_r[:, :], tok_dram.rearrange("(p n) a -> p (n a)", p=TBLK)).then_inc(s_tokr, 16)
                pool.wait_ge(s_tokT, l + 1)

            def gather_x(where, idx_col, signal):
                pool.indirect_dma_start(out=where[0:CAP, :], out_offset=None, in_=x_dram[:, :],
                                        in_offset=bass.IndirectOffsetOnAxis(ap=idx[:, idx_col:idx_col + 1], axis=0)
                                        ).then_inc(signal, 16)

            def experts(l):
                M0 = E * l

                def gather(e, b, later):
                    if later or l > 0:
                        pool.wait_ge(s_xt, e + (M0 - 1))
                    pool.tensor_copy(idx[:, b:b + 1], tokT[:, bass.ds(e, 1)]).then_inc(s_idx, 1)
                    count = in_register(pool, r_pool, e + (M0 + 1))
                    pool.wait_ge(s_xst, 16 * T * (l + 1))
                    pool.wait_ge(s_idx, count)
                    gather_x(xg[b], b, s_xg[b])

                def extras(e):
                    n = pool.value_load(extra[0:1, l, bass.ds(e, 1)], min_val=0, max_val=NBLK - 1)
                    with pool.If(n > 0):
                        with pool.Fori(0, n):
                            now = pool.snap(g, min_val=1, max_val=4096)
                            column = pool.snap(nth, min_val=0, max_val=E - 2) + E
                            pool.wait_ge(s_oxt, now)
                            pool.tensor_copy(idx[:, 2:3], tokT[:, bass.ds(column, 1)]).then_inc(s_oidx, 1)
                            pool.wait_ge(s_xst, 16 * T * (l + 1))
                            pool.wait_ge(s_oidx, now)
                            gather_x(xg[2], 2, s_oxg)
                            pool.reg_add(g, g, 1)
                            pool.reg_add(nth, nth, 1)

                pool.wait_ge(s_extra, l + 1)
                pool.reg_mov(nth, 0)
                gather(0, 0, False)
                gather(1, 1, False)
                extras(0)
                with pool.Fori(0, (E - 2) // 2) as i:
                    gather(2 * i + 2, 0, True)
                    extras(2 * i + 1)
                    gather(2 * i + 3, 1, True)
                    extras(2 * i + 2)
                extras(E - 1)

            def combine(l, n):
                stored = in_register(pool, r_pool, pool.snap(g, min_val=1, max_val=4096) * 32)
                for b in range(2):
                    pool.wait_ge(s_y[b], 32 * 8 * (l + 1))
                pool.wait_ge(s_oy, stored)

                def gather_y(t):
                    if T * l + t >= 2:
                        pool.wait_ge(s_cmb, T * l + t - 1)
                    for j in range(2):
                        pool.indirect_dma_start(out=yg[t % 2][j], out_offset=None, in_=y_dram[:, :],
                                                in_offset=bass.IndirectOffsetOnAxis(ap=rowi[:, j, t:t + 1], axis=0)
                                                ).then_inc(s_yg[t % 2], 16)

                gather_y(0)
                gather_y(1)
                for t in range(T):
                    if t + 2 < T:
                        gather_y(t + 2)
                    inverse_std(n + t)

            rows_of_tokens(0)
            experts(0)
            combine(0, 2 * T)
            pool.wait_ge(s_rows1, 16 * 5)
            for t in range(T):
                full(pool, ("Xa", t))
                full(pool, ("Xb", t))
                own(pool.tensor_scalar(x_sb[:, t, :], x_sb[:, t, :], ALPHA, None, ALU.mult))
                pool.tensor_tensor(x_sb[:, t, :], x_sb[:, t, :], resrow, ALU.add).then_inc(s_xb, 1)
                inverse_std(3 * T + t)
            rows_of_tokens(1)
            experts(1)
            combine(1, 4 * T)


_INS = ['x', 'positions', 'conv_w1', 'conv_b1', 'conv_dw', 'conv_dwb', 'conv_ln_g', 'conv_ln_b',
        'conv_w2', 'conv_b2', 'kv_w', 'kv_b', 'attn_wq', 'attn_bq', 'attn_sinks', 'attn_wo', 'attn_bo',
        'router_w', 'router_b', 'moe_w_gate', 'moe_w_up', 'moe_w_down', 'ln_g', 'ln_b']
_OUTS = [((1, 512, 1024), 'float32')]


def kernel(**inputs):
    import numpy as _np
    import concourse.bacc as _bacc
    from concourse import mybir as _mybir
    from concourse.bass_utils import run_bass_kernel_spmd as _run

    nc = _bacc.Bacc("TRN2", target_bir_lowering=False, num_devices=1)
    arrays, args = {}, []
    for name in _INS:
        a = _np.ascontiguousarray(inputs[name])
        arrays[f"in_{name}_dram"] = a
        args.append(nc.dram_tensor(f"in_{name}_dram", a.shape, _mybir.dt.from_np(a.dtype), kind="ExternalInput").ap())
    for i, (shape, dtype) in enumerate(_OUTS):
        dt = _mybir.dt.from_np(_np.dtype(dtype))
        args.append(nc.dram_tensor(f"out_{i}_dram", shape, dt, kind="ExternalOutput").ap())
    trunk(nc, *args)
    r = _run(nc, [arrays], core_ids=[0])
    got = tuple(r.results[0][f"out_{i}_dram"] for i in range(len(_OUTS)))
    return got[0]
```

```python
import math
from contextlib import ExitStack

import concourse.bass as bass
from concourse import mybir

F32 = mybir.dt.float32
BF16 = mybir.dt.bfloat16
I32 = mybir.dt.int32
U32 = mybir.dt.uint32
ALU = mybir.AluOpType
ACT = mybir.ActivationFunctionType
AX = mybir.AxisListType

P = 128
D = 1024
S = 512
T = S // P
KD = D // P
CW = 31
HD = 64
HH = HD // 2
NQ = D // HD
NKV = 4
GQ = NQ // NKV
KVD = NKV * HD
E = 16
NG = 4
EPG = E // NG
F = D // 2
DEPTH = 2
CAP = 64
NBLK = S // CAP
TBLK = 2 * E
assert 2 * S // CAP <= E
DVE_TILES = 6
ALPHA = (2.0 * DEPTH) ** 0.25
EPS = 1e-5
NEG = -1e30
THETA = 10000.0
NLN = 5 * T

PB1, PDWB, PGAM, PBET, NPRM = 0, 16, 24, 32, 40

TWO_PI = 2.0 * math.pi


def two_pi_parts():
    parts, rest = [], TWO_PI
    for bits in (6, 15, 24):
        part = math.floor(rest * 2.0 ** bits) / 2.0 ** bits
        parts.append(part)
        rest -= part
    return parts + [rest]


MAGIC = 1.5 * 2 ** 23


def trunk(nc, x_in, positions, conv_w1, conv_b1, conv_dw, conv_dwb, conv_ln_g, conv_ln_b,
          conv_w2, conv_b2, kv_w, kv_b, attn_wq, attn_bq, attn_sinks, attn_wo, attn_bo,
          router_w, router_b, moe_w_gate, moe_w_up, moe_w_down, ln_g, ln_b, out):
    x_rows = x_in.rearrange("a (t p) d -> p (a t) d", p=P)
    out_rows = out.rearrange("a (t p) d -> p (a t) d", p=P)

    x_dram = nc.dram_tensor("x_dram", [S, D], F32).ap()
    tok_dram = nc.dram_tensor("tok_dram", [E * S, 1], U32).ap()
    y_dram = nc.dram_tensor("y_dram", [TBLK * CAP, D], F32).ap()
    xd_rows = x_dram.rearrange("(t p) d -> p t d", p=P)

    with ExitStack() as ctx:
        def sb(name, shape, dt=F32):
            return ctx.enter_context(nc.sbuf_tensor(name, shape, dt))

        def sem(name):
            return ctx.enter_context(nc.semaphore(name))

        wring = sb("wring", [P, 6, KD * F])
        x_sb = sb("x_sb", [P, T, D])
        arena = sb("arena", [P, 14592])
        rows = sb("rows", [P, 2 * D + KVD * 2])
        lnrow = sb("lnrow", [P, 2, 2, D])
        prm = sb("prm", [NPRM, P])
        prmT = sb("prmT", [P, NPRM])
        dwT = sb("dwT", [P, KD, 32])
        rw = sb("rw", [P, KD, E])
        ident = sb("ident", [P, P])
        upper = sb("upper", [P, P], BF16)
        ones = sb("ones", [P, P], BF16)
        mask = sb("mask", [P, 2 * P])
        rbrow = sb("rbrow", [P, E])
        sinkb = sb("sinkb", [P, NQ])
        pos_i = sb("pos_i", [T, P], I32)
        pos_f = sb("pos_f", [T, P])
        posT = sb("posT", [P, T])
        invf = sb("invf", [P, HH])
        cosb = sb("cosb", [P, T, HH])
        sinb = sb("sinb", [P, T, HH])
        tokid = sb("tokid", [P, T], U32)
        ramp4 = sb("ramp4", [P, NG])
        ramp16 = sb("ramp16", [P, E])
        ebase = sb("ebase", [P, E])
        tbase = sb("tbase", [P, E])
        thr = sb("thr", [P, NBLK - 1])
        half = sb("half", [P, 1])
        mv = sb("mv", [P, NLN, 2])
        vareps = sb("vareps", [P, NLN])
        rstd = sb("rstd", [P, NLN])
        bns = sb("bns", [P, 2, 6])
        rankf = sb("rankf", [P, T, E])
        aff = sb("aff", [P, T, E])
        sel, seln, r1 = (sb(name, [P, E]) for name in ("sel", "seln", "r1"))
        r2, r3 = (sb(name, [P, 2, E]) for name in ("r2", "r3"))
        gs = sb("gs", [P, 5, NG])
        gsm = sb("gsm", [P, 2])
        onehot = sb("onehot", [P, 2, T, E])
        gatev = sb("gatev", [P, 2, T])
        gsum = sb("gsum", [P, T])
        gate_w = sb("gate_w", [P, 2, T])
        mask_b = sb("mask_b", [P, T, E], BF16)
        rowf = sb("rowf", [P, 2, T])
        rowi = sb("rowi", [P, 2, T], U32)
        placef = sb("placef", [P, 2])
        place_i = sb("place_i", [P, 2, T], U32)
        cntf = sb("cntf", [P, 4, E])
        before = sb("before", [P, E, E])
        extra = sb("extra", [1, DEPTH, E], I32)
        tok_r = sb("tok_r", [E * NBLK, CAP], U32)
        tok_f = sb("tok_f", [E * NBLK, CAP])
        tokT = sb("tokT", [CAP, E * NBLK], U32)
        idx = sb("idx", [CAP, 3], U32)
        exs = sb("exs", [P, 2, NQ])
        negm = sb("negm", [P, NQ])
        mxs = sb("mxs", [P, NQ])
        den = sb("den", [P, NQ])
        rden = sb("rden", [P, NQ])

        resrow, bqrow = (rows[:, i * D:(i + 1) * D] for i in range(2))
        rope_w = bqrow[:, 0:4 * T * HH].rearrange("p (a n) -> p a n", a=4)
        kvrow = rows[:, 2 * D:2 * D + 2 * KVD]

        def view(at, *shape):
            n = math.prod(shape)
            v = arena[:, at:at + n]
            if len(shape) == 2:
                v = v.rearrange("p (a b) -> p a b", a=shape[0])
            if len(shape) == 3:
                v = v.rearrange("p (a b c) -> p a b c", a=shape[0], b=shape[1])
            return v

        PADW = S + CW - 1
        xT = view(0, KD, S)
        hpad = view(4096, KD, PADW)
        cv = view(4096 + KD * PADW, KD, S)
        hc = [view(0 + i * D, KD, P) for i in range(2)]
        ntok = [view(2048 + i * D, D) for i in range(2)]
        odd = view(13568, S)
        AT = 4096 + KD * PADW + KD * S
        sgm = [view(AT + i * S, S) for i in range(2)]
        xTt = view(13568, KD, P)
        dw_r = view(AT, D)[0:CW, :]
        q_sb = view(0, D // 2)
        k_sb = view(512, KVD)
        tk = [view(768 + i * P, P) for i in range(2)]
        qr = view(1024, NQ, HD)
        kr = view(2048, NKV, 2, HD)
        tq = [view(2560 + i * 256, 256) for i in range(2)]
        kT = view(3072, NKV, S)
        v_sb = view(5120, T, KVD)
        qT = [view(6144 + i * D, KD, P) for i in range(2)]
        pr = [view(8192 + i * D, GQ, 2 * P) for i in range(2)]
        PT = view(10240, KD, P)
        oT = [view(11264 + i * D, KD, P) for i in range(2)]
        xg = [view(i * D, D) for i in range(3)]
        xgT = [view(3072 + i * S, KD, CAP) for i in range(3)]
        sg = [view(4608 + i * 256, 256) for i in range(3)]
        hh = [view(5376 + i * 256, 256) for i in range(3)]
        hT = [view(6144 + i * 256, 2, P) for i in range(3)]
        ysb = [view(6912 + i * S, S) for i in range(3)]
        yg = [[view(at + j * D, D) for j in range(2)] for at in (8448, 8448 + 2 * D, 0, 2 * D)]

        spare = view(9472, KD, F)

        rows_t = view(8448, T, E)
        rows_j = view(8448 + T * E, 2 * T, E)
        cmp7 = view(8448 + 3 * T * E, E, NBLK - 1)
        extras_before = view(8448 + 5 * T * E, E, E)

        ps = ctx.enter_context(nc.psum_tensor("ps", [P, 8, 512], F32))

        s_x = [sem(f"s_x{t}") for t in range(T)]
        s_small = sem("s_small")
        s_rows = sem("s_rows")
        s_rows1 = sem("s_rows1")
        s_rows2 = sem("s_rows2")
        s_pool0 = sem("s_pool0")
        s_pc = sem("s_pc")
        s_dc = sem("s_dc")
        s_tokinit = sem("s_tokinit")
        s_yinit = sem("s_yinit")
        s_prT = sem("s_prT")
        s_prC = sem("s_prC")
        s_x0T = sem("s_x0T")
        s_xTd = sem("s_xTd")
        s_w1 = [sem(f"s_w1_{i}") for i in range(4)]
        s_w2 = [sem(f"s_w2_{i}") for i in range(2)]
        s_g1 = sem("s_g1")
        s_sgm = sem("s_sgm")
        s_glu = sem("s_glu")
        s_tap = sem("s_tap")
        s_diag = sem("s_diag")
        s_pec = sem("s_pec")
        s_pecv = sem("s_pecv")
        s_xa = sem("s_xa")
        s_At = sem("s_At")
        s_mv = sem("s_mv")
        s_rs = sem("s_rs")
        s_nt = sem("s_nt")
        s_Bt = sem("s_Bt")
        s_hc = sem("s_hc")
        s_C = sem("s_C")
        s_cadd = sem("s_cadd")
        s_ln = sem("s_ln")
        s_xst = sem("s_xst")
        s_Dt = sem("s_Dt")
        s_xTt = sem("s_xTt")
        s_lg = sem("s_lg")
        s_aff = sem("s_aff")
        s_mask = sem("s_mask")
        s_rank = sem("s_rank")
        s_rankc = sem("s_rankc")
        s_place = sem("s_place")
        s_rowi = sem("s_rowi")
        s_extra = sem("s_extra")
        s_scat = sem("s_scat")
        s_tokr = sem("s_tokr")
        s_tokf = sem("s_tokf")
        s_tokt = sem("s_tokt")
        s_tokT = sem("s_tokT")
        s_wg = [sem(f"s_wg{i}") for i in range(2)]
        s_wu = [sem(f"s_wu{i}") for i in range(2)]
        s_wd = [sem(f"s_wd{i}") for i in range(2)]
        s_wspare = sem("s_wspare")
        s_idx = sem("s_idx")
        s_xg = [sem(f"s_xg{i}") for i in range(2)]
        s_xt = sem("s_xt")
        s_xgT = sem("s_xgT")
        s_gate = sem("s_gate")
        s_gud = sem("s_gud")
        s_sg = sem("s_sg")
        s_up = sem("s_up")
        s_h = sem("s_h")
        s_ht = sem("s_ht")
        s_hTc = sem("s_hTc")
        s_dn = sem("s_dn")
        s_yc = sem("s_yc")
        s_y = [sem(f"s_y{i}") for i in range(2)]
        s_oidx = sem("s_oidx")
        s_oxg = sem("s_oxg")
        s_oxt = sem("s_oxt")
        s_oxgT = sem("s_oxgT")
        s_ogate = sem("s_ogate")
        s_osg = sem("s_osg")
        s_oup = sem("s_oup")
        s_oh = sem("s_oh")
        s_oht = sem("s_oht")
        s_ohTc = sem("s_ohTc")
        s_od = sem("s_od")
        s_oyc = sem("s_oyc")
        s_oy = sem("s_oy")
        s_yg = [sem(f"s_yg{t}") for t in range(T)]
        s_xal = sem("s_xal")
        s_y0g = sem("s_y0g")
        s_cmb = sem("s_cmb")
        s_rope = sem("s_rope")
        s_sin = sem("s_sin")
        s_ropeT = sem("s_ropeT")
        s_wkv = sem("s_wkv")
        s_wq = [sem(f"s_wq{i}") for i in range(2)]
        s_wo = [sem(f"s_wo{i}") for i in range(2)]
        bank_full = [sem(f"bank_full{i}") for i in range(3)]
        bank_read = [sem(f"bank_read{i}") for i in range(3)]
        s_kr = sem("s_kr")
        s_qr = sem("s_qr")
        s_S = sem("s_S")
        s_ss = sem("s_ss")
        s_negm = sem("s_negm")
        s_ex = sem("s_ex")
        s_pn = sem("s_pn")
        s_PTt = sem("s_PTt")
        s_PT = sem("s_PT")
        s_O = sem("s_O")
        s_oT = sem("s_oT")
        s_xb = sem("s_xb")
        s_out = sem("s_out")

        block = ctx.enter_context(nc.Block())

        w1_src = conv_w1[0].rearrange("(p k) (h n) -> p k h n", k=KD, h=2)
        w2_src = conv_w2[0].rearrange("(j p) n -> p j n", p=P)
        kv_src = kv_w.rearrange("(p k) n -> p k n", k=KD)
        wq_src = attn_wq[0].rearrange("(p k) n -> p k n", k=KD)
        wo_src = attn_wo[0].rearrange("(k p) n -> p k n", p=P)
        gate_src = moe_w_gate.rearrange("l e (p k) f -> p (l e) (k f)", k=KD)
        up_src = moe_w_up.rearrange("l e (p k) f -> p (l e) (k f)", k=KD)
        down_src = moe_w_down.rearrange("l e (j p) n -> p (l e) j n", p=P)

        def fillers(t):
            plan = [("Xa Xb", "KV R"), ("Q0", "W0"), ("Q1", "KT"), ("QTa W1", "QTb Da Db E")]
            lag = {"X": 1, "K": 1, "Q": 1, "W": -1, "D": -2, "E": -2, "R": -3}
            units = [[[(u, t + lag[u[0]]) for u in part.split()] for part in pair] for pair in plan]
            return [tuple([(u, n) for u, n in part if 0 <= n < T] for part in pair) for pair in units]

        first_units = [(u, 0) for u in "Xa Xb KV Q0 Q1 KT QTa QTb".split()]
        last_units = [("R", T - 3), ("W0", T - 1), ("Da", T - 2), ("Db", T - 2), ("E", T - 2), ("W1", T - 1),
                      ("R", T - 2), ("Da", T - 1), ("Db", T - 1), ("E", T - 1), ("R", T - 1)]
        order = first_units + [u for t in range(T) for pair in fillers(t) for part in pair for u in part] + last_units
        place = {u: (5 + i % 3, i // 3 + 1) for i, u in enumerate(order)}

        def free(pe, u):
            bank, n = place[u]
            if n > 1:
                pe.wait_ge(bank_read[bank - 5], n - 1)

        def full(eng, u):
            bank, n = place[u]
            eng.wait_ge(bank_full[bank - 5], n)
            return bank

        def taken(eng, u):
            bank, n = place[u]
            eng.wait_ge(bank_read[bank - 5], n)

        glu_order = [0, 1, 2, 3, 4, 6, 5, 7]

        def glu_count(c):
            return glu_order.index(c) + 1

        def diag(c):
            return wring[:, 2 + c - DVE_TILES, 0:CW * P].rearrange("p (k n) -> p k n", k=CW)

        def slot(i, *dims):
            v = wring[:, i, :]
            if len(dims) == 1:
                return v.rearrange("p (k n) -> p k n", k=dims[0])
            return v.rearrange("p (k h n) -> p k h n", k=dims[0], h=dims[1])

        def in_register(eng, reg, value):
            if isinstance(value, int):
                return value
            eng.reg_mov(reg, value)
            return eng.snap(reg, min_val=0, max_val=1 << 16)

        @block.sync
        def _(sp):
            for t in range(T):
                sp.dma_start(x_sb[:, t, :], x_rows[:, t, :]).then_inc(s_x[t], 16)
            for i in range(4):
                for h in range(2):
                    sp.dma_start(slot(i, KD, 2)[:, :, h, :],
                                 w1_src[:, :, h, 256 * i:256 * i + 256]).then_inc(s_w1[i], 16)
            for i in range(2):
                sp.dma_start(slot(4 + i, 4), w2_src[:, 4 * i:4 * i + 4, :]).then_inc(s_w2[i], 16)

            def gate(l, e, b):
                sp.dma_start(wring[:, 3 * b, :], gate_src[:, bass.ds(E * l + e, 1), :]).then_inc(s_wg[b], 16)

            def up(l, e, b):
                sp.dma_start(wring[:, 3 * b + 1, :], up_src[:, bass.ds(E * l + e, 1), :]).then_inc(s_wu[b], 16)

            def down(l, e, b):
                sp.dma_start(slot(3 * b + 2, 4), down_src[:, bass.ds(E * l + e, 1), :, :]).then_inc(s_wd[b], 16)

            def gate_2(l):
                sp.dma_start(spare.rearrange("p k n -> p (k n)"), gate_src[:, E * l + 2, :]).then_inc(s_wspare, 16)

            def experts_from_2(l):
                def load(e, b, own_gate):
                    sp.wait_ge(s_gud, e + (E * l - 1))
                    if not own_gate:
                        gate(l, e, b)
                    up(l, e, b)
                    sp.wait_ge(s_dn, e + (E * l - 1))
                    down(l, e, b)

                load(2, 0, True)
                load(3, 1, False)
                with sp.Fori(0, (E - 4) // 2) as i:
                    for b in range(2):
                        load(2 * i + 4 + b, b, False)

            sp.wait_ge(s_g1, 2)
            gate(0, 0, 0)
            sp.wait_ge(s_g1, 4)
            up(0, 0, 0)
            sp.wait_ge(s_pec, 1)
            down(0, 0, 0)
            sp.wait_ge(s_pec, 2)
            gate(0, 1, 1)
            sp.wait_ge(s_At, T)
            gate_2(0)
            sp.wait_ge(s_C, T)
            up(0, 1, 1)
            down(0, 1, 1)
            experts_from_2(0)
            sp.wait_ge(s_gud, E - 1)
            sp.dma_start(slot(0, KD), kv_src).then_inc(s_wkv, 16)
            for t in range(T):
                sp.wait_ge(s_yg[t], 32)
            sp.dma_start(slot(1, KD), wq_src[:, :, 0:512]).then_inc(s_wq[0], 16)
            sp.wait_ge(s_dn, E - 1)
            sp.dma_start(slot(2, KD), wq_src[:, :, 512:1024]).then_inc(s_wq[1], 16)
            sp.wait_ge(s_gud, E)
            sp.dma_start(slot(3, KD), wo_src[:, :, 0:512]).then_inc(s_wo[0], 16)
            sp.dma_start(slot(4, KD), wo_src[:, :, 512:1024]).then_inc(s_wo[1], 16)
            sp.wait_ge(s_dn, E)
            down(1, 1, 1)
            full(sp, ("KV", T - 1))
            gate(1, 0, 0)
            full(sp, ("Q1", T - 1))
            up(1, 0, 0)
            down(1, 0, 0)
            full(sp, ("W1", T - 1))
            gate(1, 1, 1)
            up(1, 1, 1)
            gate_2(1)
            experts_from_2(1)

        @block.tensor
        def _(pe):
            g = ctx.enter_context(pe.register("pe_extra"))
            r_pe = [ctx.enter_context(pe.register(f"pe_r{i}")) for i in range(2)]
            pe.reg_mov(g, 1)

            def transposes(bank, src, signal, count=KD, step=KD):
                for j in range(count):
                    last = pe.transpose(ps[:, bank + j // 4, (j % 4) * P:(j % 4) * P + P],
                                        src(j), ident[:, :])
                last.then_inc(signal, 1)

            pe.wait_ge(s_pool0, 1)
            for t in range(T):
                pe.wait_ge(s_x[t], 16)
                if t >= 2:
                    pe.wait_ge(s_xTd, t - 1)
                transposes(2 * (t % 2), lambda j: x_sb[:, t, j::KD], s_x0T)
            pe.wait_ge(s_xTd, T)
            def parameters():
                pe.wait_ge(s_small, 16 * 6)
                pe.transpose(ps[:, 5, 0:NPRM], prm[:, :], ident[0:NPRM, 0:NPRM])
                for c in range(KD):
                    pe.transpose(ps[:, 4, 32 * c:32 * c + CW], dw_r[:, c * P:(c + 1) * P], ident[0:CW, 0:CW])
                pe.wait_ge(s_rope, 1)
                pe.transpose(ps[:, 5, 64:64 + T], pos_f[:, :], ident[0:T, 0:T]).then_inc(s_prT, 1)

            for c in range(KD):
                pe.wait_ge(s_w1[c // 2], 32)
                if c == 2:
                    pe.wait_ge(s_prC, 1)
                if c >= 4:
                    pe.wait_ge(s_glu, c - 3)
                w = slot(c // 2, KD, 2)
                for h in range(2):
                    for k in range(KD):
                        last = pe.matmul(ps[:, 2 * (c % 4) + h, :],
                                         w[:, k, h, (c % 2) * P:(c % 2) * P + P], xT[:, k, :],
                                         start=(k == 0), stop=(k == KD - 1))
                last.then_inc(s_g1, 1)
                if c == 0:
                    parameters()

            for c in range(DVE_TILES, KD):
                pe.wait_ge(s_glu, glu_count(c))
                pe.wait_ge(s_diag, c - DVE_TILES + 1)
                for k in range(CW):
                    last = pe.matmul(ps[:, 2 * (c % 4) - 4, :], diag(c)[:, k, :], hpad[:, c, k:k + S],
                                     start=(k == 0), stop=(k == CW - 1))
                last.then_inc(s_pec, 1)

            def stage_a(t):
                if t >= 1:
                    pe.wait_ge(s_nt, t)
                transposes(0, lambda c: cv[:, c, t * P:(t + 1) * P], s_At)

            def stage_b(t):
                pe.wait_ge(s_nt, t + 1)
                if t >= 1:
                    pe.wait_ge(s_hc, t)
                transposes(2, lambda c: ntok[t % 2][:, c * P:(c + 1) * P], s_Bt)

            def stage_c(t):
                pe.wait_ge(s_hc, t + 1)
                if t == 0:
                    pe.wait_ge(s_w2[0], 16)
                    pe.wait_ge(s_w2[1], 16)
                if t >= 1:
                    pe.wait_ge(s_cadd, t)
                for h in range(2):
                    for c in range(KD):
                        if h == 1 and c == KD // 2 and t + 1 < T:
                            stage_b(t + 1)
                        last = pe.matmul(ps[:, 4 + h, :], hc[t % 2][:, c, :],
                                         slot(4 + c // 4, 4)[:, c % 4, h * 512:(h + 1) * 512],
                                         start=(c == 0), stop=(c == KD - 1))
                last.then_inc(s_C, 1)

            def stage_d(t):
                pe.wait_ge(s_ln, t + 1)
                if t >= 1:
                    pe.wait_ge(s_aff, t)
                    pe.wait_ge(s_rankc, min(t, T - 2))
                transposes(6, lambda j: x_sb[:, t, j::KD], s_Dt)
                pe.wait_ge(s_xTt, t + 1)
                for k in range(KD):
                    last = pe.matmul(ps[:, 6, 0:E], xTt[:, k, :], rw[:, k, :], start=(k == 0), stop=(k == KD - 1))
                last.then_inc(s_lg, 1)

            def rank_products(l, t, bank):
                pe.wait_ge(s_mask, T * l + t + 1)
                for u in range(t + 1):
                    last = pe.matmul(ps[:, bank, 0:E], (upper if u == t else ones)[:, :], mask_b[:, u, :],
                                     start=(u == 0), stop=(u == t))
                if t == T - 1:
                    for u in range(T):
                        last = pe.matmul(ps[:, bank, E:2 * E], ones[:, :], mask_b[:, u, :],
                                         start=(u == 0), stop=(u == T - 1))
                return last

            def stage_r(t):
                if t >= 1:
                    pe.wait_ge(s_rankc, t)
                rank_products(0, t, 7).then_inc(s_rank, 1)

            pe.wait_ge(s_pecv, KD - DVE_TILES)
            pe.wait_ge(s_tap, (CW + 1) * DVE_TILES)
            stage_a(0)
            stage_b(0)
            stage_a(1)
            for t in range(T):
                stage_c(t)
                if t >= 2:
                    stage_r(t - 2)
                if t + 2 < T:
                    stage_a(t + 2)
                if t >= 1:
                    stage_d(t - 1)
            stage_d(T - 1)
            stage_r(T - 2)
            stage_r(T - 1)

            def token_table(l):
                pe.wait_ge(s_tokf, l + 1)
                pe.transpose(ps[0:CAP, 1, 0:E * NBLK], tok_f[:, :], ident[:, :]).then_inc(s_tokt, 1)

            def gathered_T(src, signal):
                for j in range(KD):
                    last = pe.transpose(ps[:, 0, j * CAP:(j + 1) * CAP], src[0:CAP, j::KD], ident[0:CAP, 0:CAP])
                last.then_inc(signal, 1)

            def half_products(bank, act, w, signal, first=None):
                for k in range(KD):
                    for h in range(2):
                        mm = pe.matmul(ps[h * CAP:(h + 1) * CAP, bank, 0:256], act[:, k, :],
                                       w[:, k, h * 256:(h + 1) * 256], start=(k == 0), stop=(k == KD - 1))
                        if first is not None and k == 0 and h == 0:
                            mm.then_inc(first, 1)
                mm.then_inc(signal, 1)

            def down_products(bank, act, w, signal):
                for j in range(4):
                    for h in range(2):
                        mm = pe.matmul(ps[h * CAP:(h + 1) * CAP, bank, :],
                                       act[:, j % 2, (j // 2) * CAP:(j // 2 + 1) * CAP],
                                       w[:, j, h * 512:(h + 1) * 512], start=(j == 0), stop=(j == 3))
                mm.then_inc(signal, 1)

            def experts(l):
                M0 = E * l
                W0 = 8 * l

                def stage_t(e, eh, b):
                    gathered = in_register(pe, r_pe[0], 16 * (eh + (W0 + 1)))
                    copied = in_register(pe, r_pe[1], e + M0)
                    pe.wait_ge(s_pool0, 1)
                    pe.wait_ge(s_xg[b], gathered)
                    if not (l == 0 and isinstance(e, int) and e == 0):
                        pe.wait_ge(s_xgT, copied)
                    gathered_T(xg[b], s_xt)

                def gate_weights(e, b):
                    return spare if isinstance(e, int) and e == 2 else slot(3 * b, KD)

                def stage_g(e, eh, b, first):
                    if isinstance(e, int) and e == 2:
                        pe.wait_ge(s_wspare, 16 * (l + 1))
                    elif b == 0 and not (isinstance(e, int) and e == 0):
                        pe.wait_ge(s_wg[0], 16 * (eh + 7 * l))
                    else:
                        pe.wait_ge(s_wg[b], 16 * (eh + ((8 - (b == 0)) * l + 1)))
                    pe.wait_ge(s_xgT, e + (M0 + 1))
                    if first or l > 0:
                        pe.wait_ge(s_sg, e + M0)
                    half_products(1, xgT[b], gate_weights(e, b), s_gate, s_gud if first else None)

                def stage_u(e, eh, b, later):
                    pe.wait_ge(s_wu[b], 16 * (eh + (W0 + 1)))
                    if later or l > 0:
                        pe.wait_ge(s_h, e + M0)
                    half_products(2, xgT[b], slot(3 * b + 1, KD), s_up)

                def stage_h(e, b, later=True, last=False):
                    pe.wait_ge(s_h, e + (M0 + 1))
                    if later or l > 0:
                        pe.wait_ge(s_hTc, e + M0)
                    for c in range(2):
                        tr = pe.transpose(ps[:, 3, c * P:(c + 1) * P], hh[b][:, c * P:(c + 1) * P], ident[:, :])
                        if last and c == 0:
                            tr.then_inc(s_gud, 1)
                    tr.then_inc(s_ht, 1)

                def stage_y(e, eh, b, later=True):
                    pe.wait_ge(s_wd[b], 16 * (eh + (W0 + 1)))
                    pe.wait_ge(s_hTc, e + (M0 + 1))
                    if later or l > 0:
                        pe.wait_ge(s_yc, e + M0)
                    down_products(4, hT[b], slot(3 * b + 2, 4), s_dn)

                def extras(e, eh, b, ahead):
                    n = pe.value_load(extra[0:1, l, bass.ds(e, 1)], min_val=0, max_val=NBLK - 1)
                    with pe.If(n > 0):
                        with pe.Fori(0, n):
                            now = pe.snap(g, min_val=1, max_val=4096)
                            gathered = in_register(pe, r_pe[0], now * 16)
                            copied = in_register(pe, r_pe[1], e + (M0 + ahead))
                            pe.wait_ge(s_pool0, 1)
                            pe.wait_ge(s_oxg, gathered)
                            pe.wait_ge(s_xgT, copied)
                            gathered_T(xg[2], s_oxt)
                            pe.wait_ge(s_oxgT, now)
                            half_products(5, xgT[2], gate_weights(e, b), s_ogate)
                            half_products(6, xgT[2], slot(3 * b + 1, KD), s_oup)
                            pe.wait_ge(s_oh, now)
                            for c in range(2):
                                tr = pe.transpose(ps[:, 3, c * P:(c + 1) * P], hh[2][:, c * P:(c + 1) * P],
                                                  ident[:, :])
                            tr.then_inc(s_oht, 1)
                            pe.wait_ge(s_ohTc, now)
                            pe.wait_ge(s_wd[b], 16 * (eh + (W0 + 1)))
                            pe.wait_ge(s_oyc, now)
                            down_products(7, hT[2], slot(3 * b + 2, 4), s_od)
                            pe.reg_add(g, g, 1)

                pe.wait_ge(s_extra, l + 1)
                stage_t(0, 0, 0)
                stage_g(0, 0, 0, False)
                stage_u(0, 0, 0, False)
                stage_t(1, 0, 1)
                extras(0, 0, 0, 2)

                def step(e, eh, b, first_h=False, last=False):
                    stage_g(e, eh, b, True)
                    stage_h(e - 1, 1 - b, later=not first_h)
                    stage_u(e, eh, b, True)
                    if not last:
                        stage_t(e + 1, eh + b, 1 - b)
                    stage_y(e - 1, eh if b else eh - 1, 1 - b, later=not first_h)
                    extras(e, eh, b, 1 if last else 2)

                step(1, 0, 1, first_h=True)
                step(2, 1, 0)
                step(3, 1, 1)
                with pe.Fori(0, (E - 6) // 2) as i:
                    step(2 * i + 4, i + 2, 0)
                    step(2 * i + 5, i + 2, 1)
                step(E - 2, E // 2 - 1, 0)
                step(E - 1, E // 2 - 1, 1, last=True)
                stage_h(E - 1, 1, last=True)
                stage_y(E - 1, E // 2 - 1, 1)

            token_table(0)
            experts(0)

            def unit(u):
                kind, t = u
                free(pe, u)
                bank = place[u][0]
                if kind in ("Xa", "Da"):
                    pe.wait_ge(s_ln, (T if kind == "Xa" else 2 * T) + t + 1)
                if kind in ("Xa", "Xb", "Da", "Db"):
                    j0 = 0 if kind[1] == "a" else 4
                    for j in range(4):
                        last = pe.transpose(ps[:, bank, j * P:(j + 1) * P], x_sb[:, t, j0 + j::KD], ident[:, :])
                elif kind in ("KV", "Q0", "Q1"):
                    taken(pe, ("Xa", t))
                    taken(pe, ("Xb", t))
                    w = {"KV": s_wkv, "Q0": s_wq[0], "Q1": s_wq[1]}[kind]
                    pe.wait_ge(w, 16)
                    at = {"KV": 0, "Q0": 1, "Q1": 2}[kind]
                    for k in range(KD):
                        last = pe.matmul(ps[:, bank, :], xTt[:, k, :], slot(at, KD)[:, k, :],
                                         start=(k == 0), stop=(k == KD - 1))
                elif kind == "KT":
                    pe.wait_ge(s_kr, t + 1)
                    for j in range(NKV):
                        last = pe.transpose(ps[:, bank, j * P:(j + 1) * P],
                                            kr[:, j, :, :].rearrange("p a b -> p (a b)"), ident[:, :])
                elif kind in ("QTa", "QTb"):
                    h = "ab".index(kind[2])
                    pe.wait_ge(s_qr, 2 * t + h + 1)
                    for j in range(4):
                        i = 8 * h + 2 * j
                        last = pe.transpose(ps[:, bank, j * P:(j + 1) * P],
                                            qr[:, i:i + 2, :].rearrange("p a b -> p (a b)"), ident[:, :])
                elif kind in ("W0", "W1"):
                    h = int(kind[1])
                    pe.wait_ge(s_oT, NKV * (t + 1))
                    pe.wait_ge(s_wo[h], 16)
                    for k in range(KD):
                        last = pe.matmul(ps[:, bank, :], oT[t % 2][:, k, :], slot(3 + h, KD)[:, k, :],
                                         start=(k == 0), stop=(k == KD - 1))
                elif kind == "R":
                    last = rank_products(1, t, bank)
                else:
                    taken(pe, ("Da", t))
                    taken(pe, ("Db", t))
                    for k in range(KD):
                        last = pe.matmul(ps[:, bank, 0:E], xTt[:, k, :], rw[:, k, :],
                                         start=(k == 0), stop=(k == KD - 1))
                last.then_inc(bank_full[bank - 5], 1)

            def scores(t, kh):
                n = NKV * t + kh
                lo = 0 if t else P
                if kh == 0:
                    taken(pe, ("KT", t))
                    taken(pe, ("QTa", t))
                if kh == 2:
                    taken(pe, ("QTb", t))
                if n >= 1:
                    pe.wait_ge(s_ss, n)
                for j in range(2):
                    for r in range(2):
                        part = slice(r * HD, (r + 1) * HD)
                        last = pe.matmul(ps[:, r, j * 256 + lo:j * 256 + 256], qT[t % 2][part, 2 * kh + j, :],
                                         kT[part, kh, (t - 1) * P + lo:(t + 1) * P], start=True, stop=True)
                last.then_inc(s_S, 1)

            def turn(t, kh):
                n = NKV * t + kh
                pe.wait_ge(s_pn, n + 1)
                if n >= 1:
                    pe.wait_ge(s_PT, n)
                for i in range(GQ):
                    for s in range(0 if t else 1, 2):
                        last = pe.transpose(ps[:, 2 + i // 2, ((2 * i + s) % 4) * P:((2 * i + s) % 4 + 1) * P],
                                            pr[n % 2][:, i, s * P:(s + 1) * P], ident[:, :])
                last.then_inc(s_PTt, 1)

            def values(t, kh):
                n = NKV * t + kh
                pe.wait_ge(s_PT, n + 1)
                if n >= 1:
                    pe.wait_ge(s_oT, n)
                s0 = 0 if t else 1
                pt = PT.rearrange("p (r j s) n -> p r j s n", r=2, s=2)
                for s in range(s0, 2):
                    for r in range(2):
                        last = pe.matmul(ps[r * HD:(r + 1) * HD, 4, 0:256], v_sb[:, t - 1 + s, kh * HD:(kh + 1) * HD],
                                         pt[:, r, :, s, :], start=(s == s0), stop=(s == 1))
                last.then_inc(s_O, 1)

            for u in first_units:
                unit(u)
            for t in range(T):
                scores(t, 0)
                for kh, (early, late) in enumerate(fillers(t)):
                    for u in early:
                        unit(u)
                    if kh:
                        values(t, kh - 1)
                    for u in late:
                        unit(u)
                    if kh + 1 < NKV:
                        scores(t, kh + 1)
                    turn(t, kh)
                values(t, NKV - 1)
            for u in last_units:
                unit(u)
            token_table(1)
            experts(1)

        @block.vector
        def _(dve):
            done = [0]
            g = ctx.enter_context(dve.register("dve_extra"))
            dve.reg_mov(g, 1)

            def own(ins):
                done[0] += 1
                ins.then_inc(s_dc, 1)
                dve.wait_ge(s_dc, done[0])

            for t in range(T):
                dve.wait_ge(s_x0T, t + 1)
                for h in range(2):
                    ins = dve.tensor_copy(xT[:, 4 * h:4 * h + 4, t * P:(t + 1) * P],
                                          ps[:, 2 * (t % 2) + h, :].rearrange("p (j n) -> p j n", j=4))
                ins.then_inc(s_xTd, 1)
            dve.wait_ge(s_prT, 1)
            dve.tensor_copy(prmT[:, :], ps[:, 5, 0:NPRM])
            dve.tensor_copy(posT[:, :], ps[:, 5, 64:64 + T])
            dve.tensor_copy(dwT[:, :, 0:CW], ps[:, 4, 0:32 * KD].rearrange("p (c k) -> p c k", k=32)[:, :, 0:CW]
                            ).then_inc(s_prC, 1)
            dve.wait_ge(s_pool0, 2)
            dve.wait_ge(s_prC, 1)

            def glu(c, parity):
                one = bass.ds(c, 1)
                bank = 2 * c if not isinstance(c, int) else 2 * (c % 4)
                dve.wait_ge(s_g1, c + 1)
                dve.wait_ge(s_sgm, c + 1)
                dve.scalar_tensor_tensor(out=hpad[:, one, CW - 1:PADW], in0=ps[:, bass.ds(bank, 1), :],
                                         scalar=prmT[:, bass.ds(c + PB1, 1)], in1=sgm[parity],
                                         op0=ALU.add, op1=ALU.mult).then_inc(s_glu, 1)

            def taps(c, glus):
                one = bass.ds(c, 1)
                even = cv[:, one, :]
                dve.wait_ge(s_glu, glus)
                dve.tensor_scalar(even, hpad[:, one, 0:S], dwT[:, one, 0:1],
                                  prmT[:, bass.ds(c + PDWB, 1)], ALU.mult, ALU.add).then_inc(s_tap, 1)
                dve.tensor_scalar(odd, hpad[:, one, 1:1 + S], dwT[:, one, 1:2], None, ALU.mult).then_inc(s_tap, 1)
                for k in range(2, CW):
                    acc = (even, odd)[k % 2]
                    dve.wait_ge(s_tap, c * (CW + 1) + (k - 1))
                    dve.scalar_tensor_tensor(out=acc, in0=hpad[:, one, k:k + S], scalar=dwT[:, one, k:k + 1],
                                             in1=acc, op0=ALU.mult, op1=ALU.add).then_inc(s_tap, 1)
                dve.wait_ge(s_tap, c * (CW + 1) + CW)
                dve.tensor_tensor(even, even, odd, ALU.add).then_inc(s_tap, 1)

            with dve.Fori(0, 2) as i:
                for b in range(2):
                    glu(2 * i + b, b)
                    taps(2 * i + b, 2 * i + (b + 1))
            glu(4, 0)
            glu(6, 0)
            taps(4, glu_count(4))
            glu(5, 1)
            glu(7, 1)
            taps(5, glu_count(5))

            def moments(src, n, signal):
                for h in range(2):
                    ins = dve.bn_stats(bns[:, h, :], src(h))
                own(ins)
                dve.bn_aggr(mv[:, n, :], bns[:, :, :]).then_inc(signal, 1)

            def norm_conv(t, n):
                dve.wait_ge(s_At, t + 1)
                moments(lambda h: ps[:, h, :], n, s_mv)
                dve.wait_ge(s_rs, n + 1)
                dve.wait_ge(s_mv, n + 1)
                if t >= 2:
                    dve.wait_ge(s_Bt, t - 1)
                dve.tensor_scalar(ntok[t % 2], ps[:, 0:2, :].rearrange("p a b -> p (a b)"), mv[:, n, 0:1],
                                  rstd[:, n:n + 1], ALU.subtract, ALU.mult).then_inc(s_nt, 1)

            def norm_x(t, n, l, which):
                xt = x_sb[:, t, :]
                moments(lambda h: x_sb[:, t, h * 512:(h + 1) * 512], n, s_mv)
                dve.wait_ge(s_mv, n + 1)
                own(dve.scalar_tensor_tensor(out=xt, in0=xt, scalar=mv[:, n, 0:1], in1=lnrow[:, which, 0, :],
                                             op0=ALU.subtract, op1=ALU.mult))
                dve.wait_ge(s_rs, n + 1)
                dve.scalar_tensor_tensor(out=xt, in0=xt, scalar=rstd[:, n:n + 1], in1=lnrow[:, which, 1, :],
                                         op0=ALU.mult, op1=ALU.add).then_inc(s_ln, 1)

            def add_product(t, bank, signal, count):
                for h in range(2):
                    ins = dve.tensor_tensor(x_sb[:, t, h * 512:(h + 1) * 512], x_sb[:, t, h * 512:(h + 1) * 512],
                                            ps[:, bank + h, :], ALU.add)
                ins.then_inc(signal, 1)
                dve.wait_ge(signal, count)

            def route(l, t):
                if l == 0:
                    dve.wait_ge(s_aff, t + 1)
                else:
                    taken(dve, ("E", t))
                at = aff[:, t, :]
                own(dve.tensor_tensor(sel[:, :], at, rbrow[:, :], ALU.add))
                v = sel[:, :].rearrange("p (g e) -> p g e", g=NG)
                a, b, c, d = (v[:, :, i] for i in range(EPG))
                dve.tensor_tensor(gs[:, 0, :], a, b, ALU.max)
                dve.tensor_tensor(gs[:, 1, :], a, b, ALU.min)
                dve.tensor_tensor(gs[:, 2, :], c, d, ALU.max)
                own(dve.tensor_tensor(gs[:, 3, :], c, d, ALU.min))
                dve.tensor_tensor(gs[:, 4, :], gs[:, 0, :], gs[:, 2, :], ALU.max)
                dve.tensor_tensor(gs[:, 1, :], gs[:, 1, :], gs[:, 3, :], ALU.max)
                own(dve.tensor_tensor(gs[:, 0, :], gs[:, 0, :], gs[:, 2, :], ALU.min))
                own(dve.tensor_tensor(gs[:, 1, :], gs[:, 1, :], gs[:, 0, :], ALU.max))
                own(dve.tensor_tensor(gs[:, 4, :], gs[:, 4, :], gs[:, 1, :], ALU.add))

                def first_of_max(score, ramp, out, tmp):
                    own(dve.tensor_reduce(gsm[:, 0:1], score, AX.X, ALU.max))
                    own(dve.scalar_tensor_tensor(out=tmp, in0=score, scalar=gsm[:, 0:1], in1=ramp[:, :],
                                                 op0=ALU.is_equal, op1=ALU.mult))
                    own(dve.tensor_reduce(gsm[:, 1:2], tmp, AX.X, ALU.min))
                    own(dve.tensor_scalar(out, ramp[:, :], gsm[:, 1:2], None, ALU.is_equal))

                first_of_max(gs[:, 4, :], ramp4, gs[:, 0, :], gs[:, 1, :])
                dve.tensor_scalar(gs[:, 1, :], gs[:, 0, :], -NEG, NEG, ALU.mult, ALU.add)
                full = [P, NG, EPG]
                sv = seln[:, :].rearrange("p (g e) -> p g e", g=NG)
                own(dve.tensor_tensor(sv, v, gs[:, 0, :].unsqueeze(2).to_broadcast(full), ALU.mult))
                own(dve.tensor_tensor(sv, sv, gs[:, 1, :].unsqueeze(2).to_broadcast(full), ALU.add))
                first_of_max(seln[:, :], ramp16, onehot[:, 0, t, :], r1[:, :])
                own(dve.scalar_tensor_tensor(out=seln[:, :], in0=onehot[:, 0, t, :], scalar=-3e38, in1=seln[:, :],
                                             op0=ALU.mult, op1=ALU.add))
                first_of_max(seln[:, :], ramp16, onehot[:, 1, t, :], r1[:, :])
                dve.tensor_tensor(mask_b[:, t, :], onehot[:, 0, t, :], onehot[:, 1, t, :], ALU.add).then_inc(s_mask, 1)
                own(dve.tensor_tensor(r3[:, :, :], onehot[:, :, t, :], at.unsqueeze(1).to_broadcast([P, 2, E]),
                                      ALU.mult))
                own(dve.tensor_reduce(gatev[:, :, t], r3[:, :, :], AX.X, ALU.add))

            def places(l, t, bank):
                if l == 0:
                    dve.wait_ge(s_rank, t + 1)
                own(dve.tensor_tensor(r1[:, :], ps[:, bank, 0:E], tbase[:, :], ALU.add))
                own(dve.tensor_tensor(r2[:, :, :], onehot[:, :, t, :], r1[:, :].unsqueeze(1).to_broadcast([P, 2, E]),
                                      ALU.mult))
                own(dve.tensor_reduce(placef[:, :], r2[:, :, :], AX.X, ALU.add))
                dve.tensor_copy(place_i[:, :, t], placef[:, :]).then_inc(s_place, 1)
                if t == T - 1:
                    dve.tensor_copy(cntf[:, 0, :], ps[:, bank, E:2 * E])
                kept = dve.tensor_copy(rankf[:, t, :], ps[:, bank, 0:E])
                kept.then_inc(s_rankc if l == 0 else bank_read[bank - 5], 1)
                if l == 0:
                    dve.wait_ge(s_rankc, t + 1)
                else:
                    taken(dve, ("R", t))

            def table(l):
                count, more, first, shift = (cntf[:, i, :] for i in range(4))
                shape = [P, E, NBLK - 1]
                own(dve.tensor_tensor(cmp7[:, :, :], count.unsqueeze(2).to_broadcast(shape),
                                      thr[:, :].unsqueeze(1).to_broadcast(shape), ALU.is_gt))
                own(dve.tensor_reduce(more, cmp7[:, :, :], AX.X, ALU.add))
                dve.tensor_copy(extra[:, l, :], more[0:1, :]).then_inc(s_extra, 1)
                own(dve.tensor_tensor(extras_before[:, :, :], before[:, :, :],
                                      more.unsqueeze(1).to_broadcast([P, E, E]), ALU.mult))
                own(dve.tensor_reduce(first, extras_before[:, :, :], AX.X, ALU.add))
                own(dve.scalar_tensor_tensor(out=shift, in0=first, scalar=float(CAP), in1=ebase[:, :],
                                             op0=ALU.mult, op1=ALU.subtract))
                own(dve.tensor_scalar(shift, shift, float(CAP * (E - 1)), None, ALU.add))
                wide = [P, T, E]
                own(dve.tensor_scalar(rows_t[:, :, :], rankf[:, :, :], float(CAP), None, ALU.is_ge))
                own(dve.tensor_tensor(rows_t[:, :, :], rows_t[:, :, :], shift.unsqueeze(1).to_broadcast(wide), ALU.mult))
                own(dve.tensor_tensor(rows_t[:, :, :], rows_t[:, :, :], rankf[:, :, :], ALU.add))
                own(dve.tensor_tensor(rows_t[:, :, :], rows_t[:, :, :], ebase[:, :].unsqueeze(1).to_broadcast(wide),
                                      ALU.add))
                for j in range(2):
                    ins = dve.tensor_tensor(rows_j[:, j * T:(j + 1) * T, :], rows_t[:, :, :], onehot[:, j, :, :], ALU.mult)
                own(ins)
                dve.tensor_tensor(gsum[:, :], gatev[:, 0, :], gatev[:, 1, :], ALU.add)
                own(dve.tensor_reduce(rowf[:, :, :].rearrange("p j t -> p (j t)"), rows_j[:, :, :], AX.X, ALU.add))
                dve.tensor_copy(rowi[:, :, :], rowf[:, :, :]).then_inc(s_rowi, 1)
                own(dve.reciprocal(gsum[:, :], gsum[:, :]))
                dve.tensor_tensor(gate_w[:, :, :], gatev[:, :, :], gsum[:, :].unsqueeze(1).to_broadcast([P, 2, T]),
                                  ALU.mult)
                dve.wait_ge(s_tokr, 16 * (l + 1))
                dve.tensor_copy(tok_f[:, :], tok_r[:, :]).then_inc(s_tokf, 1)
                dve.wait_ge(s_tokt, l + 1)
                dve.tensor_copy(tokT[:, :], ps[0:CAP, 1, 0:E * NBLK]).then_inc(s_tokT, 1)

            dve.wait_ge(s_rows, 16 * 8)
            n = 0
            norm_conv(0, n)
            n += 1
            norm_conv(1, n)
            n += 1
            for t in range(T):
                if t >= 2:
                    places(0, t - 2, 7)
                dve.wait_ge(s_C, t + 1)
                dve.wait_ge(s_xa, t + 1)
                add_product(t, 4, s_cadd, t + 1)
                norm_x(t, n, 0, 0)
                n += 1
                if t + 2 < T:
                    norm_conv(t + 2, n)
                    n += 1
                if t >= 1:
                    route(0, t - 1)
            places(0, T - 2, 7)
            route(0, T - 1)
            places(0, T - 1, 7)
            table(0)

            def experts(l):
                M0 = E * l

                def copy_t(e, b, later):
                    dve.wait_ge(s_xt, e + (M0 + 1))
                    if later or l > 0:
                        dve.wait_ge(s_up, e + (M0 - 1))
                    dve.tensor_copy(xgT[b].rearrange("p a b -> p (a b)"), ps[:, 0, :]).then_inc(s_xgT, 1)

                def gated(e, b, later):
                    dve.wait_ge(s_up, e + (M0 + 1))
                    dve.wait_ge(s_sg, e + (M0 + 1))
                    if later or l > 0:
                        dve.wait_ge(s_ht, e + (M0 - 1))
                    dve.tensor_tensor(hh[b], sg[b], ps[:, 2, 0:256], ALU.mult).then_inc(s_h, 1)

                def copy_h(e, b, later):
                    dve.wait_ge(s_ht, e + (M0 + 1))
                    if later or l > 0:
                        dve.wait_ge(s_dn, e + (M0 - 1))
                    dve.tensor_copy(hT[b].rearrange("p a b -> p (a b)"), ps[:, 3, 0:256]).then_inc(s_hTc, 1)

                def extras(e):
                    k = dve.value_load(extra[0:1, l, bass.ds(e, 1)], min_val=0, max_val=NBLK - 1)
                    with dve.If(k > 0):
                        with dve.Fori(0, k):
                            now = dve.snap(g, min_val=1, max_val=4096)
                            dve.wait_ge(s_oxt, now + 1)
                            dve.tensor_copy(xgT[2].rearrange("p a b -> p (a b)"), ps[:, 0, :]).then_inc(s_oxgT, 1)
                            dve.wait_ge(s_oup, now)
                            dve.wait_ge(s_osg, now)
                            dve.tensor_tensor(hh[2], sg[2], ps[:, 6, 0:256], ALU.mult).then_inc(s_oh, 1)
                            dve.wait_ge(s_oht, now)
                            dve.tensor_copy(hT[2].rearrange("p a b -> p (a b)"), ps[:, 3, 0:256]).then_inc(s_ohTc, 1)
                            dve.reg_add(g, g, 1)

                dve.wait_ge(s_extra, l + 1)
                copy_t(0, 0, False)
                gated(0, 0, False)
                copy_t(1, 1, False)
                extras(0)
                copy_h(0, 0, False)
                gated(1, 1, False)
                copy_t(2, 0, True)
                extras(1)

                def step(e, b, last=False):
                    copy_h(e - 1, 1 - b, True)
                    gated(e, b, True)
                    if not last:
                        copy_t(e + 1, 1 - b, True)
                    extras(e)

                with dve.Fori(0, (E - 4) // 2) as i:
                    step(2 * i + 2, 0)
                    step(2 * i + 3, 1)
                step(E - 2, 0)
                step(E - 1, 1, last=True)
                copy_h(E - 1, 1, True)

            def combine(l, n):
                dve.wait_ge(s_xal, T * (l + 1))
                for t in range(T):
                    y0, y1 = yg[t]
                    dve.wait_ge(s_yg[t], 32 * (l + 1))
                    own(dve.scalar_tensor_tensor(out=x_sb[:, t, :], in0=y1, scalar=gate_w[:, 1, t:t + 1],
                                                 in1=x_sb[:, t, :], op0=ALU.mult, op1=ALU.add))
                    dve.wait_ge(s_y0g, T * l + t + 1)
                    dve.tensor_tensor(x_sb[:, t, :], x_sb[:, t, :], y0, ALU.add).then_inc(s_cmb, 1)
                    dve.wait_ge(s_cmb, T * l + t + 1)
                    norm_x(t, n + t, l, 1)

            experts(0)
            combine(0, n)
            n += T

            dve.wait_ge(s_ropeT, 1)
            dve.wait_ge(s_rows1, 16 * 5)

            def rotate(t, src, heads, dst, tmp):
                cs = cosb[:, t, :].unsqueeze(1).to_broadcast([P, heads, HH])
                sn = sinb[:, t, :].unsqueeze(1).to_broadcast([P, heads, HH])
                lo, hi = src[:, :, 0:HH], src[:, :, HH:HD]
                ta = tmp[0].rearrange("p (h d) -> p h d", h=heads)
                tb = tmp[1].rearrange("p (h d) -> p h d", h=heads)
                dve.tensor_tensor(ta, lo, cs, ALU.mult)
                own(dve.tensor_tensor(tb, hi, sn, ALU.mult))
                own(dve.tensor_tensor(dst[0], ta, tb, ALU.subtract))
                dve.tensor_tensor(ta, hi, cs, ALU.mult)
                own(dve.tensor_tensor(tb, lo, sn, ALU.mult))
                return dve.tensor_tensor(dst[1], ta, tb, ALU.add)

            def norm_tile(t, n):
                taken(dve, ("W0", t))
                taken(dve, ("W1", t))
                norm_x(t, n + t, 1, 0)

            def take(u, n):
                kind, t = u
                if kind == "E":
                    route(1, t)
                    return
                if kind[0] in "XD" or kind in ("KT", "QTa", "QTb"):
                    return
                bank = full(dve, u)
                if kind == "KV":
                    if t >= 1:
                        full(dve, ("KT", t - 1))
                    dve.tensor_tensor(v_sb[:, t, :], ps[:, bank, KVD:2 * KVD], kvrow[:, KVD:2 * KVD], ALU.add)
                    dve.tensor_tensor(k_sb, ps[:, bank, 0:KVD], kvrow[:, 0:KVD], ALU.add
                                      ).then_inc(bank_read[bank - 5], 1)
                    taken(dve, u)
                    own(rotate(t, k_sb.rearrange("p (h d) -> p h d", h=NKV), NKV,
                               (kr[:, :, 0, 0:HH], kr[:, :, 0, HH:HD]), tk))
                    dve.tensor_copy(kr[:, :, 1, :], kr[:, :, 0, :]).then_inc(s_kr, 1)
                elif kind in ("Q0", "Q1"):
                    h = int(kind[1])
                    if t >= 1:
                        full(dve, ("QT" + "ab"[h], t - 1))
                    dve.tensor_tensor(q_sb, ps[:, bank, :], bqrow[:, h * 512:(h + 1) * 512], ALU.add
                                      ).then_inc(bank_read[bank - 5], 1)
                    taken(dve, u)
                    part = qr[:, 8 * h:8 * h + 8, :]
                    rotate(t, q_sb.rearrange("p (h d) -> p h d", h=8), 8,
                           (part[:, :, 0:HH], part[:, :, HH:HD]), tq).then_inc(s_qr, 1)
                elif kind in ("W0", "W1"):
                    h = int(kind[1])
                    dve.wait_ge(s_xb, t + 1)
                    half_x = x_sb[:, t, h * 512:(h + 1) * 512]
                    dve.tensor_tensor(half_x, half_x, ps[:, bank, :], ALU.add).then_inc(bank_read[bank - 5], 1)
                    if h == 1 and t == T - 1:
                        norm_tile(t, n)
                else:
                    places(1, t, bank)

            def soft(t, kh):
                m = NKV * t + kh
                lo = 0 if t else P
                dve.wait_ge(s_S, m + 1)
                if m >= 2:
                    dve.wait_ge(s_PTt, m - 1)
                sc = ps[:, 0:2, :].rearrange("p a (j s) -> p (a j) s", j=2)[:, :, lo:256]
                sv = pr[m % 2][:, :, lo:256]
                dve.scalar_tensor_tensor(out=sv, in0=sc, scalar=1.0 / math.sqrt(HD),
                                         in1=mask[:, lo:256].unsqueeze(1).to_broadcast([P, GQ, 256 - lo]),
                                         op0=ALU.mult, op1=ALU.add).then_inc(s_ss, 1)
                dve.wait_ge(s_ss, m + 1)
                gq = slice(kh * GQ, (kh + 1) * GQ)
                own(dve.tensor_reduce(mxs[:, gq], sv, AX.X, ALU.max))
                sk = sinkb[:, gq].rearrange("p (j r) -> p r j", r=2)
                mx = mxs[:, gq].rearrange("p (r j) -> p r j", r=2)
                own(dve.tensor_tensor(mx, mx, sk, ALU.max))
                dve.tensor_tensor(exs[:, 0, gq].rearrange("p (r j) -> p r j", r=2), sk, mx, ALU.subtract)
                dve.tensor_scalar(negm[:, gq], mxs[:, gq], -1.0, None, ALU.mult).then_inc(s_negm, 1)

            def normed_probs(t, kh):
                m = NKV * t + kh
                lo = 0 if t else P
                gq = slice(kh * GQ, (kh + 1) * GQ)
                dve.wait_ge(s_ex, m + 1)
                own(dve.tensor_tensor(den[:, gq], den[:, gq], exs[:, 1, gq], ALU.add))
                own(dve.reciprocal(rden[:, gq], den[:, gq]))
                sv = pr[m % 2][:, :, lo:256]
                dve.tensor_tensor(sv, sv, rden[:, gq].unsqueeze(2).to_broadcast([P, GQ, 256 - lo]), ALU.mult
                                  ).then_inc(s_pn, 1)

            for u in first_units:
                take(u, n)
            for t in range(T):
                soft(t, 0)
                for kh, (early, late) in enumerate(fillers(t)):
                    normed_probs(t, kh)
                    if kh == 0 and t >= 2:
                        norm_tile(t - 2, n)
                    for u in early + late:
                        take(u, n)
                    if kh + 1 < NKV:
                        soft(t, kh + 1)
            norm_tile(T - 2, n)
            for u in last_units:
                take(u, n)
            n += T
            table(1)
            experts(1)
            dve.wait_ge(s_rows2, 16 * 2)
            combine(1, n)

        @block.scalar
        def _(act):
            g = ctx.enter_context(act.register("act_extra"))
            act.reg_mov(g, 1)
            nth = ctx.enter_context(act.register("act_nth"))
            act.sem_inc(s_oyc, 1)
            act.sem_inc(s_oy, 32)
            act.dma_start(prm[PB1:PB1 + 16, :], conv_b1.rearrange("a (j p) -> (a j) p", p=P)).then_inc(s_small, 16)
            act.dma_start(prm[PDWB:PDWB + KD, :], conv_dwb.rearrange("a (j p) -> (a j) p", p=P)).then_inc(s_small, 16)
            act.dma_start(prm[PGAM:PGAM + KD, :], conv_ln_g.rearrange("a (j p) -> (a j) p", p=P)).then_inc(s_small, 16)
            act.dma_start(prm[PBET:PBET + KD, :], conv_ln_b.rearrange("a (j p) -> (a j) p", p=P)).then_inc(s_small, 16)
            act.dma_start(dw_r[:, :], conv_dw[0]).then_inc(s_small, 16)
            act.dma_start(pos_i[:, :], positions.rearrange("a (t p) -> (a t) p", p=P)).then_inc(s_small, 16)

            def norm_rows(l, w, signal):
                act.dma_start(lnrow[:, w, 0, :], ln_g[l, w].partition_broadcast(P)).then_inc(signal, 16)
                act.dma_start(lnrow[:, w, 1, :], ln_b[l, w].partition_broadcast(P)).then_inc(signal, 16)

            def later_loads():
                act.wait_ge(s_pool0, 2)
                act.wait_ge(s_w1[KD // 2 - 1], 32)
                act.dma_start(resrow, conv_b2[0].partition_broadcast(P)).then_inc(s_rows, 16)
                act.dma_start(rw[:, :, :], router_w.rearrange("(p k) e -> p k e", k=KD)).then_inc(s_rows, 16)
                for w in range(2):
                    norm_rows(0, w, s_rows)
                act.dma_start(rbrow[:, :], router_b.partition_broadcast(P)).then_inc(s_rows, 16)
                act.dma_start(sinkb[:, :], attn_sinks[0].partition_broadcast(P)).then_inc(s_rows, 16)
                act.dma_start(y_dram[E * CAP:, :].rearrange("(p n) (h d) -> p (n h) d", p=P, h=2),
                              cv[:, KD - 1, :].unsqueeze(1).to_broadcast([P, (TBLK - E) * CAP // P * 2, S])
                              ).then_inc(s_yinit, 16)

            act.wait_ge(s_prC, 1)
            for c in range(KD):
                act.wait_ge(s_g1, c + 1)
                if c >= 2:
                    act.wait_ge(s_glu, glu_count(c - 2))
                act.activation(sgm[c % 2], ps[:, 1 + 2 * (c % 4), :], ACT.Sigmoid,
                               bias=prmT[:, PB1 + KD + c:PB1 + KD + c + 1]).then_inc(s_sgm, 1)
                if c == 0:
                    later_loads()
            act.wait_ge(s_yinit, 16)
            for c in range(DVE_TILES, KD):
                act.wait_ge(s_pec, c - DVE_TILES + 1)
                act.activation(cv[:, c, :], ps[:, 2 * (c % 4) - 4, :], ACT.Identity,
                               bias=prmT[:, PDWB + c:PDWB + c + 1]).then_inc(s_pecv, 1)
            act.wait_ge(s_rope, 2)
            act.activation(rope_w[:, 1, :], rope_w[:, 0, :], ACT.Sin, scale=0.5)
            act.activation(rope_w[:, 3, :], rope_w[:, 2, :], ACT.Sin, scale=1.0).then_inc(s_sin, 1)

            def silu_conv(t):
                act.wait_ge(s_Bt, t + 1)
                if t >= 2:
                    act.wait_ge(s_C, t - 1)
                for c in range(KD):
                    ins = act.activation(hc[t % 2][:, c, :], ps[:, 2 + c // 4, (c % 4) * P:(c % 4 + 1) * P], ACT.Silu,
                                         bias=prmT[:, PBET + c:PBET + c + 1], scale=prmT[:, PGAM + c:PGAM + c + 1])
                ins.then_inc(s_hc, 1)

            def normed(t):
                act.wait_ge(s_ln, t + 1)
                act.dma_start(xd_rows[:, t, :], x_sb[:, t, :]).then_inc(s_xst, 16)
                act.wait_ge(s_Dt, t + 1)
                act.activation(xTt.rearrange("p a b -> p (a b)"), ps[:, 6:8, :].rearrange("p a b -> p (a b)"),
                               ACT.Copy).then_inc(s_xTt, 1)
                act.wait_ge(s_lg, t + 1)
                act.activation(aff[:, t, :], ps[:, 6, 0:E], ACT.Sigmoid).then_inc(s_aff, 1)

            silu_conv(0)
            for t in range(T):
                if t + 1 < T:
                    silu_conv(t + 1)
                if t >= 1:
                    normed(t - 1)
            normed(T - 1)
            act.dma_start(resrow, attn_bo[0].partition_broadcast(P)).then_inc(s_rows1, 16)
            norm_rows(1, 0, s_rows1)
            act.wait_ge(s_ropeT, 1)
            act.dma_start(bqrow, attn_bq[0].partition_broadcast(P)).then_inc(s_rows1, 16)
            act.dma_start(kvrow, kv_b.partition_broadcast(P)).then_inc(s_rows1, 16)

            def experts(l):
                M0 = E * l

                def silu(e, b, later):
                    act.wait_ge(s_gate, e + (M0 + 1))
                    if later or l > 0:
                        act.wait_ge(s_h, e + (M0 - 1))
                    act.activation(sg[b], ps[:, 1, 0:256], ACT.Silu).then_inc(s_sg, 1)

                def store(e, eh, b, later):
                    act.wait_ge(s_dn, e + (M0 + 1))
                    if later or l > 0:
                        act.wait_ge(s_y[b], 32 * (eh + 8 * l))
                    act.activation(ysb[b], ps[:, 4, :], ACT.Copy).then_inc(s_yc, 1)
                    act.wait_ge(s_yc, e + (M0 + 1))
                    for h in range(2):
                        act.dma_start(y_dram[bass.ds(e * CAP, CAP), h * 512:(h + 1) * 512],
                                      ysb[b][h * CAP:(h + 1) * CAP, :]).then_inc(s_y[b], 16)

                def extras(e):
                    n = act.value_load(extra[0:1, l, bass.ds(e, 1)], min_val=0, max_val=NBLK - 1)
                    with act.If(n > 0):
                        with act.Fori(0, n):
                            now = act.snap(g, min_val=1, max_val=4096)
                            row = act.snap(nth, min_val=0, max_val=E - 2) * CAP + E * CAP
                            act.wait_ge(s_ogate, now)
                            act.activation(sg[2], ps[:, 5, 0:256], ACT.Silu).then_inc(s_osg, 1)
                            act.wait_ge(s_od, now)
                            act.wait_ge(s_oy, now * 32)
                            act.activation(ysb[2], ps[:, 7, :], ACT.Copy).then_inc(s_oyc, 1)
                            act.wait_ge(s_oyc, now + 1)
                            for h in range(2):
                                act.dma_start(y_dram[bass.ds(row, CAP), h * 512:(h + 1) * 512],
                                              ysb[2][h * CAP:(h + 1) * CAP, :]).then_inc(s_oy, 16)
                            act.reg_add(g, g, 1)
                            act.reg_add(nth, nth, 1)

                act.wait_ge(s_xst, 16 * T * (l + 1))
                for t in range(T):
                    act.activation(x_sb[:, t, :], x_sb[:, t, :], ACT.Copy, scale=ALPHA).then_inc(s_xal, 1)
                act.wait_ge(s_extra, l + 1)
                act.reg_mov(nth, 0)
                silu(0, 0, False)
                extras(0)
                silu(1, 1, False)
                store(0, 0, 0, False)
                extras(1)
                silu(2, 0, True)
                store(1, 0, 1, False)
                extras(2)
                silu(3, 1, True)
                store(2, 1, 0, True)
                extras(3)
                with act.Fori(0, (E - 4) // 2) as i:
                    silu(2 * i + 4, 0, True)
                    store(2 * i + 3, i + 1, 1, True)
                    extras(2 * i + 4)
                    silu(2 * i + 5, 1, True)
                    store(2 * i + 4, i + 2, 0, True)
                    extras(2 * i + 5)
                store(E - 1, E // 2 - 1, 1, True)

            def gated_y(l, t):
                y0 = yg[t][0]
                act.wait_ge(s_yg[t], 32 * (l + 1))
                act.activation(y0, y0, ACT.Copy, scale=gate_w[:, 0, t:t + 1]).then_inc(s_y0g, 1)

            experts(0)
            for t in range(T - 1):
                gated_y(0, t)
            def take(u):
                kind, t = u
                into = {"Xa": xTt[:, 0:4, :], "Xb": xTt[:, 4:8, :], "Da": xTt[:, 0:4, :], "Db": xTt[:, 4:8, :],
                        "KT": kT[:, :, t * P:(t + 1) * P], "QTa": qT[t % 2][:, 0:4, :],
                        "QTb": qT[t % 2][:, 4:8, :]}.get(kind)
                if kind == "Da":
                    act.wait_ge(s_ln, 2 * T + t + 1)
                    act.dma_start(xd_rows[:, t, :], x_sb[:, t, :]).then_inc(s_xst, 16)
                if kind == "E":
                    bank = full(act, u)
                    act.activation(aff[:, t, :], ps[:, bank, 0:E], ACT.Sigmoid).then_inc(bank_read[bank - 5], 1)
                if into is not None:
                    bank = full(act, u)
                    act.activation(into, ps[:, bank, :].rearrange("p (j n) -> p j n", j=4), ACT.Copy
                                   ).then_inc(bank_read[bank - 5], 1)

            def exps(t, kh):
                m = NKV * t + kh
                lo = 0 if t else P
                act.wait_ge(s_negm, m + 1)
                gq = slice(kh * GQ, (kh + 1) * GQ)
                for i in range(GQ):
                    h = kh * GQ + i
                    act.activation(pr[m % 2][:, i, lo:256], pr[m % 2][:, i, lo:256], ACT.Exp,
                                   bias=negm[:, h:h + 1], accum_out=den[:, h:h + 1])
                act.activation(exs[:, 1, gq], exs[:, 0, gq], ACT.Exp).then_inc(s_ex, 1)

            def keep_pt(t, kh):
                m = NKV * t + kh
                act.wait_ge(s_PTt, m + 1)
                if m >= 1:
                    act.wait_ge(s_O, m)
                s0 = 0 if t else 1
                pt = PT.rearrange("p (i s) n -> p i s n", s=2)[:, :, s0:2, :]
                src = ps[:, 2:4, :].rearrange("p a (i s n) -> p (a i) s n", i=2, s=2)[:, :, s0:2, :]
                act.activation(pt, src, ACT.Copy).then_inc(s_PT, 1)

            def keep_o(t, kh):
                m = NKV * t + kh
                act.wait_ge(s_O, m + 1)
                if t >= 2 and kh == 0:
                    full(act, ("W1", t - 2))
                act.activation(oT[t % 2][:, 2 * kh:2 * kh + 2, :], ps[:, 4, 0:256].rearrange("p (j n) -> p j n", j=2),
                               ACT.Copy).then_inc(s_oT, 1)

            for i, u in enumerate(first_units):
                take(u)
                if i == 1:
                    gated_y(0, T - 1)
            for t in range(T):
                for kh, (early, late) in enumerate(fillers(t)):
                    if kh:
                        exps(t, kh)
                    for u in early:
                        take(u)
                    if kh == 0:
                        exps(t, 0)
                    if kh:
                        keep_o(t, kh - 1)
                    for u in late:
                        take(u)
                    keep_pt(t, kh)
                keep_o(t, NKV - 1)
            for u in last_units:
                take(u)
            norm_rows(1, 1, s_rows2)
            experts(1)
            for t in range(T):
                gated_y(1, t)
            for t in range(T):
                act.wait_ge(s_ln, 3 * T + t + 1)
                act.dma_start(out_rows[:, t, :], x_sb[:, t, :]).then_inc(s_out, 16)
            act.wait_ge(s_out, 16 * T)

        @block.gpsimd
        def _(pool):
            done = [0]
            g = ctx.enter_context(pool.register("pool_extra"))
            r_pool = ctx.enter_context(pool.register("pool_r"))
            pool.reg_mov(g, 1)
            nth = ctx.enter_context(pool.register("pool_nth"))
            pool.sem_inc(s_oxt, 1)

            def own(ins):
                done[0] += 1
                ins.then_inc(s_pc, 1)
                pool.wait_ge(s_pc, done[0])

            own(pool.memset(ident[:, :], 0.0))
            pool.affine_select(out=ident[:, :], in_=ident[:, :], compare_op=ALU.not_equal, fill=1.0, base=0,
                               pattern=[[-1, P]], channel_multiplier=1).then_inc(s_pool0, 1)
            pool.memset(half[:, :], -0.5)
            pool.memset(cv[:, KD - 1, :], 0.0)
            pool.memset(hpad[:, :, 0:CW - 1], 0.0).then_inc(s_pool0, 1)
            pool.wait_ge(s_small, 16 * 6)
            pool.tensor_copy(pos_f[:, :], pos_i[:, :]).then_inc(s_rope, 1)
            own(pool.memset(tok_r[:, :], 0))
            pool.dma_start(tok_dram.rearrange("(p n) a -> p (n a)", p=P), tok_r[:, :]).then_inc(s_tokinit, 16)
            own(pool.memset(ones[:, :], 1.0))
            pool.affine_select(out=upper[:, :], in_=ones[:, :], compare_op=ALU.is_gt, fill=0.0, base=0,
                               pattern=[[1, P]], channel_multiplier=-1)
            own(pool.memset(before[:, :, :], 1.0))
            pool.affine_select(out=before[:, :, :], in_=before[:, :, :], compare_op=ALU.is_gt, fill=0.0, base=0,
                               pattern=[[1, E], [-1, E]], channel_multiplier=0)
            own(pool.memset(mask[:, :], 0.0))
            pool.affine_select(out=mask[:, 0:P], in_=mask[:, 0:P], compare_op=ALU.is_gt, fill=NEG, base=0,
                               pattern=[[1, P]], channel_multiplier=-1)
            pool.affine_select(out=mask[:, P:2 * P], in_=mask[:, P:2 * P], compare_op=ALU.is_ge, fill=NEG, base=0,
                               pattern=[[-1, P]], channel_multiplier=1)
            pool.iota(tokid[:, :], pattern=[[P, T]], base=0, channel_multiplier=1)
            exact = {"allow_small_or_imprecise_dtypes": True}
            pool.iota(ramp4[:, :], pattern=[[1, NG]], base=-NG, channel_multiplier=0, **exact)
            pool.iota(ramp16[:, :], pattern=[[1, E]], base=-E, channel_multiplier=0, **exact)
            pool.iota(ebase[:, :], pattern=[[CAP, E]], base=0, channel_multiplier=0, **exact)
            pool.iota(tbase[:, :], pattern=[[S, E]], base=0, channel_multiplier=0, **exact)
            own(pool.iota(thr[:, :], pattern=[[CAP, NBLK - 1]], base=CAP, channel_multiplier=0, **exact))
            for i in range(HH):
                ins = pool.memset(invf[:, i:i + 1], float(THETA ** (-2.0 * i / HD)))
            own(ins)
            pool.wait_ge(s_x0T, T)
            pool.wait_ge(s_rows, 16 * 8)
            for t in range(T):
                own(pool.tensor_scalar(x_sb[:, t, :], x_sb[:, t, :], ALPHA, None, ALU.mult))
                pool.tensor_tensor(x_sb[:, t, :], x_sb[:, t, :], resrow, ALU.add).then_inc(s_xa, 1)
            pool.wait_ge(s_prC, 1)
            for c in range(DVE_TILES, KD):
                pool.wait_ge(s_g1, c if c < KD - 1 else KD)
                pool.affine_select(out=diag(c), in_=dwT[:, c, 0:CW].unsqueeze(2).to_broadcast([P, CW, P]),
                                   compare_op=ALU.is_equal, fill=0.0, base=0, pattern=[[0, CW], [-1, P]],
                                   channel_multiplier=1).then_inc(s_diag, 1)
            ang, turns, tmp = rope_w[:, 0, :], rope_w[:, 1, :], rope_w[:, 2, :]
            for t in range(T):
                ins = pool.tensor_scalar(rope_w[:, 0, t * HH:(t + 1) * HH], invf[:, :], posT[:, t:t + 1], None, ALU.mult)
            own(ins)
            own(pool.tensor_scalar(turns, ang, 1.0 / TWO_PI, None, ALU.mult))
            own(pool.tensor_scalar(turns, turns, MAGIC, None, ALU.add))
            own(pool.tensor_scalar(turns, turns, -MAGIC, None, ALU.add))
            for part in two_pi_parts():
                own(pool.tensor_scalar(tmp, turns, part, None, ALU.mult))
                own(pool.tensor_tensor(ang, ang, tmp, ALU.subtract))
            own(pool.tensor_scalar(ang, ang, 3.1415925, -3.1415925, ALU.min, ALU.max))
            pool.tensor_scalar(tmp, ang, 0.5, math.pi / 2, ALU.mult, ALU.add).then_inc(s_rope, 1)
            pool.wait_ge(s_sin, 1)
            sv, cv_ = rope_w[:, 1, :], rope_w[:, 3, :]
            sflat, cflat = (b[:, :, :].rearrange("p t d -> p (t d)") for b in (sinb, cosb))
            own(pool.tensor_tensor(sflat, sv, cv_, ALU.mult))
            pool.tensor_scalar(sflat, sflat, 2.0, None, ALU.mult)
            own(pool.tensor_tensor(cflat, sv, sv, ALU.mult))
            pool.tensor_scalar(cflat, cflat, -2.0, 1.0, ALU.mult, ALU.add).then_inc(s_ropeT, 1)

            def inverse_std(n):
                pool.wait_ge(s_mv, n + 1)
                own(pool.tensor_scalar(vareps[:, n:n + 1], mv[:, n, 1:2], EPS, None, ALU.add))
                pool.tensor_tensor(rstd[:, n:n + 1], vareps[:, n:n + 1], half[:, :], ALU.pow).then_inc(s_rs, 1)

            def scatter(l, t):
                if l == 0 and t == 0:
                    pool.wait_ge(s_tokinit, 16)
                pool.wait_ge(s_place, T * l + t + 1)
                for j in range(2):
                    pool.indirect_dma_start(out=tok_dram[:, :],
                                            out_offset=bass.IndirectOffsetOnAxis(ap=place_i[:, j, t:t + 1], axis=0),
                                            in_=tokid[:, t:t + 1], in_offset=None).then_inc(s_scat, 16)

            def token_table(l):
                pool.wait_ge(s_scat, 16 * 2 * T * (l + 1))
                pool.dma_start(tok_r[:, :], tok_dram.rearrange("(p n) a -> p (n a)", p=E * NBLK)).then_inc(s_tokr, 16)
                pool.wait_ge(s_tokT, l + 1)

            def gather_x(where, idx_col, signal):
                pool.indirect_dma_start(out=where[0:CAP, :], out_offset=None, in_=x_dram[:, :],
                                        in_offset=bass.IndirectOffsetOnAxis(ap=idx[:, idx_col:idx_col + 1], axis=0)
                                        ).then_inc(signal, 16)

            def experts(l):
                M0 = E * l

                def gather(e, b, later):
                    if later or l > 0:
                        pool.wait_ge(s_xt, e + (M0 - 1))
                    pool.tensor_copy(idx[:, b:b + 1], tokT[:, bass.ds(e * NBLK, 1)]).then_inc(s_idx, 1)
                    count = in_register(pool, r_pool, e + (M0 + 1))
                    pool.wait_ge(s_xst, 16 * T * (l + 1))
                    pool.wait_ge(s_idx, count)
                    gather_x(xg[b], b, s_xg[b])

                def extras(e):
                    n = pool.value_load(extra[0:1, l, bass.ds(e, 1)], min_val=0, max_val=NBLK - 1)
                    with pool.If(n > 0):
                        pool.reg_mov(nth, 1)
                        with pool.Fori(0, n):
                            now = pool.snap(g, min_val=1, max_val=4096)
                            column = pool.snap(nth, min_val=1, max_val=NBLK - 1) + e * NBLK
                            pool.wait_ge(s_oxt, now)
                            pool.tensor_copy(idx[:, 2:3], tokT[:, bass.ds(column, 1)]).then_inc(s_oidx, 1)
                            pool.wait_ge(s_xst, 16 * T * (l + 1))
                            pool.wait_ge(s_oidx, now)
                            gather_x(xg[2], 2, s_oxg)
                            pool.reg_add(g, g, 1)
                            pool.reg_add(nth, nth, 1)

                gather(0, 0, False)
                gather(1, 1, False)
                pool.wait_ge(s_extra, l + 1)
                extras(0)
                with pool.Fori(0, (E - 2) // 2) as i:
                    gather(2 * i + 2, 0, True)
                    extras(2 * i + 1)
                    gather(2 * i + 3, 1, True)
                    extras(2 * i + 2)
                extras(E - 1)

            def combine(l, n):
                stored = in_register(pool, r_pool, pool.snap(g, min_val=1, max_val=4096) * 32)
                for b in range(2):
                    pool.wait_ge(s_y[b], 32 * 8 * (l + 1))
                pool.wait_ge(s_oy, stored)
                pool.wait_ge(s_rowi, l + 1)

                for t in range(T):
                    for j in range(2):
                        pool.indirect_dma_start(out=yg[t][j], out_offset=None, in_=y_dram[:, :],
                                                in_offset=bass.IndirectOffsetOnAxis(ap=rowi[:, j, t:t + 1], axis=0)
                                                ).then_inc(s_yg[t], 16)
                    if t >= 2:
                        inverse_std(n + t - 2)
                for t in range(T - 2, T):
                    inverse_std(n + t)

            for n in range(2 * T):
                if n >= 2 * T - 2:
                    scatter(0, n - (2 * T - 2))
                inverse_std(n)
            for t in range(2, T):
                scatter(0, t)
            token_table(0)
            experts(0)
            combine(0, 2 * T)
            pool.wait_ge(s_rows1, 16 * 5)
            def residual(t):
                full(pool, ("Xa", t))
                full(pool, ("Xb", t))
                own(pool.tensor_scalar(x_sb[:, t, :], x_sb[:, t, :], ALPHA, None, ALU.mult))
                pool.tensor_tensor(x_sb[:, t, :], x_sb[:, t, :], resrow, ALU.add).then_inc(s_xb, 1)

            residual(0)
            for t in range(T):
                if t + 1 < T:
                    residual(t + 1)
                inverse_std(3 * T + t)
                if t >= 2:
                    scatter(1, t - 2)
            for t in range(T - 2, T):
                scatter(1, t)
            token_table(1)
            experts(1)
            combine(1, 4 * T)


_INS = ['x', 'positions', 'conv_w1', 'conv_b1', 'conv_dw', 'conv_dwb', 'conv_ln_g', 'conv_ln_b',
        'conv_w2', 'conv_b2', 'kv_w', 'kv_b', 'attn_wq', 'attn_bq', 'attn_sinks', 'attn_wo', 'attn_bo',
        'router_w', 'router_b', 'moe_w_gate', 'moe_w_up', 'moe_w_down', 'ln_g', 'ln_b']
_OUTS = [((1, 512, 1024), 'float32')]


def kernel(**inputs):
    import numpy as _np
    import concourse.bacc as _bacc
    from concourse import mybir as _mybir
    from concourse.bass_utils import run_bass_kernel_spmd as _run

    nc = _bacc.Bacc("TRN2", target_bir_lowering=False, num_devices=1)
    arrays, args = {}, []
    for name in _INS:
        a = _np.ascontiguousarray(inputs[name])
        arrays[f"in_{name}_dram"] = a
        args.append(nc.dram_tensor(f"in_{name}_dram", a.shape, _mybir.dt.from_np(a.dtype), kind="ExternalInput").ap())
    for i, (shape, dtype) in enumerate(_OUTS):
        dt = _mybir.dt.from_np(_np.dtype(dtype))
        args.append(nc.dram_tensor(f"out_{i}_dram", shape, dt, kind="ExternalOutput").ap())
    trunk(nc, *args)
    r = _run(nc, [arrays], core_ids=[0])
    got = tuple(r.results[0][f"out_{i}_dram"] for i in range(len(_OUTS)))
    return got[0]
```
